# Optimizing a Trainium2 kernel written in Bass

```python
import math
import jax, jax.numpy as jnp
from jax import lax
import numpy as np

D_MODEL = 1024
BATCH = 1
SEQ = 1024
DEPTH = 1
DEC_BATCH = 8
DEC_SEQ = 16
PAST_LEN = 1024

CHUNK = 64
HEAD_DIM = 64
WINDOW = 128
WIN_CHUNKS = WINDOW // CHUNK
WIN_ROWS = WIN_CHUNKS * CHUNK
BAND = (WIN_CHUNKS + 1) * CHUNK
A_HEADS = 8
A_KV_HEADS = 2
A_GROUP = A_HEADS // A_KV_HEADS
A_WIDTH = A_HEADS * HEAD_DIM
A_KV_COLS = A_KV_HEADS * HEAD_DIM
B_HEADS = 4
B_V_DIM = 2 * HEAD_DIM
B_WIDTH = B_HEADS * B_V_DIM
B_QK_COLS = B_HEADS * 2 * HEAD_DIM
MIX_WIDTH = A_WIDTH + B_WIDTH
PLE_DIM = 256
Q_BLOCK = 128
NORM_EPS = 1e-6
SUBLN_EPS = 1e-5
NEG_INF = -1e30
IN_SIZES = (A_WIDTH, A_KV_COLS, A_KV_COLS, A_WIDTH, B_QK_COLS, B_QK_COLS, B_WIDTH, B_WIDTH)
IN_COLS = sum(IN_SIZES)
SPLIT_AT = tuple(int(c) for c in np.cumsum(IN_SIZES)[:-1])

kernel_name = 'hymba_swa_sink_diffattn_alibi_streaming_step'

def rms_norm(x, g, eps=NORM_EPS):
    x32 = x.astype(jnp.float32)
    y = x32 * lax.rsqrt(jnp.mean(x32 * x32, axis=-1, keepdims=True) + eps)
    return y.astype(x.dtype) * g

def alibi_slopes(n):
    return jnp.exp2(-8.0 * jnp.arange(1, n + 1, dtype=jnp.float32) / n)

def lambda_init(layer):
    return 0.8 - 0.6 * math.exp(-0.3 * layer)

def split_in(h, w_in):
    B, S = h.shape[:2]
    qa, ka, va, za, qb, kb, vb, zb = jnp.split(h @ w_in, SPLIT_AT, axis=-1)
    return (qa.reshape(B, S, A_KV_HEADS, A_GROUP, HEAD_DIM),
            ka.reshape(B, S, A_KV_HEADS, HEAD_DIM),
            va.reshape(B, S, A_KV_HEADS, HEAD_DIM),
            za,
            qb.reshape(B, S, B_HEADS, 2, HEAD_DIM),
            kb.reshape(B, S, B_HEADS, 2, HEAD_DIM),
            vb.reshape(B, S, B_HEADS, B_V_DIM),
            zb)

def sink_softmax(logits, sink):
    m = jnp.maximum(jnp.max(logits, axis=-1, keepdims=True), sink)
    e = jnp.exp(logits - m)
    return e / (jnp.sum(e, axis=-1, keepdims=True) + jnp.exp(sink - m))

def window_attn_prompt(q, k, v, sinks):
    B, S = q.shape[:2]
    NC = S // CHUNK
    qc = q.reshape(B, NC, CHUNK, A_KV_HEADS, A_GROUP, HEAD_DIM)
    pad = ((0, 0), (WIN_CHUNKS, 0), (0, 0), (0, 0), (0, 0))
    kp = jnp.pad(k.reshape(B, NC, CHUNK, A_KV_HEADS, HEAD_DIM), pad)
    vp = jnp.pad(v.reshape(B, NC, CHUNK, A_KV_HEADS, HEAD_DIM), pad)
    kb = jnp.concatenate([kp[:, j:j + NC] for j in range(WIN_CHUNKS + 1)], axis=2)
    vb = jnp.concatenate([vp[:, j:j + NC] for j in range(WIN_CHUNKS + 1)], axis=2)
    s = jnp.einsum('bnikgd,bnjkd->bnkgij', qc, kb,
                   preferred_element_type=jnp.float32) * (HEAD_DIM ** -0.5)
    qi = jnp.arange(CHUNK)
    kj = jnp.arange(BAND)
    dist = jnp.abs(qi[:, None] + WIN_ROWS - kj[None, :]).astype(jnp.float32)
    bias = -alibi_slopes(A_HEADS).reshape(A_KV_HEADS, A_GROUP, 1, 1) * dist
    valid = (jnp.arange(NC)[:, None] * CHUNK - WIN_ROWS + kj[None, :]) >= 0
    s = jnp.where(valid[:, None, None, None, :], s + bias, NEG_INF)
    p = sink_softmax(s, sinks.astype(jnp.float32).reshape(A_KV_HEADS, A_GROUP, 1, 1))
    o = jnp.einsum('bnkgij,bnjkd->bnikgd', p.astype(v.dtype), vb)
    return o.reshape(B, S, A_WIDTH)

def window_attn_sample(q, k, v, ck, cv, sinks):
    Bd, T = q.shape[:2]
    kk = jnp.concatenate([ck, k], axis=1)
    vv = jnp.concatenate([cv, v], axis=1)
    s = jnp.einsum('bikgd,bjkd->bkgij', q, kk,
                   preferred_element_type=jnp.float32) * (HEAD_DIM ** -0.5)
    dist = jnp.abs(jnp.arange(T)[:, None] + WIN_ROWS
                   - jnp.arange(WIN_ROWS + T)[None, :]).astype(jnp.float32)
    s = s - alibi_slopes(A_HEADS).reshape(A_KV_HEADS, A_GROUP, 1, 1) * dist
    p = sink_softmax(s, sinks.astype(jnp.float32).reshape(A_KV_HEADS, A_GROUP, 1, 1))
    o = jnp.einsum('bkgij,bjkd->bikgd', p.astype(v.dtype), vv)
    return o.reshape(Bd, T, A_WIDTH), kk[:, -WIN_ROWS:], vv[:, -WIN_ROWS:]

def diff_lambda(lq1, lk1, lq2, lk2, layer):
    f = jnp.float32
    return (jnp.exp(jnp.sum(lq1.astype(f) * lk1.astype(f)))
            - jnp.exp(jnp.sum(lq2.astype(f) * lk2.astype(f))) + lambda_init(layer))

def diff_weighted_values(q, k, v, qpos, kpos, valid, lam):
    s = jnp.einsum('bihmd,bjhmd->bhmij', q, k,
                   preferred_element_type=jnp.float32) * (HEAD_DIM ** -0.5)
    dist = jnp.abs(qpos[:, None] - kpos[None, :]).astype(jnp.float32)
    s = s - alibi_slopes(B_HEADS)[:, None, None, None] * dist
    if valid is not None:
        s = jnp.where(valid, s, NEG_INF)
    p = jax.nn.softmax(s, axis=-1)
    a = p[:, :, 0] - lam * p[:, :, 1]
    return jnp.einsum('bhij,bjhe->bihe', a.astype(v.dtype), v)

def diff_attn_prompt(q, k, v, lam):
    B, S = q.shape[:2]
    NQB = S // Q_BLOCK
    qb = q.reshape(B, NQB, Q_BLOCK, B_HEADS, 2, HEAD_DIM).transpose(1, 0, 2, 3, 4, 5)
    kpos = jnp.arange(S)

    def block(args):
        qblk, n = args
        qpos = n * Q_BLOCK + jnp.arange(Q_BLOCK)
        valid = (kpos[None, :] // CHUNK) <= (qpos[:, None] // CHUNK)
        return diff_weighted_values(qblk, k, v, qpos, kpos, valid, lam)

    o = lax.map(block, (qb, jnp.arange(NQB)))
    return o.transpose(1, 0, 2, 3, 4).reshape(B, S, B_HEADS, B_V_DIM)

def diff_attn_sample(q, k, v, ck, cv, lam):
    Bd, T = q.shape[:2]
    P = ck.shape[1]
    kk = jnp.concatenate([ck.reshape(Bd, P, B_HEADS, 2, HEAD_DIM), k], axis=1)
    vv = jnp.concatenate([cv, v], axis=1)
    qpos = P + jnp.arange(T)
    kpos = jnp.arange(P + T)
    return diff_weighted_values(q, kk, vv, qpos, kpos, None, lam)

def diff_out(o, subln_g, layer):
    B, S = o.shape[:2]
    o = rms_norm(o, subln_g, SUBLN_EPS) * (1.0 - lambda_init(layer))
    return o.reshape(B, S, B_WIDTH)

def merge(oa, za, ob, zb, w_out):
    return jnp.concatenate([oa * jax.nn.silu(za), ob * jax.nn.silu(zb)], axis=-1) @ w_out

def finish(x, mix, p, post_g, w_gate, w_ple, ple_g):
    h = x + rms_norm(mix, post_g)
    return h + jax.nn.sigmoid(h @ w_gate) * rms_norm(p @ w_ple, ple_g)

def setup_inputs(seed: int = 0) -> dict:
    key = jax.random.key(seed)
    ks = jax.random.split(key, 24)
    f = jnp.float32
    n = lambda k, shape, s=1.0: (jax.random.normal(k, shape, f) * s).astype(f)
    return {
        'x_prompt': n(ks[0], (BATCH, SEQ, D_MODEL)),
        'x_sample': n(ks[1], (DEC_BATCH, DEC_SEQ, D_MODEL)),
        'cache_a_k': n(ks[2], (DEPTH, DEC_BATCH, WIN_ROWS, A_KV_HEADS, HEAD_DIM)),
        'cache_a_v': n(ks[3], (DEPTH, DEC_BATCH, WIN_ROWS, A_KV_HEADS, HEAD_DIM)),
        'cache_b_k': n(ks[4], (DEPTH, DEC_BATCH, PAST_LEN, B_HEADS, 2 * HEAD_DIM)),
        'cache_b_v': n(ks[5], (DEPTH, DEC_BATCH, PAST_LEN, B_HEADS, B_V_DIM)),
        'p_prompt': n(ks[6], (DEPTH, BATCH, SEQ, PLE_DIM)),
        'p_sample': n(ks[7], (DEPTH, DEC_BATCH, DEC_SEQ, PLE_DIM)),
        'pre_norm_g': 1.0 + n(ks[8], (DEPTH, D_MODEL), 0.05),
        'post_norm_g': 1.0 + n(ks[9], (DEPTH, D_MODEL), 0.05),
        'w_in': n(ks[10], (DEPTH, D_MODEL, IN_COLS), D_MODEL ** -0.5),
        'a_sinks': n(ks[11], (DEPTH, A_HEADS), 0.5),
        'b_lambda_q1': n(ks[12], (DEPTH, HEAD_DIM), 0.1),
        'b_lambda_k1': n(ks[13], (DEPTH, HEAD_DIM), 0.1),
        'b_lambda_q2': n(ks[14], (DEPTH, HEAD_DIM), 0.1),
        'b_lambda_k2': n(ks[15], (DEPTH, HEAD_DIM), 0.1),
        'b_subln_g': 1.0 + n(ks[16], (DEPTH, B_V_DIM), 0.05),
        'w_out': n(ks[17], (DEPTH, MIX_WIDTH, D_MODEL), MIX_WIDTH ** -0.5),
        'w_gate': n(ks[18], (DEPTH, D_MODEL, D_MODEL), D_MODEL ** -0.5),
        'w_ple': n(ks[19], (DEPTH, PLE_DIM, D_MODEL), PLE_DIM ** -0.5),
        'ple_norm_g': 1.0 + n(ks[20], (DEPTH, D_MODEL), 0.05),
    }

def reference(x_prompt, x_sample, cache_a_k, cache_a_v, cache_b_k, cache_b_v,
              p_prompt, p_sample, pre_norm_g, post_norm_g, w_in, a_sinks,
              b_lambda_q1, b_lambda_k1, b_lambda_q2, b_lambda_k2, b_subln_g,
              w_out, w_gate, w_ple, ple_norm_g):
    xp, xs = x_prompt, x_sample
    akp, avp, bkp, bvp = [], [], [], []
    aks, avs, bks, bvs = [], [], [], []
    for l in range(DEPTH):
        lam = diff_lambda(b_lambda_q1[l], b_lambda_k1[l], b_lambda_q2[l], b_lambda_k2[l], l)

        B, S = xp.shape[:2]
        qa, ka, va, za, qb, kb, vb, zb = split_in(rms_norm(xp, pre_norm_g[l]), w_in[l])
        oa = window_attn_prompt(qa, ka, va, a_sinks[l])
        ob = diff_out(diff_attn_prompt(qb, kb, vb, lam), b_subln_g[l], l)
        mix = merge(oa, za, ob, zb, w_out[l])
        xp = finish(xp, mix, p_prompt[l], post_norm_g[l], w_gate[l], w_ple[l], ple_norm_g[l])
        akp.append(ka[:, S - WIN_ROWS:])
        avp.append(va[:, S - WIN_ROWS:])
        bkp.append(kb.reshape(B, S, B_HEADS, 2 * HEAD_DIM))
        bvp.append(vb)

        Bd, T = xs.shape[:2]
        qa, ka, va, za, qb, kb, vb, zb = split_in(rms_norm(xs, pre_norm_g[l]), w_in[l])
        oa, nak, nav = window_attn_sample(qa, ka, va, cache_a_k[l], cache_a_v[l], a_sinks[l])
        ob = diff_out(diff_attn_sample(qb, kb, vb, cache_b_k[l], cache_b_v[l], lam), b_subln_g[l], l)
        mix = merge(oa, za, ob, zb, w_out[l])
        xs = finish(xs, mix, p_sample[l], post_norm_g[l], w_gate[l], w_ple[l], ple_norm_g[l])
        aks.append(nak)
        avs.append(nav)
        bks.append(kb.reshape(Bd, T, B_HEADS, 2 * HEAD_DIM))
        bvs.append(vb)

    return (xp, xs,
            jnp.stack(akp), jnp.stack(avp), jnp.stack(bkp), jnp.stack(bvp),
            jnp.stack(aks), jnp.stack(avs), jnp.stack(bks), jnp.stack(bvs))


_drawn_inputs = setup_inputs


def setup_inputs(seed=0):
    import zlib

    import numpy as np

    out = dict(_drawn_inputs(seed))
    spreads = {}
    factors = {'a_sinks': 5.123, 'b_lambda_q2': 8.0, 'ple_norm_g': 3.191}
    for name, (base, spread) in spreads.items():
        noise = np.random.default_rng([zlib.crc32(name.encode()), seed]).standard_normal(out[name].shape)
        drawn = base * np.exp(spread * noise) if base else spread * noise
        out[name] = __import__('jax').numpy.asarray(drawn.astype(out[name].dtype))
    for name, factor in factors.items():
        out[name] = (out[name] * factor).astype(out[name].dtype)
    return out
```

```python
from contextlib import ExitStack

import numpy as np
import concourse.bass as bass
from concourse import mybir

F32 = mybir.dt.float32
F32R = mybir.dt.float32r
ALU = mybir.AluOpType
ACT = mybir.ActivationFunctionType
AX_X = mybir.AxisListType.X

P = 128
D = 1024
KT = D // P
SEQ = 1024
NT = SEQ // P
DEC = 8
DSEQ = 16
TOK = SEQ + DEC * DSEQ
TT = TOK // P
NCH = 3
RUN = TOK // NCH
PAST = 1024
CHUNK = 64
NCHUNK = SEQ // CHUNK
BAND = 3 * CHUNK
WIN = 2 * CHUNK
HD = 64
AG = 4
BH = 4
PLE = 256
PKT = PLE // P
ROWS = 5 * P
LAMBDA_INIT = 0.2
EPS = 1e-6
SUB_EPS = 1e-5
MASKED = -1e30
LOWEST = -3e38
SCALE = HD ** -0.5

NQ = 8
NKV = 5
NZ = 8
NB_IN = NQ + 2 * NKV + NZ
G_KV = NQ // 2
G_Z = G_KV + NKV
G_IN = NB_IN // 2


def wait(eng, sem, value):
    if not isinstance(value, int) or value > 0:
        eng.wait_ge(sem, value)


def stages(eng, first, last, period, steps, fresh=True):
    most = max(lag for lag, _ in steps)

    def tick(group, newest, low, high):
        for lag, step in steps:
            at = newest - lag
            g = group + at // period
            if not isinstance(g, int) or low <= g < high:
                step(g, at % period)

    peel = -(-(most + (2 if fresh else 0)) // period)
    start = min(first + peel, last)
    for g in range(first, start):
        for r in range(period):
            tick(g, r, first, last)
    if start < last:
        if last - start == 1:
            for r in range(period):
                tick(start, r, first, last)
        else:
            with eng.Fori(start, last) as g:
                for r in range(period):
                    tick(g, r, first, last)
    for extra in range(most):
        tick(last, extra, first, last)


def encoder_step(nc, xT, pT, w_in, w_out, w_gate, w_ple, gains, lam_in, sinks, tables,
                 kb_cache, vb_cache, ka_cache, va_cache, yT, kT_out, vT_out, rolled_k, rolled_v):
    q_dram = nc.dram_tensor("q_scratch", [NQ, P, TOK], F32, kind="Internal").ap()
    z_dram = nc.dram_tensor("z_scratch", [NZ, P, TOK], F32, kind="Internal").ap()
    vnew_dram = nc.dram_tensor("v_new_scratch", [DEC * DSEQ, ROWS], F32, kind="Internal").ap()

    with ExitStack() as whole:
        oT = whole.enter_context(nc.sbuf_tensor("oT", [P, 8, TOK], F32))
        consts = whole.enter_context(nc.sbuf_tensor("consts", [P, 2 * P], F32))
        ident = consts[:, 0:P]
        ones = consts[:, P:2 * P]
        gain = whole.enter_context(nc.sbuf_tensor("gain", [P, gains.shape[1]], F32))
        g_pre, g_post, g_ple, g_sub = gain[:, 0:8], gain[:, 8:16], gain[:, 16:24], gain[:, 24:25]
        with ExitStack() as attention:
            kT = attention.enter_context(nc.sbuf_tensor("kT", [P, 5, TOK], F32))
            v_tok = attention.enter_context(nc.sbuf_tensor("v_tok", [P, TT, ROWS], F32))
            project(nc, xT, w_in, gains, tables, q_dram, z_dram, vnew_dram, kT_out, vT_out,
                    ka_cache, va_cache, rolled_k, rolled_v, oT, kT, v_tok, consts, gain)
            diff_prompt(nc, q_dram, lam_in, tables, oT, kT, v_tok, ident, g_sub)
            window_prompt(nc, q_dram, sinks, tables, oT, kT, v_tok, ident)
            sample(nc, q_dram, vnew_dram, lam_in, sinks, tables, kb_cache, vb_cache, ka_cache, va_cache,
                   oT, kT, ident, g_sub)
        merge(nc, xT, pT, w_out, w_gate, w_ple, z_dram, yT, oT, ident, ones, g_post, g_ple)


class Maker:

    def __init__(self, nc, ctx, phase):
        self.nc, self.ctx, self.phase = nc, ctx, phase

    def sb(self, name, shape, dtype=F32):
        return self.ctx.enter_context(self.nc.sbuf_tensor(f"{self.phase}_{name}", shape, dtype))

    def ps(self, name, shape):
        return self.ctx.enter_context(self.nc.psum_tensor(f"{self.phase}_{name}", shape, F32))

    def sem(self, name):
        return self.ctx.enter_context(self.nc.semaphore(f"{self.phase}_{name}"))


class Rsqrt:

    def __init__(self, mk, name, rows, cols, width, eps):
        self.v = mk.sb(name + "_mean", [rows, cols])
        self.s = mk.sb(name + "_root", [rows, cols])
        self.y = mk.sb(name + "_guess", [rows, cols])
        self.h = mk.sb(name + "_half", [rows, cols])
        self.c = mk.sb(name + "_corr", [rows, cols])
        self.out = mk.sb(name + "_rstd", [rows, cols])
        self.by_dve = mk.sem(name + "_dve")
        self.by_act = mk.sem(name + "_act")
        self.width, self.eps = width, eps

    def vector(self, dve, total, then=1.0):
        dve.tensor_scalar(self.v[:], total, 1.0 / self.width, self.eps, ALU.mult, ALU.add).then_inc(self.by_dve, 1)
        dve.wait_ge(self.by_act, 1)
        dve.reciprocal(self.y[:], self.s[:]).then_inc(self.by_dve, 1)
        dve.wait_ge(self.by_dve, 2)
        dve.scalar_tensor_tensor(out=self.h[:], in0=self.y[:], scalar=-0.5, in1=self.y[:],
                                 op0=ALU.mult, op1=ALU.mult).then_inc(self.by_dve, 1)
        dve.wait_ge(self.by_dve, 3)
        dve.tensor_tensor(self.c[:], self.h[:], self.v[:], ALU.mult).then_inc(self.by_dve, 1)
        dve.wait_ge(self.by_dve, 4)
        last = dve.scalar_tensor_tensor(out=self.out[:], in0=self.c[:], scalar=1.5, in1=self.y[:],
                                        op0=ALU.add, op1=ALU.mult)
        last.then_inc(self.by_dve, 1)
        dve.wait_ge(self.by_dve, 5)
        if then != 1.0:
            dve.tensor_scalar(self.out[:], self.out[:], then, None, ALU.mult).then_inc(self.by_dve, 1)
            dve.wait_ge(self.by_dve, 6)

    def scalar(self, act):
        act.wait_ge(self.by_dve, 1)
        act.activation(self.s[:], self.v[:], ACT.Sqrt).then_inc(self.by_act, 1)


def three_passes(pe, out, w_hi, w_lo, x_hi, x_lo, start, stop):
    pe.matmul(out, w_hi, x_hi, start=start, stop=False)
    pe.matmul(out, w_hi, x_lo, start=False, stop=False)
    return pe.matmul(out, w_lo, x_hi, start=False, stop=stop)


def run(x, n):
    return x[:, n * RUN:(n + 1) * RUN]


def by_runs(x):
    return x.rearrange("p (n c) -> p n c", n=NCH)


def project(nc, xT, w_in, gains, tables, q_dram, z_dram, vnew_dram, kT_out, vT_out,
            ka_cache, va_cache, rolled_k, rolled_v, oT, kT, v_tok, consts, gain):
    ident, ones, g_pre = consts[:, 0:P], consts[:, P:2 * P], gain[:, 0:8]
    with ExitStack() as ctx:
        mk = Maker(nc, ctx, "in")
        x_hi, x_lo = mk.sb("x_hi", [P, KT, TOK], F32R), mk.sb("x_lo", [P, KT, TOK], F32R)
        w_raw = [mk.sb(f"w_raw{s}", [P, KT, P]) for s in range(2)]
        w_hi = [mk.sb(f"w_hi{s}", [P, KT, P], F32R) for s in range(2)]
        w_lo = [mk.sb(f"w_lo{s}", [P, KT, P], F32R) for s in range(2)]
        squares = [mk.sb(f"squares{s}", [P, TOK]) for s in range(2)]
        rms = mk.sb("rms", [P, TOK])
        tmp = [mk.sb(f"tmp{s}", [P, TOK]) for s in range(2)]
        total = tmp[1]
        diag = total
        norm = Rsqrt(mk, "norm", P, TT, D, EPS)
        x_raw = oT
        acc = [mk.ps(f"acc{s}", [P, NCH, 512]) for s in range(2)]
        small = mk.ps("small", [P, 2, 512])

        consts_in = mk.sem("consts_in")
        x_in = [mk.sem(f"x_in{k}") for k in range(KT)]
        w_in_sem = [mk.sem(f"w_in{s}") for s in range(2)]
        stored = [mk.sem(f"stored{s}") for s in range(2)]
        vnew_stored, rolled = mk.sem("vnew_stored"), mk.sem("rolled")
        x_hi_done, x_lo_done = mk.sem("x_hi_done"), mk.sem("x_lo_done")
        squared, added = mk.sem("squared"), mk.sem("added")
        w_hi_done, w_lo_done = mk.sem("w_hi_done"), mk.sem("w_lo_done")
        product = mk.sem("product")
        evacuated = mk.sem("evacuated")
        sums, diag_done, spread, rms_done = mk.sem("sums"), mk.sem("diag"), mk.sem("spread"), mk.sem("rms_done")
        v_turned, v_copied = mk.sem("v_turned"), mk.sem("v_copied")
        sigmoid, silu = mk.sem("sigmoid"), mk.sem("silu")

        def acc_runs(r):
            return acc[r][:, :, 0:RUN]

        block = ctx.enter_context(nc.Block())

        @block.sync
        def _(sp):
            sp.dma_start(gain[:], gains).then_inc(consts_in, 16)
            sp.dma_start(x_raw[:, 0, :], xT[:, 0, :]).then_inc(x_in[0], 16)
            sp.dma_start(consts[:], tables["consts"]).then_inc(consts_in, 16)

            def load(g, r):
                wait(sp, w_lo_done, 2 * g + r - 1)
                sp.dma_start(w_raw[r][:], w_in[2 * g + r]).then_inc(w_in_sem[r], 16)
                if isinstance(g, int) and g == 0:
                    for k in range(1 + 4 * r, 5 + 3 * r):
                        sp.dma_start(x_raw[:, k, :], xT[:, k, :]).then_inc(x_in[k], 16)

            def store_q(g, r):
                sp.wait_ge(evacuated, 2 * g + r + 1)
                sp.dma_start(q_dram[2 * g + r], tmp[r][:]).then_inc(stored[r], 16)

            def store_kv(g, r):
                sp.wait_ge(evacuated, 2 * g + r + 1)
                if r == 0:
                    sp.dma_start(kT_out[g - G_KV], kT[:, g - G_KV, :]).then_inc(stored[0], 16)
                else:
                    sp.dma_start(vT_out[g - G_KV], tmp[1][:]).then_inc(stored[1], 16)

            def store_z(g, r):
                sp.wait_ge(silu, 2 * (g - G_Z) + r + 1)
                sp.dma_start(z_dram[2 * (g - G_Z) + r], squares[r][:]).then_inc(stored[r], 16)

            stages(sp, 0, G_KV, 2, [(0, load), (1, store_q)])
            stages(sp, G_KV, G_Z, 2, [(0, load), (1, store_kv)], fresh=False)
            sp.dma_start(rolled_k, ka_cache[:, :, DSEQ:WIN]).then_inc(rolled, 16)
            sp.dma_start(rolled_v, va_cache[:, DSEQ:WIN, :]).then_inc(rolled, 16)
            stages(sp, G_Z, G_IN, 2, [(0, load), (2, store_z)], fresh=False)
            sp.wait_ge(v_copied, NKV * 3)
            sp.dma_start(vnew_dram, v_tok[:, TT - 1, :]).then_inc(vnew_stored, 16)
            for s in stored:
                sp.wait_ge(s, 16 * G_IN)
            sp.wait_ge(vnew_stored, 16)
            sp.wait_ge(rolled, 32)

        @block.scalar
        def _(act):
            act.wait_ge(consts_in, 32)
            for k in range(KT):
                act.wait_ge(x_in[k], 16)
                act.activation(x_hi[:, k, :], x_raw[:, k, :], ACT.Copy, scale=g_pre[:, k:k + 1]).then_inc(x_hi_done, 1)
                if k == 0:
                    for r in range(2):
                        act.wait_ge(w_in_sem[r], 16)
                        act.activation(w_hi[r][:], w_raw[r][:], ACT.Copy).then_inc(w_hi_done, 1)
                if k >= 2:
                    act.wait_ge(added, max(2, k - 1))
                act.activation(squares[k % 2][:], x_raw[:, k, :], ACT.Square).then_inc(squared, 1)
            norm.scalar(act)

            def high(g, r):
                act.wait_ge(w_in_sem[r], 16 * (g + 1))
                act.wait_ge(product, 2 * g + r - 1)
                act.activation(w_hi[r][:], w_raw[r][:], ACT.Copy).then_inc(w_hi_done, 1)

            def copy_v(g, r):
                if r == 0:
                    return
                for j, (t0, n) in enumerate(((0, 4), (4, 4), (8, 1))):
                    act.wait_ge(v_turned, 3 * (g - G_KV) + j + 1)
                    act.activation(v_tok[:, t0:t0 + n, bass.ds((g - G_KV) * P, P)],
                                   small[:, j % 2, 0:n * P].rearrange("p (t c) -> p t c", t=n),
                                   ACT.Copy).then_inc(v_copied, 1)

            def gate(g, r):
                act.wait_ge(evacuated, 2 * g + r + 1)
                act.wait_ge(stored[r], 16 * g)
                act.activation(squares[r][:], tmp[r][:], ACT.Sigmoid).then_inc(sigmoid, 1)

            stages(act, 1, G_KV, 2, [(0, high)], fresh=False)
            stages(act, G_KV, G_Z, 2, [(0, high), (2, copy_v)], fresh=False)
            stages(act, G_Z, G_IN, 2, [(0, high), (2, gate)], fresh=True)

        @block.gpsimd
        def _(pool):
            def low(g, r):
                pool.wait_ge(w_hi_done, 2 * g + r + 1)
                wait(pool, product, 2 * g + r - 1)
                pool.tensor_tensor(w_lo[r][:], w_raw[r][:], w_hi[r][:].bitcast(F32),
                                   ALU.subtract).then_inc(w_lo_done, 1)

            low(0, 0)
            pool.wait_ge(squared, 2)
            pool.tensor_tensor(total[:], squares[0][:], squares[1][:], ALU.add).then_inc(added, 2)
            low(0, 1)
            for k in range(2, KT):
                pool.wait_ge(squared, k + 1)
                pool.wait_ge(added, k)
                pool.tensor_tensor(total[:], total[:], squares[k % 2][:], ALU.add).then_inc(added, 1)

            def swish(g, r):
                pool.wait_ge(sigmoid, 2 * (g - G_Z) + r + 1)
                pool.tensor_tensor(squares[r][:], tmp[r][:], squares[r][:], ALU.mult).then_inc(silu, 1)

            stages(pool, 1, G_Z, 2, [(0, low)], fresh=False)
            stages(pool, G_Z, G_IN, 2, [(0, low), (2, swish)], fresh=False)

        @block.tensor
        def _(pe):
            def multiply(g, r):
                pe.wait_ge(w_lo_done, 2 * g + r + 1)
                wait(pe, evacuated, 2 * g + r - 1)
                for k in range(KT):
                    if isinstance(g, int) and g == 0 and r == 0:
                        pe.wait_ge(x_hi_done, k + 1)
                        pe.wait_ge(x_lo_done, k + 1)
                    for n in range(NCH):
                        last = three_passes(pe, acc[r][:, n, 0:RUN], w_hi[r][:, k, :], w_lo[r][:, k, :],
                                            run(x_hi[:, k, :], n), run(x_lo[:, k, :], n),
                                            start=(k == 0), stop=(k == KT - 1))
                last.then_inc(product, 1)

            def turn_v(g, r):
                if r == 0:
                    return
                pe.wait_ge(evacuated, 2 * g + 2)
                for j, (t0, n) in enumerate(((0, 4), (4, 4), (8, 1))):
                    wait(pe, v_copied, 3 * (g - G_KV) + (0, -1, 1)[j])
                    for t in range(n):
                        last = pe.transpose(small[:, j % 2, t * P:(t + 1) * P],
                                            tmp[1][:, (t0 + t) * P:(t0 + t + 1) * P], ident)
                    last.then_inc(v_turned, 1)

            multiply(0, 0)
            pe.wait_ge(added, KT)
            for t in range(TT):
                last = pe.matmul(small[:, 0, t:t + 1], total[:, t * P:(t + 1) * P], ones[:, 0:1],
                                 start=True, stop=True)
            last.then_inc(sums, 1)
            multiply(0, 1)
            pe.wait_ge(diag_done, TT)
            for n in range(NCH):
                if n == 2:
                    pe.wait_ge(rms_done, 1)
                pe.matmul(small[:, n % 2, 0:RUN], ones, run(diag[:], n), start=True, stop=True).then_inc(spread, 1)
            stages(pe, 1, G_KV, 2, [(0, multiply)], fresh=False)
            stages(pe, G_KV, G_Z, 2, [(0, multiply), (1, turn_v)])
            stages(pe, G_Z, G_IN, 2, [(0, multiply)], fresh=False)

        @block.vector
        def _(dve):
            for k in range(KT):
                dve.wait_ge(x_hi_done, k + 1)
                dve.scalar_tensor_tensor(out=x_lo[:, k, :], in0=x_raw[:, k, :], scalar=g_pre[:, k:k + 1],
                                         in1=x_hi[:, k, :].bitcast(F32), op0=ALU.mult,
                                         op1=ALU.subtract).then_inc(x_lo_done, 1)
            dve.wait_ge(sums, 1)
            norm.vector(dve, small[:, 0, 0:TT])
            for t in range(TT):
                dve.tensor_scalar(diag[:, t * P:(t + 1) * P], ident, norm.out[:, t:t + 1], None,
                                  ALU.mult).then_inc(diag_done, 1)
            for n in range(NCH):
                dve.wait_ge(spread, n + 1)
                dve.tensor_copy(run(rms[:], n), small[:, n % 2, 0:RUN]).then_inc(rms_done, 1)
            dve.wait_ge(rms_done, NCH)

            def out_q(g, r):
                dve.wait_ge(product, 2 * g + r + 1)
                wait(dve, stored[r], 16 * g)
                dve.scalar_tensor_tensor(out=by_runs(tmp[r][:]), in0=acc_runs(r), scalar=SCALE,
                                         in1=by_runs(rms[:]), op0=ALU.mult, op1=ALU.mult).then_inc(evacuated, 1)

            def out_kv(g, r):
                dve.wait_ge(product, 2 * g + r + 1)
                if r == 0:
                    to = kT[:, g - G_KV, :]
                else:
                    dve.wait_ge(stored[1], 16 * g)
                    if not isinstance(g, int) or g > G_KV:
                        dve.wait_ge(v_turned, 3 * (g - G_KV))
                    to = tmp[1][:]
                dve.tensor_tensor(by_runs(to), acc_runs(r), by_runs(rms[:]), ALU.mult).then_inc(evacuated, 1)

            def out_z(g, r):
                dve.wait_ge(product, 2 * g + r + 1)
                if isinstance(g, int) and g == G_Z:
                    dve.wait_ge(stored[r], 16 * g)
                    dve.wait_ge(v_turned, 3 * NKV)
                else:
                    dve.wait_ge(silu, 2 * (g - G_Z) + r - 1)
                dve.tensor_tensor(by_runs(tmp[r][:]), acc_runs(r), by_runs(rms[:]), ALU.mult).then_inc(evacuated, 1)

            stages(dve, 0, G_KV, 2, [(0, out_q)])
            stages(dve, G_KV, G_Z, 2, [(0, out_kv)])
            stages(dve, G_Z, G_IN, 2, [(0, out_z)])


def neg_lambda(mk, lam_in):
    vec, prod = mk.sb("lam_vec", [P, 4, HD]), mk.sb("lam_prod", [P, 2, HD])
    dots, exps = mk.sb("lam_dots", [P, 2]), mk.sb("lam_exps", [P, 2])
    out = mk.sb("neg_lambda", [P, 1])
    arrived, by_dve, by_act = mk.sem("lam_in"), mk.sem("lam_dve"), mk.sem("lam_act")

    def load(sp):
        sp.dma_start(vec[:], lam_in).then_inc(arrived, 16)

    def vector(dve):
        dve.wait_ge(arrived, 16)
        dve.tensor_tensor(prod[:], vec[:, 0:4:2, :], vec[:, 1:4:2, :], ALU.mult).then_inc(by_dve, 1)
        dve.wait_ge(by_dve, 1)
        dve.reduce_sum(dots[:], prod[:], axis=AX_X).then_inc(by_dve, 1)
        dve.wait_ge(by_act, 1)
        dve.tensor_scalar(exps[:, 0:1], exps[:, 0:1], LAMBDA_INIT, None, ALU.add).then_inc(by_dve, 1)
        dve.wait_ge(by_dve, 3)
        dve.tensor_tensor(out[:], exps[:, 1:2], exps[:, 0:1], ALU.subtract).then_inc(by_dve, 1)
        dve.wait_ge(by_dve, 4)

    def scalar(act):
        act.wait_ge(by_dve, 2)
        act.activation(exps[:], dots[:], ACT.Exp).then_inc(by_act, 1)

    return out, load, vector, scalar


def diff_prompt(nc, q_dram, lam_in, tables, oT, kT, v_tok, ident, g_sub):
    with ExitStack() as ctx:
        mk = Maker(nc, ctx, "diff")
        q = mk.sb("q", [P, BH, SEQ])
        strip = mk.sb("strip", [P, SEQ])
        slot = [[mk.sb(f"slot{p}{m}", [P, P]) for m in range(2)] for p in range(2)]
        probs = mk.sb("prob", [P, 2, 2, SEQ])
        prob = [probs[:, p] for p in range(2)]
        prob_all = probs[:].rearrange("p a m (b c) -> p (a m b) c", c=P)
        turned = [mk.sb(f"turned{p}", [P, NT, P]) for p in range(2)]
        o = mk.sb("o", [P, BH * NT, P])
        nmax = [mk.sb(f"nmax{p}", [P, 2]) for p in range(2)]
        top = [mk.sb(f"top{p}", [P, 2]) for p in range(2)]
        norm = [mk.sb(f"norm{p}", [P, 2]) for p in range(2)]
        inv = [mk.sb(f"inv{p}", [P, 2]) for p in range(4)]
        coef = mk.sb("coef", [P, 1])
        waited = mk.sb("waited", [P, 1])
        neg_lam, load_lambda, lambda_vector, lambda_scalar = neg_lambda(mk, lam_in)
        ssq = mk.sb("ssq", [P, BH * NT])
        sub = Rsqrt(mk, "sub", P, BH * NT, P, SUB_EPS)
        score = [mk.ps(f"score{m}", [P, SEQ]) for m in range(2)]
        blocks = mk.ps("blocks", [P, 2, 512])
        mixed = mk.ps("mixed", [P, 512])

        q_in, strip_in = mk.sem("q_in"), mk.sem("strip_in")
        padded, q_ready, scored, biased = mk.sem("padded"), mk.sem("q_ready"), mk.sem("scored"), mk.sem("biased")
        max_ready, exp_done, inv_done = mk.sem("max_ready"), mk.sem("exp_done"), mk.sem("inv_done")
        coef_done, weighted = mk.sem("coef_done"), mk.sem("weighted")
        block_ready, block_out = mk.sem("block_ready"), mk.sem("block_out")
        av_done, o_done, stripped = mk.sem("av_done"), mk.sem("o_done"), mk.sem("stripped")
        o_squared, ssq_done, scaled = mk.sem("o_squared"), mk.sem("ssq_done"), mk.sem("scaled")
        o_turned, o_out = mk.sem("o_turned"), mk.sem("o_out")

        banks_before = [sum(1 + (u >= 4) for u in range(t)) for t in range(NT + 1)]
        PER_HEAD = banks_before[NT]

        def banks(t):
            return [(b, min(4, t + 1 - 4 * b)) for b in range(1 + (t >= 4))]

        block = ctx.enter_context(nc.Block())

        @block.sync
        def _(sp):
            load_lambda(sp)
            sp.dma_start(strip[:], tables["strip"]).then_inc(strip_in, 16)
            sp.dma_start(q[:], q_dram[NQ // 2:NQ, :, 0:SEQ].rearrange("b p t -> p b t")).then_inc(q_in, 16)

        @block.gpsimd
        def _(pool):
            for p in range(2):
                for m in range(2):
                    pool.memset(slot[p][m][:], 0.0).then_inc(padded, 1)
            pool.wait_ge(q_in, 16)
            pool.wait_ge(padded, 4)

            def place(h, t):
                wait(pool, scored, 2 * (8 * h + t) - 2)
                for m in range(2):
                    rows = slice(m * HD, (m + 1) * HD)
                    pool.tensor_copy(slot[t % 2][m][rows, :], q[rows, h, t * P:(t + 1) * P]).then_inc(q_ready, 1)

            stages(pool, 0, BH, NT, [(0, place)])

        @block.tensor
        def _(pe):
            def scores(h, t):
                for m in range(2):
                    pe.wait_ge(q_ready, 2 * (8 * h + t) + m + 1)
                    wait(pe, biased, 2 * (8 * h + t) + m - 1)
                    for c in range(0, (t + 1) * P, 512):
                        n = min(512, (t + 1) * P - c)
                        last = pe.matmul(score[m][:, c:c + n], slot[t % 2][m][:], kT[:, h + 1, c:c + n],
                                         start=True, stop=True)
                    last.then_inc(scored, 1)

            def turn(h, t):
                pe.wait_ge(weighted, 8 * h + t + 1)
                for b, n in banks(t):
                    count = PER_HEAD * h + banks_before[t] + b
                    wait(pe, block_out, count - 1)
                    side = (banks_before[t] + b) % 2
                    for j in range(n):
                        k = 4 * b + j
                        last = pe.transpose(blocks[:, side, j * P:(j + 1) * P],
                                            prob[t % 2][:, 0, k * P:(k + 1) * P], ident)
                    last.then_inc(block_ready, 1)

            def average(h, t):
                pe.wait_ge(block_out, PER_HEAD * h + banks_before[t + 1])
                wait(pe, o_done, 8 * h + t)
                for k in range(t + 1):
                    last = pe.matmul(mixed[:, 0:P], turned[t % 2][:, k, :], v_tok[:, k, bass.ds((h + 1) * P, P)],
                                     start=(k == 0), stop=(k == t))
                last.then_inc(av_done, 1)

            stages(pe, 0, BH, NT, [(0, scores), (1, turn), (2, average)])
            for j in range(BH * NT // 4):
                pe.wait_ge(scaled, BH * NT)
                if j >= 2:
                    pe.wait_ge(o_out, j - 1)
                for i in range(4):
                    last = pe.transpose(blocks[:, j % 2, i * P:(i + 1) * P], o[:, 4 * j + i, :], ident)
                last.then_inc(o_turned, 1)

        @block.vector
        def _(dve):
            dve.wait_ge(strip_in, 16)
            lambda_vector(dve)

            def negate(item, t, m):
                dve.wait_ge(biased, 2 * item + m + 1)
                dve.tensor_scalar(nmax[t % 2][:, m:m + 1], top[t % 2][:, m:m + 1], -1.0, None,
                                  ALU.mult).then_inc(max_ready, 1)

            def bias(h, t):
                item = 8 * h + t
                if t == 0 and not (isinstance(h, int) and h == 0):
                    dve.wait_ge(biased, 2 * item)
                    dve.tensor_scalar(strip[:], strip[:], 0.25, None, ALU.mult).then_inc(stripped, 1)
                    dve.wait_ge(stripped, h)
                n = (t + 1) * P
                wait(dve, block_ready, PER_HEAD * h + (banks_before[t - 1] if t else -2))
                dve.wait_ge(scored, 2 * item + 1)
                dve.memset(waited[:], 0.0)
                for m in range(2):
                    if m:
                        dve.wait_ge(scored, 2 * item + 2)
                        negate(item, t, 0)
                    dve.tensor_tensor_reduce(prob[t % 2][:, m, 0:n], score[m][:, 0:n], strip[:, SEQ - n:SEQ],
                                             1.0, LOWEST, ALU.add, ALU.max,
                                             top[t % 2][:, m:m + 1]).then_inc(biased, 1)
                negate(item, t, 1)

            def weigh(h, t):
                item = 8 * h + t
                dve.wait_ge(exp_done, 2 * item + 2)
                dve.reciprocal(inv[t % 4][:], norm[t % 2][:]).then_inc(inv_done, 1)
                dve.wait_ge(inv_done, item + 1)
                dve.scalar_tensor_tensor(out=coef[:], in0=inv[t % 4][:, 1:2], scalar=neg_lam[:, 0:1],
                                         in1=norm[t % 2][:, 0:1], op0=ALU.mult, op1=ALU.mult).then_inc(coef_done, 1)
                dve.wait_ge(coef_done, item + 1)
                n = (t + 1) * P
                dve.scalar_tensor_tensor(out=prob[t % 2][:, 0, 0:n], in0=prob[t % 2][:, 1, 0:n],
                                         scalar=coef[:, 0:1], in1=prob[t % 2][:, 0, 0:n],
                                         op0=ALU.mult, op1=ALU.add).then_inc(weighted, 1)

            def take(h, t):
                dve.wait_ge(av_done, 8 * h + t + 1)
                dve.tensor_scalar(o[:, 8 * h + t, :], mixed[:, 0:P], inv[t % 4][:, 0:1], None,
                                  ALU.mult).then_inc(o_done, 1)

            stages(dve, 0, BH, NT, [(3, take), (1, weigh), (0, bias)])
            dve.wait_ge(o_squared, 1)
            dve.reduce_sum(ssq[:], prob_all, axis=AX_X).then_inc(ssq_done, 1)
            dve.wait_ge(ssq_done, 1)
            sub.vector(dve, ssq[:], then=1.0 - LAMBDA_INIT)
            for i in range(BH * NT):
                dve.tensor_scalar(o[:, i, :], o[:, i, :], sub.out[:, i:i + 1], None, ALU.mult).then_inc(scaled, 1)

        @block.scalar
        def _(act):
            lambda_scalar(act)

            def clear(h, t):
                wait(act, av_done, 8 * h + t - 1)
                for b, n in banks(t):
                    count = PER_HEAD * h + banks_before[t] + b
                    side = (banks_before[t] + b) % 2
                    act.wait_ge(block_ready, count + 1)
                    act.activation(turned[t % 2][:, 4 * b:4 * b + n, :],
                                   blocks[:, side, 0:n * P].rearrange("p (k c) -> p k c", k=n),
                                   ACT.Copy).then_inc(block_out, 1)

            def exponent(h, t):
                item = 8 * h + t
                wait(act, weighted, item - 1)
                n = (t + 1) * P
                for m in range(2):
                    act.wait_ge(max_ready, 2 * item + m + 1)
                    act.activation(prob[t % 2][:, m, 0:n], prob[t % 2][:, m, 0:n], ACT.Exp,
                                   bias=nmax[t % 2][:, m:m + 1],
                                   accum_out=norm[t % 2][:, m:m + 1]).then_inc(exp_done, 1)

            stages(act, 0, BH, NT, [(1, clear), (0, exponent)])
            act.wait_ge(o_done, BH * NT)
            act.activation(prob_all, o[:], ACT.Square).then_inc(o_squared, 1)
            sub.scalar(act)
            for j in range(BH * NT // 4):
                act.wait_ge(o_turned, j + 1)
                act.activation(oT[:, 4 + j // 2, 512 * (j % 2):512 * (j % 2) + 512], blocks[:, j % 2, :],
                               ACT.Copy, scale=g_sub).then_inc(o_out, 1)
            act.wait_ge(o_out, BH * NT // 4)


def window_prompt(nc, q_dram, sinks, tables, oT, kT, v_tok, ident):
    with ExitStack() as ctx:
        mk = Maker(nc, ctx, "win")
        q = mk.sb("q", [P, AG, SEQ])
        bias_tab = mk.sb("bias", [P, AG, BAND])
        nsink = mk.sb("nsink", [P, AG])
        slot = [mk.sb(f"slot{p}", [P, AG, P]) for p in range(2)]
        prob = [mk.sb(f"prob{p}", [P, AG, 2 * P]) for p in range(2)]
        turned = [mk.sb(f"turned{p}", [P, 2, AG * P]) for p in range(2)]
        o = [mk.sb(f"o{p}", [P, AG, P]) for p in range(2)]
        top = [mk.sb(f"top{p}", [P, AG]) for p in range(2)]
        nmax = [mk.sb(f"nmax{p}", [P, AG]) for p in range(2)]
        over = [mk.sb(f"over{p}", [P, AG]) for p in range(2)]
        sink_e = [mk.sb(f"sink_e{p}", [P, AG]) for p in range(2)]
        norm = [mk.sb(f"norm{p}", [P, AG]) for p in range(2)]
        den = [mk.sb(f"den{p}", [P, AG]) for p in range(2)]
        inv = [mk.sb(f"inv{p}", [P, AG]) for p in range(2)]
        waited = mk.sb("waited", [P, 1])
        score = [mk.ps(f"score{p}", [P, 2, 512]) for p in range(2)]
        blocks = mk.ps("blocks", [P, 2, 512])
        mixed = mk.ps("mixed", [P, 512])
        o_turn = mk.ps("o_turn", [P, 512])

        tabs_in, q_in = mk.sem("tabs_in"), mk.sem("q_in")
        padded, nsink_done, q_ready, scored = mk.sem("padded"), mk.sem("nsink_done"), mk.sem("q_ready"), mk.sem("scored")
        biased, max_ready, over_done = mk.sem("biased"), mk.sem("max_ready"), mk.sem("over_done")
        exp_done, den_done, inv_done = mk.sem("exp_done"), mk.sem("den_done"), mk.sem("inv_done")
        block_ready, out_act, out_dve = mk.sem("block_ready"), mk.sem("out_act"), mk.sem("out_dve")
        av_done, o_done, o_turned, o_out = mk.sem("av_done"), mk.sem("o_done"), mk.sem("o_turned"), mk.sem("o_out")

        def seen(g, r):
            if isinstance(g, int) and g == 0:
                return P, CHUNK * (r + 1)
            return CHUNK * r, BAND

        block = ctx.enter_context(nc.Block())

        @block.sync
        def _(sp):
            sp.dma_start(q[:], q_dram[0:AG, :, 0:SEQ].rearrange("b p t -> p b t")).then_inc(q_in, 16)
            sp.dma_start(bias_tab[:], tables["band"]).then_inc(tabs_in, 16)
            sp.dma_start(nsink[:], sinks[:, 0:AG]).then_inc(tabs_in, 16)

        @block.gpsimd
        def _(pool):
            for p in range(2):
                pool.memset(slot[p][:], 0.0).then_inc(padded, 1)
                pool.memset(prob[p][:], 0.0).then_inc(padded, 1)
            pool.wait_ge(q_in, 16)
            pool.wait_ge(padded, 4)

            def place(g, r):
                wait(pool, scored, 2 * g + r - 1)
                for m in range(2):
                    rows, cols = slice(m * HD, (m + 1) * HD), slice(m * CHUNK, (m + 1) * CHUNK)
                    pool.tensor_copy(slot[r][rows, :, cols],
                                     q[rows, :, bass.ds((2 * g + r) * CHUNK, CHUNK)]).then_inc(q_ready, 1)

            stages(pool, 0, NCHUNK // 2, 2, [(0, place)])

        @block.tensor
        def _(pe):
            def scores(g, r):
                item = 2 * g + r
                _, n = seen(g, r)
                pe.wait_ge(q_ready, 2 * item + 2)
                wait(pe, biased, AG * (item - 1))
                for h in range(AG):
                    last = pe.matmul(score[r][:, h // 2, (h % 2) * 256:(h % 2) * 256 + n], slot[r][:, h, :],
                                     kT[:, 0, bass.ds((item + 1) * CHUNK - n, n)], start=True, stop=True)
                last.then_inc(scored, 1)

            def turn(g, r):
                item = 2 * g + r
                pe.wait_ge(exp_done, (AG + 1) * (item + 1))
                first = 1 if isinstance(g, int) and g == 0 else 0
                for b in range(first, 2):
                    wait(pe, (out_act, out_dve)[b], item)
                    for h in range(AG):
                        last = pe.transpose(blocks[:, b, h * P:(h + 1) * P],
                                            prob[r][:, h, b * P:(b + 1) * P], ident)
                last.then_inc(block_ready, 1)

            def average(g, r):
                item = 2 * g + r
                pe.wait_ge(out_act, item + 1)
                pe.wait_ge(out_dve, item + 1)
                wait(pe, o_done, item)
                first = 1 if isinstance(g, int) and g == 0 else 0
                for h in range(AG):
                    for b in range(first, 2):
                        last = pe.matmul(mixed[:, h * P:(h + 1) * P], turned[r][:, b, h * P:(h + 1) * P],
                                         v_tok[:, g - 1 + b, 0:P], start=(b == first), stop=(b == 1))
                last.then_inc(av_done, 1)

            def turn_o(g, r):
                item = 2 * g + r
                pe.wait_ge(o_done, item + 1)
                wait(pe, o_out, 2 * item)
                for h in range(AG):
                    last = pe.transpose(o_turn[:, h * P:(h + 1) * P], o[r][:, h, :], ident)
                last.then_inc(o_turned, 1)

            stages(pe, 0, NCHUNK // 2, 2, [(0, scores), (1, turn), (2, average), (3, turn_o)])

        @block.vector
        def _(dve):
            dve.wait_ge(tabs_in, 32)
            dve.wait_ge(padded, 4)
            dve.tensor_scalar(nsink[:], nsink[:], -1.0, None, ALU.mult).then_inc(nsink_done, 1)
            dve.wait_ge(nsink_done, 1)

            def bias(g, r):
                item = 2 * g + r
                col, n = seen(g, r)
                dve.wait_ge(scored, item + 1)
                wait(dve, block_ready, item - 1)
                dve.memset(waited[:], 0.0)
                for h in range(AG):
                    dve.tensor_tensor_reduce(prob[r][:, h, col:col + n],
                                             score[r][:, h // 2, (h % 2) * 256:(h % 2) * 256 + n],
                                             bias_tab[:, h, BAND - n:BAND], 1.0, LOWEST, ALU.add, ALU.max,
                                             top[r][:, h:h + 1]).then_inc(biased, 1)
                dve.wait_ge(biased, AG * (item + 1))
                dve.scalar_tensor_tensor(out=nmax[r][:], in0=top[r][:], scalar=-1.0, in1=nsink[:],
                                         op0=ALU.mult, op1=ALU.min).then_inc(max_ready, 1)
                dve.wait_ge(max_ready, item + 1)
                dve.tensor_tensor(over[r][:], nmax[r][:], nsink[:], ALU.subtract).then_inc(over_done, 1)

            def total(g, r):
                item = 2 * g + r
                dve.wait_ge(exp_done, (AG + 1) * (item + 1))
                dve.tensor_tensor(den[r][:], norm[r][:], sink_e[r][:], ALU.add).then_inc(den_done, 1)
                dve.wait_ge(den_done, item + 1)
                dve.reciprocal(inv[r][:], den[r][:]).then_inc(inv_done, 1)

            def clear(g, r):
                item = 2 * g + r
                dve.wait_ge(block_ready, item + 1)
                dve.tensor_copy(turned[r][:, 1, :], blocks[:, 1, :]).then_inc(out_dve, 1)

            def take(g, r):
                item = 2 * g + r
                dve.wait_ge(av_done, item + 1)
                wait(dve, o_turned, item - 1)
                dve.tensor_tensor(o[r][:], mixed[:].rearrange("p (h c) -> p h c", h=AG),
                                  inv[r][:, :, None].to_broadcast([P, AG, P]), ALU.mult).then_inc(o_done, 1)

            stages(dve, 0, NCHUNK // 2, 2, [(3, take), (1, total), (0, bias), (1, clear)])

        @block.scalar
        def _(act):
            def exponent(g, r):
                item = 2 * g + r
                col, n = seen(g, r)
                act.wait_ge(over_done, item + 1)
                for h in range(AG):
                    act.activation(prob[r][:, h, col:col + n], prob[r][:, h, col:col + n], ACT.Exp,
                                   bias=nmax[r][:, h:h + 1], accum_out=norm[r][:, h:h + 1]).then_inc(exp_done, 1)
                act.activation(sink_e[r][:], over[r][:], ACT.Exp).then_inc(exp_done, 1)

            def clear(g, r):
                item = 2 * g + r
                act.wait_ge(block_ready, item + 1)
                if isinstance(g, int) and g == 0:
                    act.nop().then_inc(out_act, 1)
                else:
                    act.activation(turned[r][:, 0, :], blocks[:, 0, :], ACT.Copy).then_inc(out_act, 1)

            def store_o(g, r):
                item = 2 * g + r
                act.wait_ge(o_turned, item + 1)
                for m in range(2):
                    rows = slice(m * HD, (m + 1) * HD)
                    act.activation(oT[rows, 0:AG, bass.ds(item * CHUNK, CHUNK)],
                                   o_turn[:].rearrange("p (h c) -> p h c", h=AG)[rows, :, m * CHUNK:(m + 1) * CHUNK],
                                   ACT.Copy).then_inc(o_out, 1)

            stages(act, 0, NCHUNK // 2, 2, [(1, clear), (0, exponent), (3, store_o)])


def sample(nc, q_dram, vnew_dram, lam_in, sinks, tables, kb_cache, vb_cache, ka_cache, va_cache,
           oT, kT, ident, g_sub):
    ROW = 2 * DSEQ
    with ExitStack() as ctx:
        mk = Maker(nc, ctx, "smp")
        kb = [mk.sb(f"kb{p}", [P, BH, PAST]) for p in range(2)]
        vb = [mk.sb(f"vb{p}", [P, PAST // P, BH * P]) for p in range(2)]
        ka = [mk.sb(f"ka{p}", [P, WIN]) for p in range(2)]
        va = [mk.sb(f"va{p}", [P, P]) for p in range(2)]
        vn = [mk.sb(f"vn{p}", [DSEQ, ROWS]) for p in range(2)]
        bias_b, bias_a = mk.sb("bias_b", [P, PAST + DSEQ]), mk.sb("bias_a", [P, WIN + DSEQ])
        pick = mk.sb("pick", [P, HD])
        is_map = mk.sb("is_map", [P, 2])
        sink = mk.sb("sink", [P, AG + 1])
        nsink = mk.sb("nsink", [P, 1])
        row_coef = mk.sb("row_coef", [P, 1])
        q = mk.sb("q", [P, 8, DEC * DSEQ])
        slot_b = [mk.sb(f"slot_b{p}", [P, BH * P]) for p in range(2)]
        slot_a = [mk.sb(f"slot_a{p}", [P, P]) for p in range(2)]
        prob_b = [mk.sb(f"prob_b{p}", [P, PAST + DSEQ]) for p in range(2)]
        prob_a = [mk.sb(f"prob_a{p}", [P, WIN + DSEQ]) for p in range(2)]
        turned = [mk.sb(f"turned{p}", [P, 11, P]) for p in range(2)]
        waited = mk.sb("waited", [P, 1])
        o_b, o_a = mk.sb("o_b", [P, P]), mk.sb("o_a", [P, P])
        o_all = mk.sb("o_all", [HD, DEC, P])
        o_sq = mk.sb("o_sq", [HD, DEC, P])
        ssq = mk.sb("ssq", [HD, DEC])
        sub = Rsqrt(mk, "sub", HD, DEC, P, SUB_EPS)
        neg_lam, load_lambda, lambda_vector, lambda_scalar = neg_lambda(mk, lam_in)
        top = [mk.sb(f"top{p}", [P, 2]) for p in range(2)]
        nmax = [mk.sb(f"nmax{p}", [P, 2]) for p in range(2)]
        over = [mk.sb(f"over{p}", [P, 1]) for p in range(2)]
        norm = [mk.sb(f"norm{p}", [P, 3]) for p in range(2)]
        den = [mk.sb(f"den{p}", [P, 2]) for p in range(2)]
        inv = [mk.sb(f"inv{p}", [P, 2]) for p in range(2)]
        coef = [mk.sb(f"coef{p}", [P, 1]) for p in range(2)]
        score = mk.ps("score", [P, 3, 512])
        blocks = mk.ps("blocks", [P, 2, 512])
        mixed_b, mixed_a, post = mk.ps("mixed_b", [P, 512]), mk.ps("mixed_a", [P, 512]), mk.ps("post", [P, 512])
        score_b = score[:].rearrange("p b c -> p (b c)")[:, 0:PAST + DSEQ]
        score_a = score[:, 2, P:P + WIN + DSEQ]

        tabs_in, q_in = mk.sem("tabs_in"), mk.sem("q_in")
        kb_in = [mk.sem(f"kb_in{p}") for p in range(2)]
        vb_in = [mk.sem(f"vb_in{p}") for p in range(2)]
        padded, rows_done, q_ready, scored = mk.sem("padded"), mk.sem("rows_done"), mk.sem("q_ready"), mk.sem("scored")
        biased, max_ready, over_done = mk.sem("biased"), mk.sem("max_ready"), mk.sem("over_done")
        exp_done, den_done, inv_done = mk.sem("exp_done"), mk.sem("den_done"), mk.sem("inv_done")
        coef_done, block_ready = mk.sem("coef_done"), mk.sem("block_ready")
        out_act, out_dve = mk.sem("out_act"), mk.sem("out_dve")
        av_done, o_done, posted = mk.sem("av_done"), mk.sem("o_done"), mk.sem("posted")
        kept, stored_a = mk.sem("kept"), mk.sem("stored_a")
        o_squared, ssq_done, scaled = mk.sem("o_squared"), mk.sem("ssq_done"), mk.sem("scaled")
        o_turned = mk.sem("o_turned")

        block = ctx.enter_context(nc.Block())

        @block.sync
        def _(sp):
            load_lambda(sp)
            sp.dma_start(q[:], q_dram[:, :, SEQ:TOK].rearrange("b p t -> p b t")).then_inc(q_in, 16)
            sp.dma_start(bias_b[:], tables["sample_b"]).then_inc(tabs_in, 16)
            sp.dma_start(bias_a[:], tables["sample_a"]).then_inc(tabs_in, 16)
            sp.dma_start(pick[:], tables["pick"]).then_inc(tabs_in, 16)
            sp.dma_start(is_map[:], tables["is_map"]).then_inc(tabs_in, 16)
            sp.dma_start(sink[:], sinks).then_inc(tabs_in, 16)

            def load(g, r):
                item = 2 * g + r
                wait(sp, scored, item - 1)
                sp.dma_start(kb[r][:], kb_cache[item]).then_inc(kb_in[r], 16)
                sp.dma_start(ka[r][:], ka_cache[item]).then_inc(kb_in[r], 16)
                wait(sp, av_done, item - 1)
                sp.dma_start(vb[r][:], vb_cache[item]).then_inc(vb_in[r], 16)
                sp.dma_start(va[r][:], va_cache[item]).then_inc(vb_in[r], 16)
                sp.dma_start(vn[r][:], vnew_dram[bass.ds(item * DSEQ, DSEQ), :]).then_inc(vb_in[r], 16)

            stages(sp, 0, DEC // 2, 2, [(0, load)])

        @block.gpsimd
        def _(pool):
            for p in range(2):
                pool.memset(slot_b[p][:], 0.0).then_inc(padded, 1)
                pool.memset(slot_a[p][:], 0.0).then_inc(padded, 1)
            pool.wait_ge(q_in, 16)
            pool.wait_ge(padded, 4)

            def place(g, r):
                item = 2 * g + r
                wait(pool, scored, item - 1)
                for m in range(2):
                    rows = slice(m * HD, (m + 1) * HD)
                    to = slot_b[r][rows, :].rearrange("p (h x) -> p h x", x=P)
                    for h in range(BH):
                        pool.tensor_copy(to[:, h, h * ROW + m * DSEQ:h * ROW + (m + 1) * DSEQ],
                                         q[rows, BH + h, bass.ds(item * DSEQ, DSEQ)]).then_inc(q_ready, 1)
                    pool.tensor_copy(slot_a[r][rows, m * HD:(m + 1) * HD].rearrange("p (g t) -> p g t", g=AG),
                                     q[rows, 0:AG, bass.ds(item * DSEQ, DSEQ)]).then_inc(q_ready, 1)

            stages(pool, 0, DEC // 2, 2, [(0, place)])

        @block.tensor
        def _(pe):
            def scores(g, r):
                item = 2 * g + r
                pe.wait_ge(kb_in[r], 32 * (g + 1))
                pe.wait_ge(q_ready, 10 * (item + 1))
                wait(pe, biased, 2 * item)
                for c in range(3):
                    n = 512 if c < 2 else DSEQ
                    for h in range(BH):
                        keys = (kb[r][:, h, c * 512:(c + 1) * 512] if c < 2 else
                                kT[:, h + 1, bass.ds(SEQ + item * DSEQ, DSEQ)])
                        pe.matmul(score[:, c, 0:n], slot_b[r][:, h * P:(h + 1) * P], keys,
                                  start=(h == 0), stop=(h == BH - 1))
                pe.matmul(score_a[:, 0:WIN], slot_a[r][:], ka[r][:], start=True, stop=True)
                pe.matmul(score_a[:, WIN:WIN + DSEQ], slot_a[r][:], kT[:, 0, bass.ds(SEQ + item * DSEQ, DSEQ)],
                          start=True, stop=True).then_inc(scored, 1)

            def turn(g, r):
                item = 2 * g + r
                pe.wait_ge(exp_done, 3 * (item + 1))
                for j in range(3):
                    side = (r + j) % 2
                    wait(pe, (out_act, out_dve, out_act)[j], 2 * item + (0, 0, 1)[j])
                    if j < 2:
                        for i in range(4):
                            last = pe.transpose(blocks[:, side, i * P:(i + 1) * P],
                                                prob_b[r][:, (4 * j + i) * P:(4 * j + i + 1) * P], ident)
                    else:
                        pe.transpose(blocks[:, side, 0:P], prob_a[r][:, 0:P], ident)
                        pe.transpose(blocks[0:DSEQ, side, P:2 * P], prob_b[r][:, PAST:PAST + DSEQ], ident)
                        last = pe.transpose(blocks[0:DSEQ, side, 2 * P:3 * P], prob_a[r][:, WIN:WIN + DSEQ], ident)
                    last.then_inc(block_ready, 1)

            def average(g, r):
                item = 2 * g + r
                pe.wait_ge(vb_in[r], 48 * (g + 1))
                pe.wait_ge(out_act, 2 * (item + 1))
                pe.wait_ge(out_dve, 2 * (item + 1))
                wait(pe, o_done, 5 * item)
                for k in range(PAST // P):
                    pe.matmul(mixed_b[:], turned[r][:, k, :], vb[r][:, k, :], start=(k == 0), stop=False)
                pe.matmul(mixed_b[:], turned[r][0:DSEQ, 9, :], vn[r][:, P:ROWS], start=False, stop=True)
                pe.matmul(mixed_a[:, 0:P], turned[r][:, 8, :], va[r][:], start=True, stop=False)
                pe.matmul(mixed_a[:, 0:P], turned[r][0:DSEQ, 10, :], vn[r][:, 0:P],
                          start=False, stop=True).then_inc(av_done, 1)

            def finish(g, r):
                item = 2 * g + r
                pe.wait_ge(o_done, 5 * (item + 1))
                wait(pe, kept, item)
                wait(pe, stored_a, 2 * item)
                pe.matmul(post[0:HD, 0:P], pick[:], o_b[:], start=True, stop=True)
                pe.transpose(post[:, P:2 * P], o_a[:], ident).then_inc(posted, 1)

            pe.wait_ge(tabs_in, 80)
            stages(pe, 0, DEC // 2, 2, [(0, scores), (2, finish), (1, turn), (1, average)])
            pe.wait_ge(scaled, DEC)
            for b in range(DEC):
                last = pe.transpose(post[:, b * HD:(b + 1) * HD], o_all[:, b, :], ident[0:HD, 0:HD])
            last.then_inc(o_turned, 1)

        @block.vector
        def _(dve):
            lambda_vector(dve)
            dve.wait_ge(tabs_in, 80)
            dve.tensor_scalar(nsink[:], sink[:, AG:AG + 1], -1.0, None, ALU.mult).then_inc(rows_done, 1)
            dve.scalar_tensor_tensor(out=row_coef[:], in0=is_map[:, 1:2], scalar=neg_lam[:, 0:1],
                                     in1=is_map[:, 0:1], op0=ALU.mult, op1=ALU.add).then_inc(rows_done, 1)
            dve.wait_ge(rows_done, 2)

            def bias(g, r):
                item = 2 * g + r
                dve.wait_ge(scored, item + 1)
                wait(dve, block_ready, 3 * item - 3)
                dve.memset(waited[:], 0.0)
                dve.tensor_tensor_reduce(prob_b[r][:], score_b, bias_b[:], 1.0, LOWEST, ALU.add, ALU.max,
                                         top[r][:, 0:1]).then_inc(biased, 1)
                dve.tensor_tensor_reduce(prob_a[r][:], score_a, bias_a[:], 1.0, LOWEST, ALU.add, ALU.max,
                                         top[r][:, 1:2]).then_inc(biased, 1)
                dve.wait_ge(biased, 2 * (item + 1))
                dve.tensor_scalar(nmax[r][:, 0:1], top[r][:, 0:1], -1.0, None, ALU.mult).then_inc(max_ready, 1)
                dve.scalar_tensor_tensor(out=nmax[r][:, 1:2], in0=top[r][:, 1:2], scalar=-1.0, in1=nsink[:],
                                         op0=ALU.mult, op1=ALU.min).then_inc(max_ready, 1)
                dve.wait_ge(max_ready, 2 * (item + 1))
                dve.tensor_tensor(over[r][:], nmax[r][:, 1:2], nsink[:], ALU.subtract).then_inc(over_done, 1)

            def total(g, r):
                item = 2 * g + r
                dve.wait_ge(exp_done, 3 * (item + 1))
                dve.tensor_copy(den[r][:, 0:1], norm[r][:, 0:1]).then_inc(den_done, 1)
                dve.tensor_tensor(den[r][:, 1:2], norm[r][:, 1:2], norm[r][:, 2:3], ALU.add).then_inc(den_done, 1)
                dve.wait_ge(den_done, 2 * (item + 1))
                dve.reciprocal(inv[r][:], den[r][:]).then_inc(inv_done, 1)
                dve.wait_ge(inv_done, item + 1)
                dve.tensor_tensor(coef[r][:], inv[r][:, 0:1], row_coef[:], ALU.mult).then_inc(coef_done, 1)

            def clear(g, r):
                item = 2 * g + r
                side = r % 2
                dve.wait_ge(block_ready, 3 * (item + 1))
                dve.tensor_copy(turned[r][:, 8, :], blocks[:, side, 0:P]).then_inc(out_dve, 1)
                dve.tensor_copy(turned[r][0:DSEQ, 9:11, :],
                                blocks[0:DSEQ, side, P:3 * P].rearrange("p (k c) -> p k c", k=2)).then_inc(out_dve, 1)

            def take(g, r):
                item = 2 * g + r
                dve.wait_ge(av_done, item + 1)
                wait(dve, posted, item)
                dve.wait_ge(coef_done, item + 1)
                for h in range(BH):
                    rows = slice(h * ROW, (h + 1) * ROW)
                    dve.tensor_scalar(o_b[rows, :], mixed_b[rows, h * P:(h + 1) * P], coef[r][rows, 0:1], None,
                                      ALU.mult).then_inc(o_done, 1)
                dve.tensor_scalar(o_a[:], mixed_a[:, 0:P], inv[r][:, 1:2], None, ALU.mult).then_inc(o_done, 1)

            def keep(g, r):
                item = 2 * g + r
                dve.wait_ge(posted, item + 1)
                dve.tensor_copy(o_all[:, item, :], post[0:HD, 0:P]).then_inc(kept, 1)

            stages(dve, 0, DEC // 2, 2, [(0, bias), (2, keep), (1, total), (1, clear), (1, take)])
            dve.wait_ge(o_squared, 1)
            dve.reduce_sum(ssq[:], o_sq[:], axis=AX_X).then_inc(ssq_done, 1)
            dve.wait_ge(ssq_done, 1)
            sub.vector(dve, ssq[:], then=1.0 - LAMBDA_INIT)
            for b in range(DEC):
                dve.tensor_scalar(o_all[:, b, :], o_all[:, b, :], sub.out[:, b:b + 1], None, ALU.mult).then_inc(scaled, 1)

        @block.scalar
        def _(act):
            lambda_scalar(act)

            def exponent(g, r):
                item = 2 * g + r
                act.wait_ge(over_done, item + 1)
                act.activation(prob_b[r][:], prob_b[r][:], ACT.Exp, bias=nmax[r][:, 0:1],
                               accum_out=norm[r][:, 0:1]).then_inc(exp_done, 1)
                act.activation(prob_a[r][:], prob_a[r][:], ACT.Exp, bias=nmax[r][:, 1:2],
                               accum_out=norm[r][:, 1:2]).then_inc(exp_done, 1)
                act.activation(norm[r][:, 2:3], over[r][:], ACT.Exp).then_inc(exp_done, 1)

            def clear(g, r):
                item = 2 * g + r
                for j in range(2):
                    act.wait_ge(block_ready, 3 * item + j + 1)
                    act.activation(turned[r][:, 4 * j:4 * j + 4, :],
                                   blocks[:, (r + j) % 2, :].rearrange("p (k c) -> p k c", k=4),
                                   ACT.Copy).then_inc(out_act, 1)

            def store_a(g, r):
                item = 2 * g + r
                act.wait_ge(posted, item + 1)
                act.wait_ge(kept, item + 1)
                for m in range(2):
                    rows = slice(m * HD, (m + 1) * HD)
                    act.activation(oT[rows, 0:AG, bass.ds(SEQ + item * DSEQ, DSEQ)],
                                   post[rows, P + m * HD:P + (m + 1) * HD].rearrange("p (g t) -> p g t", g=AG),
                                   ACT.Copy).then_inc(stored_a, 1)

            stages(act, 0, DEC // 2, 2, [(0, exponent), (2, store_a), (1, clear)])
            act.wait_ge(kept, DEC)
            act.activation(o_sq[:], o_all[:], ACT.Square).then_inc(o_squared, 1)
            sub.scalar(act)
            act.wait_ge(o_turned, 1)
            act.activation(oT[:, AG:8, SEQ:TOK].rearrange("p h (b t) -> p b h t", b=DEC),
                           post[:].rearrange("p (b h t) -> p b h t", b=DEC, h=BH), ACT.Copy,
                           scale=g_sub).then_inc(stored_a, 1)
            act.wait_ge(stored_a, 2 * DEC + 1)


def merge(nc, xT, pT, w_out, w_gate, w_ple, z_dram, yT, oT, ident, ones, g_post, g_ple):
    G_PLE, G_GATE, G_ALL = 4, 8, 12
    NB = 8
    with ExitStack() as ctx:
        mk = Maker(nc, ctx, "mrg")
        a_hi, a_lo = mk.sb("a_hi", [P, KT, TOK], F32R), mk.sb("a_lo", [P, KT, TOK], F32R)
        mix = mk.sb("mix", [P, KT, TOK])
        x = oT
        p_emb = mk.sb("p_emb", [P, PKT, TOK])
        w_raw = [mk.sb(f"w_raw{s}", [P, KT, P]) for s in range(2)]
        w_hi = [mk.sb(f"w_hi{s}", [P, KT, P], F32R) for s in range(2)]
        w_lo = [mk.sb(f"w_lo{s}", [P, KT, P], F32R) for s in range(2)]
        work = [mk.sb(f"work{s}", [P, TOK]) for s in range(2)]
        total = mk.sb("total", [P, TOK])
        rms = mk.sb("rms", [P, TOK])
        mix_norm = Rsqrt(mk, "mix_norm", P, TT, D, EPS)
        ple_norm = Rsqrt(mk, "ple_norm", P, TT, D, EPS)
        acc = [mk.ps(f"acc{s}", [P, NCH, 512]) for s in range(2)]
        small = mk.ps("small", [P, 2, 512])

        z_in = [mk.sem(f"z_in{s}") for s in range(2)]
        w_in = [mk.sem(f"w_in{s}") for s in range(2)]
        x_in, p_in, y_out = mk.sem("x_in"), mk.sem("p_in"), mk.sem("y_out")
        gated, a_hi_done, a_lo_done = mk.sem("gated"), mk.sem("a_hi_done"), mk.sem("a_lo_done")
        w_hi_done, w_lo_done = mk.sem("w_hi_done"), mk.sem("w_lo_done")
        product, evacuated = mk.sem("product"), mk.sem("evacuated")
        squared, added = mk.sem("squared"), mk.sem("added")
        sums, diag_done, spread, rms_done = mk.sem("sums"), mk.sem("diag"), mk.sem("spread"), mk.sem("rms_done")
        normed, h_done, h_hi_done, h_lo_done = mk.sem("normed"), mk.sem("h_done"), mk.sem("h_hi"), mk.sem("h_lo")
        sigmoid, ple_scaled, ple_gated, y_done = mk.sem("sigmoid"), mk.sem("ple_scaled"), mk.sem("ple_gated"), mk.sem("y_done")

        block = ctx.enter_context(nc.Block())

        @block.sync
        def _(sp):
            def load(source, first, free, ahead):
                def step(g, r):
                    wait(sp, free, 2 * (g - first) + r + ahead)
                    dst = w_raw[r][:] if source is not w_ple else w_raw[r][:, 0:PKT, :]
                    sp.dma_start(dst, source[2 * (g - base[id(source)]) + r]).then_inc(w_in[r], 16)
                return step

            base = {id(w_out): 0, id(w_ple): G_PLE, id(w_gate): G_GATE}
            split_out = load(w_out, 0, w_lo_done, -1)
            for r in range(2):
                sp.dma_start(work[r][:], z_dram[r]).then_inc(z_in[r], 16)
                split_out(0, r)
            sp.dma_start(p_emb[:], pT).then_inc(p_in, 16)
            for k in range(2, KT):
                sp.wait_ge(gated, k - 1)
                sp.dma_start(work[k % 2][:], z_dram[k]).then_inc(z_in[k % 2], 16)
            for r in range(2):
                split_out(1, r)
            for k in range(KT):
                sp.wait_ge(a_lo_done, k + 1)
                sp.dma_start(x[:, k, :], xT[:, k, :]).then_inc(x_in, 16)
            stages(sp, 2, G_PLE, 2, [(0, split_out)], fresh=False)
            stages(sp, G_PLE, G_PLE + 1, 2, [(0, load(w_ple, 0, w_lo_done, -1))], fresh=False)
            stages(sp, G_PLE + 1, G_GATE, 2, [(0, load(w_ple, 0, product, -1))], fresh=False)
            stages(sp, G_GATE, G_GATE + 1, 2, [(0, load(w_gate, 0, product, -1))], fresh=False)

            def store_y(g, r):
                sp.wait_ge(y_done, 2 * (g - G_GATE) + r + 1)
                sp.dma_start(yT[2 * (g - G_GATE) + r], mix[:, 2 * (g - G_GATE) + r, :]).then_inc(y_out, 16)

            for g in range(G_GATE, G_ALL):
                for r in range(2):
                    if g < G_ALL - 1:
                        load(w_gate, NB // 2 + 1, w_lo_done, 1)(g + 1, r)
                    if g > G_GATE:
                        store_y(g - 1, r)
            for r in range(2):
                store_y(G_ALL - 1, r)
            sp.wait_ge(y_out, 16 * NB)

        @block.scalar
        def _(act):
            def high(g, r):
                act.wait_ge(w_in[r], 16 * (g + 1))
                wait(act, product, 2 * g + r - 1)
                act.activation(w_hi[r][:], w_raw[r][:], ACT.Copy).then_inc(w_hi_done, 1)

            def square(first, counted):
                def step(g, r):
                    j = 2 * (g - first) + r
                    act.wait_ge(evacuated, 2 * g + r + 1)
                    wait(act, added, counted + j - 1)
                    act.activation(work[r][:], mix[:, j, :], ACT.Square).then_inc(squared, 1)
                return step

            high(0, 0)
            high(0, 1)
            for k in range(KT):
                act.wait_ge(gated, k + 1)
                act.activation(a_hi[:, k, :], oT[:, k, :], ACT.Copy).then_inc(a_hi_done, 1)
            square_mix = square(0, 0)
            for g in range(1, G_PLE):
                for r in range(2):
                    high(g, r)
                    square_mix(g - 1, r)
            for r in range(2):
                square_mix(G_PLE - 1, r)
            mix_norm.scalar(act)

            def h_high(g, r):
                j = 2 * (g - G_PLE) + r
                act.wait_ge(h_done, j + 1)
                act.activation(a_hi[:, j, :], x[:, j, :], ACT.Copy).then_inc(h_hi_done, 1)

            square_ple = square(G_PLE, NB)
            for g in range(G_PLE, G_GATE):
                for r in range(2):
                    h_high(g, r)
                    square_ple(g, r)
            high(G_GATE, 0)
            high(G_GATE, 1)
            ple_norm.scalar(act)

            def gate(g, r):
                j = 2 * (g - G_GATE) + r
                act.wait_ge(product, 2 * g + r + 1)
                if isinstance(g, int) and g == G_GATE:
                    act.wait_ge(added, 2 * NB)
                else:
                    act.wait_ge(ple_gated, j - 1)
                act.activation(by_runs(work[r][:]), acc[r][:, :, 0:RUN], ACT.Sigmoid).then_inc(sigmoid, 1)

            for g in range(G_GATE, G_ALL):
                for r in range(2):
                    gate(g, r)
                    if g < G_ALL - 1:
                        high(g + 1, r)

        @block.gpsimd
        def _(pool):
            def low(g, r, done):
                pool.wait_ge(w_hi_done, done)
                pool.tensor_tensor(w_lo[r][:], w_raw[r][:], w_hi[r][:].bitcast(F32),
                                   ALU.subtract).then_inc(w_lo_done, 1)

            def add(j, counted):
                pool.wait_ge(squared, counted + j + 1)
                if j == 0:
                    if counted:
                        pool.wait_ge(spread, NCH)
                    pool.tensor_copy(total[:], work[0][:]).then_inc(added, 1)
                else:
                    pool.wait_ge(added, counted + j)
                    pool.tensor_tensor(total[:], total[:], work[j % 2][:], ALU.add).then_inc(added, 1)

            low(0, 0, 1)
            low(0, 1, 2)
            for g in range(1, G_PLE):
                for r in range(2):
                    low(g, r, 2 * g + r + 1)
                    add(2 * (g - 1) + r, 0)
            for r in range(2):
                add(2 * (G_PLE - 1) + r, 0)
            for j in range(NB):
                add(j, NB)
            for g in range(G_GATE, G_ALL):
                for r in range(2):
                    low(g, r, NB + 2 * (g - G_GATE) + r + 1)

        @block.tensor
        def _(pe):
            def free_banks(g, r):
                if g > G_GATE:
                    pe.wait_ge(sigmoid, 2 * (g - G_GATE) + r - 1)
                else:
                    wait(pe, evacuated, 2 * g + r - 1)

            def multiply(g, r, split, done, part):
                pe.wait_ge(w_lo_done, split)
                free_banks(g, r)
                for k in range(KT):
                    if done is not None:
                        for s in done:
                            pe.wait_ge(s, k + 1)
                    for n in range(NCH):
                        last = three_passes(pe, acc[r][:, n, 0:RUN], w_hi[r][:, k, :], w_lo[r][:, k, :],
                                            run(a_hi[:, k, :], n), run(a_lo[:, k, :], n),
                                            start=(k == 0), stop=(k == KT - 1))
                last.then_inc(product, 1)

            def embed(g, r):
                pe.wait_ge(w_in[r], 16 * (g + 1))
                free_banks(g, r)
                for k in range(PKT):
                    for n in range(NCH):
                        last = pe.matmul(acc[r][:, n, 0:RUN], w_raw[r][:, k, :], run(p_emb[:, k, :], n),
                                         start=(k == 0), stop=(k == PKT - 1))
                last.then_inc(product, 1)

            def statistics(which):
                pe.wait_ge(added, NB * (which + 1))
                for t in range(TT):
                    last = pe.matmul(small[:, 0, t:t + 1], total[:, t * P:(t + 1) * P], ones[:, 0:1],
                                     start=True, stop=True)
                last.then_inc(sums, 1)

            def to_all(which):
                pe.wait_ge(diag_done, TT * (which + 1))
                for n in range(NCH):
                    if n == 2:
                        pe.wait_ge(rms_done, NCH * which + 1)
                    pe.matmul(small[:, n % 2, 0:RUN], ones, run(total[:], n), start=True, stop=True).then_inc(spread, 1)

            for g in range(G_PLE):
                for r in range(2):
                    multiply(g, r, 2 * g + r + 1, (a_hi_done, a_lo_done) if g == r == 0 else None, 0)
            pe.wait_ge(p_in, 16)
            embed(G_PLE, 0)
            embed(G_PLE, 1)
            statistics(0)
            to_all(0)
            for g in range(G_PLE + 1, G_GATE):
                for r in range(2):
                    embed(g, r)
            statistics(1)
            to_all(1)
            for g in range(G_GATE, G_ALL):
                for r in range(2):
                    multiply(g, r, NB + 2 * (g - G_GATE) + r + 1,
                             (h_hi_done, h_lo_done) if g == G_GATE and r == 0 else None, 1)

        @block.vector
        def _(dve):
            for k in range(KT):
                dve.wait_ge(z_in[k % 2], 16 * (k // 2 + 1))
                dve.tensor_tensor(oT[:, k, :], oT[:, k, :], work[k % 2][:], ALU.mult).then_inc(gated, 1)
                if k >= 1:
                    dve.wait_ge(a_hi_done, k)
                    dve.tensor_tensor(a_lo[:, k - 1, :], oT[:, k - 1, :], a_hi[:, k - 1, :].bitcast(F32),
                                      ALU.subtract).then_inc(a_lo_done, 1)
            dve.wait_ge(a_hi_done, KT)
            dve.tensor_tensor(a_lo[:, KT - 1, :], oT[:, KT - 1, :], a_hi[:, KT - 1, :].bitcast(F32),
                              ALU.subtract).then_inc(a_lo_done, 1)

            def out_mix(g, r):
                dve.wait_ge(product, 2 * g + r + 1)
                dve.tensor_copy(by_runs(mix[:, 2 * g + r, :]), acc[r][:, :, 0:RUN]).then_inc(evacuated, 1)

            def spread_norm(norm, which):
                dve.wait_ge(sums, which + 1)
                norm.vector(dve, small[:, 0, 0:TT])
                for t in range(TT):
                    dve.tensor_scalar(total[:, t * P:(t + 1) * P], ident, norm.out[:, t:t + 1], None,
                                      ALU.mult).then_inc(diag_done, 1)
                for n in range(NCH):
                    dve.wait_ge(spread, NCH * which + n + 1)
                    dve.tensor_copy(run(rms[:], n), small[:, n % 2, 0:RUN]).then_inc(rms_done, 1)
                dve.wait_ge(rms_done, NCH * (which + 1))

            def make_h(j):
                dve.scalar_tensor_tensor(out=mix[:, j, :], in0=mix[:, j, :], scalar=g_post[:, j:j + 1],
                                         in1=rms[:], op0=ALU.mult, op1=ALU.mult).then_inc(normed, 1)
                dve.wait_ge(normed, j + 1)
                dve.tensor_tensor(x[:, j, :], x[:, j, :], mix[:, j, :], ALU.add).then_inc(h_done, 1)

            def h_low(j):
                dve.wait_ge(h_hi_done, j + 1)
                dve.tensor_tensor(a_lo[:, j, :], x[:, j, :], a_hi[:, j, :].bitcast(F32),
                                  ALU.subtract).then_inc(h_lo_done, 1)

            for g in range(G_PLE):
                for r in range(2):
                    out_mix(g, r)
            spread_norm(mix_norm, 0)
            dve.wait_ge(x_in, 16 * KT)
            for j in range(NB):
                make_h(j)
                dve.wait_ge(product, 2 * G_PLE + j + 1)
                dve.wait_ge(h_done, j + 1)
                dve.tensor_copy(by_runs(mix[:, j, :]), acc[j % 2][:, :, 0:RUN]).then_inc(evacuated, 1)
                h_low(j)
            spread_norm(ple_norm, 1)

            def finish(j):
                dve.scalar_tensor_tensor(out=mix[:, j, :], in0=mix[:, j, :], scalar=g_ple[:, j:j + 1],
                                         in1=rms[:], op0=ALU.mult, op1=ALU.mult).then_inc(ple_scaled, 1)
                dve.wait_ge(ple_scaled, j + 1)
                dve.wait_ge(sigmoid, j + 1)
                dve.tensor_tensor(mix[:, j, :], mix[:, j, :], work[j % 2][:], ALU.mult).then_inc(ple_gated, 1)
                dve.wait_ge(ple_gated, j + 1)
                dve.tensor_tensor(mix[:, j, :], mix[:, j, :], x[:, j, :], ALU.add).then_inc(y_done, 1)

            for j in range(NB):
                finish(j)



def _slopes(n):
    return 2.0 ** (-8.0 * np.arange(1, n + 1) / n)


def _tables():
    row = np.arange(P)
    eye = np.eye(P)
    dist = np.abs(row[:, None] + SEQ - P - np.arange(SEQ)[None, :])
    strip = -_slopes(BH)[0] * dist
    strip[:CHUNK, SEQ - CHUNK:] = MASKED * 64
    rel = np.abs((row % CHUNK)[:, None] + WIN - np.arange(BAND)[None, :])
    slope_a = _slopes(2 * AG).reshape(2, AG)
    band = np.stack([-slope_a[row // CHUNK, g][:, None] * rel for g in range(AG)], 1)
    query = row % DSEQ
    sample_b = -_slopes(BH)[row // (2 * DSEQ)][:, None] * np.abs(query[:, None] + PAST - np.arange(PAST + DSEQ)[None, :])
    sample_a = -slope_a.reshape(-1)[row // DSEQ][:, None] * np.abs(query[:, None] + WIN - np.arange(WIN + DSEQ)[None, :])
    pick = (np.arange(HD)[None, :] == (row // (2 * DSEQ) * DSEQ + query)[:, None])
    second = (row // DSEQ) % 2
    made = dict(consts=np.concatenate([eye, np.ones((P, P))], 1), strip=strip, band=band,
                sample_b=sample_b, sample_a=sample_a, pick=pick, is_map=np.stack([1 - second, second], 1))
    return {k: np.ascontiguousarray(v, dtype=np.float32) for k, v in made.items()}


def _blocks(w, columns):
    picked = w[:, columns]
    k = w.shape[0] // P
    return picked.reshape(k, P, -1, P).transpose(2, 1, 0, 3)


def _feature_major(a):
    return a.reshape(TOK, -1, P).transpose(2, 1, 0)


def kernel(**inputs):
    import concourse.bacc as _bacc
    from concourse.bass_utils import run_bass_kernel_spmd as _run

    f = {k: np.asarray(v) for k, v in inputs.items()}
    window = np.concatenate([np.concatenate([m * 4 * HD + g * HD + np.arange(HD) for m in range(2)])
                             for g in range(AG)])
    a_q, a_k, a_v, a_z, b_q, b_k, b_v, b_z = np.cumsum([0, 512, 128, 128, 512, 512, 512, 512])
    ks = [a_k + np.arange(P)] + [b_k + h * P + np.arange(P) for h in range(BH)]
    vs = [a_v + np.arange(P)] + [b_v + h * P + np.arange(P) for h in range(BH)]
    order = np.concatenate([a_q + window, b_q + np.arange(512)] + [c for kv in zip(ks, vs) for c in kv]
                           + [a_z + window, b_z + np.arange(512)])
    x_all = np.concatenate([f["x_prompt"].reshape(SEQ, D), f["x_sample"].reshape(-1, D)])
    p_all = np.concatenate([f["p_prompt"].reshape(SEQ, PLE), f["p_sample"].reshape(-1, PLE)])
    gains = np.concatenate([f[k][0].reshape(KT, P).T for k in ("pre_norm_g", "post_norm_g", "ple_norm_g")]
                           + [f["b_subln_g"][0][:, None]], 1)
    sink = f["a_sinks"][0]
    sinks = np.concatenate([np.repeat(sink.reshape(2, AG), CHUNK, 0), np.repeat(sink, DSEQ)[:, None]], 1)
    lam = np.stack([f["b_lambda_" + k][0] for k in ("q1", "k1", "q2", "k2")])
    arrays = dict(
        xT=_feature_major(x_all), pT=_feature_major(p_all),
        w_in=_blocks(f["w_in"][0], order),
        w_out=_blocks(f["w_out"][0][np.concatenate([window, 512 + np.arange(512)])], np.arange(D)),
        w_gate=_blocks(f["w_gate"][0], np.arange(D)), w_ple=_blocks(f["w_ple"][0], np.arange(D)),
        gains=gains, lam_in=np.broadcast_to(lam, (P, 4, HD)), sinks=sinks,
        kb_cache=f["cache_b_k"][0].transpose(0, 3, 2, 1),
        vb_cache=f["cache_b_v"][0].reshape(DEC, PAST // P, P, BH * P).transpose(0, 2, 1, 3),
        ka_cache=f["cache_a_k"][0].reshape(DEC, WIN, P).transpose(0, 2, 1),
        va_cache=f["cache_a_v"][0].reshape(DEC, WIN, P),
    )
    arrays = {k: np.ascontiguousarray(v) for k, v in arrays.items()}
    tables = _tables()
    nc = _bacc.Bacc("TRN2", target_bir_lowering=False, num_devices=1)

    def dram(name, shape, kind):
        return nc.dram_tensor(name, list(shape), F32, kind=kind).ap()

    args = {k: dram(k, v.shape, "ExternalInput") for k, v in arrays.items()}
    table_args = {k: dram("table_" + k, v.shape, "ExternalInput") for k, v in tables.items()}
    outs = {"yT": (KT, P, TOK), "kT_out": (5, P, TOK), "vT_out": (5, P, TOK),
            "rolled_k": (DEC, P, WIN - DSEQ), "rolled_v": (DEC, WIN - DSEQ, P)}
    args.update({k: dram(k, s, "ExternalOutput") for k, s in outs.items()})
    encoder_step(nc, tables=table_args, **args)
    arrays.update({"table_" + k: v for k, v in tables.items()})
    r = _run(nc, [arrays], core_ids=[0]).results[0]

    y = r["yT"].reshape(D, TOK).T
    k_all, v_all = (r[n].reshape(ROWS, TOK).T for n in ("kT_out", "vT_out"))
    new_a, new_b = [], []
    for a in (k_all, v_all):
        new_a.append((a[SEQ - WIN:SEQ, 0:P].reshape(1, 1, WIN, 2, HD), a[SEQ:, 0:P].reshape(1, DEC, DSEQ, 2, HD)))
        new_b.append((a[:SEQ, P:].reshape(1, 1, SEQ, BH, P), a[SEQ:, P:].reshape(1, DEC, DSEQ, BH, P)))
    kept = (r["rolled_k"].transpose(0, 2, 1), r["rolled_v"])
    rolled = [np.concatenate([kept[i].reshape(1, DEC, WIN - DSEQ, 2, HD), new_a[i][1]], 2) for i in range(2)]
    return tuple(np.ascontiguousarray(a) for a in (
        y[:SEQ].reshape(1, SEQ, D), y[SEQ:].reshape(DEC, DSEQ, D),
        new_a[0][0], new_a[1][0], new_b[0][0], new_b[1][0], rolled[0], rolled[1], new_b[0][1], new_b[1][1]))
```

```python
from contextlib import ExitStack

import numpy as np
import concourse.bass as bass
from concourse import mybir

F32 = mybir.dt.float32
F32R = mybir.dt.float32r
ALU = mybir.AluOpType
ACT = mybir.ActivationFunctionType
AX_X = mybir.AxisListType.X

P = 128
D = 1024
KT = D // P
SEQ = 1024
NT = SEQ // P
DEC = 8
DSEQ = 16
TOK = SEQ + DEC * DSEQ
TT = TOK // P
NCH = 3
RUN = TOK // NCH
PAST = 1024
CHUNK = 64
NCHUNK = SEQ // CHUNK
BAND = 3 * CHUNK
WIN = 2 * CHUNK
HD = 64
AG = 4
BH = 4
PLE = 256
PKT = PLE // P
ROWS = 5 * P
LAMBDA_INIT = 0.2
EPS = 1e-6
SUB_EPS = 1e-5
MASKED = -1e30
LOWEST = -3e38
SCALE = HD ** -0.5

NZ = 8
NKV = 5
NQ = 8
NB_IN = NZ + 2 * NKV + NQ
G_KV = NZ // 2
G_Q = G_KV + NKV
G_IN = NB_IN // 2


def wait(eng, sem, value):
    if not isinstance(value, int) or value > 0:
        eng.wait_ge(sem, value)


def pipeline(eng, lags, pieces, period):
    most, end = max(lags), pieces[-1][0]

    def tick(group, newest, piece=None):
        for i, lag in enumerate(lags):
            at = newest - lag
            g = group + at // period
            if isinstance(g, int):
                steps = next((s for last, s in pieces if g < last), None) if g >= 0 else None
            else:
                steps = piece
            if steps and steps[i]:
                steps[i](g, at % period)

    first = 0
    for last, steps in pieces:
        start = min(first - (-(most + 2) // period), last)
        if last - start == 1:
            start = last
        for g in range(first, start):
            for r in range(period):
                tick(g, r)
        if start < last:
            with eng.Fori(start, last) as g:
                for r in range(period):
                    tick(g, r, steps)
        first = last
    for extra in range(most):
        tick(end, extra)


def stages(eng, last, period, steps):
    pipeline(eng, [lag for lag, _ in steps], [(last, [step for _, step in steps])], period)


def encoder_step(nc, xT, pT, w_in, w_out, w_gate, w_ple, gains, lam_in, sinks, tables,
                 kb_cache, vb_cache, ka_cache, va_cache, yT, kT_out, vT_out, rolled_k, rolled_v):
    z_dram = nc.dram_tensor("z_scratch", [NZ, P, TOK], F32, kind="Internal").ap()
    vnew_dram = nc.dram_tensor("v_new_scratch", [DEC * DSEQ, ROWS], F32, kind="Internal").ap()

    with ExitStack() as whole:
        qo = whole.enter_context(nc.sbuf_tensor("qo", [P, 8, TOK], F32))
        consts = whole.enter_context(nc.sbuf_tensor("consts", [P, 2 * P], F32))
        ident = consts[:, 0:P]
        ones = consts[:, P:2 * P]
        gain = whole.enter_context(nc.sbuf_tensor("gain", [P, gains.shape[1]], F32))
        g_pre, g_post, g_ple, g_sub = gain[:, 0:8], gain[:, 8:16], gain[:, 16:24], gain[:, 24:25]
        with ExitStack() as attention:
            kT = attention.enter_context(nc.sbuf_tensor("kT", [P, 5, TOK], F32))
            v_tok = attention.enter_context(nc.sbuf_tensor("v_tok", [P, TT, ROWS], F32))
            project(nc, xT, w_in, gains, tables, z_dram, vnew_dram, kT_out, vT_out,
                    ka_cache, va_cache, rolled_k, rolled_v, qo, kT, v_tok, consts, gain)
            ahead = Ahead(nc, attention, lam_in, sinks, tables, kb_cache, vb_cache, ka_cache, va_cache, vnew_dram)
            with ExitStack() as prompt:
                diff_o = prompt.enter_context(nc.sbuf_tensor("diff_o", [P, BH * NT, P], F32))
                diff_prompt(nc, ahead, diff_o, qo, kT, v_tok, ident)
                window_prompt(nc, ahead, diff_o, qo, kT, v_tok, ident, g_sub)
            sample(nc, ahead, z_dram, qo, kT, ident)
        merge(nc, xT, pT, w_out, w_gate, w_ple, z_dram, yT, qo, ident, ones, g_sub, g_post, g_ple)


class Maker:

    def __init__(self, nc, ctx, phase):
        self.nc, self.ctx, self.phase = nc, ctx, phase

    def sb(self, name, shape, dtype=F32):
        return self.ctx.enter_context(self.nc.sbuf_tensor(f"{self.phase}_{name}", shape, dtype))

    def ps(self, name, shape):
        return self.ctx.enter_context(self.nc.psum_tensor(f"{self.phase}_{name}", shape, F32))

    def sem(self, name):
        return self.ctx.enter_context(self.nc.semaphore(f"{self.phase}_{name}"))


class Rsqrt:

    STEPS = 5

    def __init__(self, mk, name, rows, cols, width, eps, places=None):
        if places is None:
            places = [mk.sb(f"{name}_{what}", [rows, cols])[:] for what in ("mean", "root", "guess", "rstd")]
        self.v, self.s, self.y, self.out = places
        self.by_dve = mk.sem(name + "_dve")
        self.by_act = mk.sem(name + "_act")
        self.width, self.eps = width, eps

    def mean(self, dve, total):
        dve.tensor_scalar(self.v, total, 1.0 / self.width, self.eps, ALU.mult, ALU.add).then_inc(self.by_dve, 1)

    def scalar(self, act, before=0):
        act.wait_ge(self.by_dve, self.STEPS * before + 1)
        act.activation(self.s, self.v, ACT.Sqrt).then_inc(self.by_act, 1)

    def invert(self, dve, before=0):
        done = self.STEPS * before
        dve.wait_ge(self.by_act, before + 1)
        dve.reciprocal(self.y, self.s).then_inc(self.by_dve, 1)
        dve.wait_ge(self.by_dve, done + 2)
        dve.scalar_tensor_tensor(out=self.s, in0=self.y, scalar=-0.5, in1=self.y,
                                 op0=ALU.mult, op1=ALU.mult).then_inc(self.by_dve, 1)
        dve.wait_ge(self.by_dve, done + 3)
        dve.tensor_tensor(self.v, self.s, self.v, ALU.mult).then_inc(self.by_dve, 1)
        dve.wait_ge(self.by_dve, done + 4)
        dve.scalar_tensor_tensor(out=self.out, in0=self.v, scalar=1.5, in1=self.y,
                                 op0=ALU.add, op1=ALU.mult).then_inc(self.by_dve, 1)
        dve.wait_ge(self.by_dve, done + 5)

    def vector(self, dve, total, before=0):
        self.mean(dve, total)
        self.invert(dve, before)


def three_passes(pe, out, w_hi, w_lo, x_hi, x_lo, start, stop):
    pe.matmul(out, w_hi, x_hi, start=start, stop=False)
    pe.matmul(out, w_hi, x_lo, start=False, stop=False)
    return pe.matmul(out, w_lo, x_hi, start=False, stop=stop)


def run(x, n):
    return x[:, n * RUN:(n + 1) * RUN]


def by_runs(x):
    return x.rearrange("p (n c) -> p n c", n=NCH)


def project(nc, xT, w_in, gains, tables, z_dram, vnew_dram, kT_out, vT_out,
            ka_cache, va_cache, rolled_k, rolled_v, qo, kT, v_tok, consts, gain):
    ident, ones, g_pre = consts[:, 0:P], consts[:, P:2 * P], gain[:, 0:8]
    with ExitStack() as ctx:
        mk = Maker(nc, ctx, "in")
        x_hi, x_lo = mk.sb("x_hi", [P, KT, TOK], F32R), mk.sb("x_lo", [P, KT, TOK], F32R)
        w_raw = [mk.sb(f"w_raw{s}", [P, KT, P]) for s in range(2)]
        w_hi = [mk.sb(f"w_hi{s}", [P, KT, P], F32R) for s in range(2)]
        w_lo = [mk.sb(f"w_lo{s}", [P, KT, P], F32R) for s in range(2)]
        squares = [mk.sb(f"squares{s}", [P, TOK]) for s in range(2)]
        rms = mk.sb("rms", [P, TOK])
        tmp = [mk.sb(f"tmp{s}", [P, TOK]) for s in range(2)]
        total = tmp[1]
        half = rms
        diag = total
        norm = Rsqrt(mk, "norm", P, TT, D, EPS)
        x_raw = qo
        acc = [mk.ps(f"acc{s}", [P, NCH, 512]) for s in range(2)]
        small = mk.ps("small", [P, 2, 512])

        consts_in, gain_in = mk.sem("consts_in"), mk.sem("gain_in")
        x_in = [mk.sem(f"x_in{k}") for k in range(KT)]
        w_in_sem = [mk.sem(f"w_in{s}") for s in range(2)]
        stored = [mk.sem(f"stored{s}") for s in range(2)]
        vnew_stored, rolled = mk.sem("vnew_stored"), mk.sem("rolled")
        x_hi_done, x_lo_done = mk.sem("x_hi_done"), mk.sem("x_lo_done")
        squared, added, half_steps = mk.sem("squared"), mk.sem("added"), mk.sem("half_steps")
        w_hi_done, w_lo_done = mk.sem("w_hi_done"), mk.sem("w_lo_done")
        product = mk.sem("product")
        evacuated = mk.sem("evacuated")
        sums, diag_done, spread, rms_done = mk.sem("sums"), mk.sem("diag"), mk.sem("spread"), mk.sem("rms_done")
        v_turned, v_copied = mk.sem("v_turned"), mk.sem("v_copied")
        sigmoid, silu = mk.sem("sigmoid"), mk.sem("silu")

        def acc_runs(r):
            return acc[r][:, :, 0:RUN]

        block = ctx.enter_context(nc.Block())

        @block.sync
        def _(sp):
            def load(g, r):
                wait(sp, w_lo_done, 2 * g + r - 1)
                sp.dma_start(w_raw[r][:], w_in[2 * g + r]).then_inc(w_in_sem[r], 16)
                if isinstance(g, int) and g == 0:
                    if r == 0:
                        sp.dma_start(gain[:], gains).then_inc(gain_in, 16)
                    for k in range(5 * r, 5 + 3 * r):
                        sp.dma_start(x_raw[:, k, :], xT[:, k, :]).then_inc(x_in[k], 16)
                    if r == 0:
                        sp.dma_start(consts[:], tables["consts"]).then_inc(consts_in, 16)

            stages(sp, G_IN, 2, [(0, load)])
            sp.dma_start(rolled_k, ka_cache[:, :, DSEQ:WIN]).then_inc(rolled, 16)
            sp.dma_start(rolled_v, va_cache[:, DSEQ:WIN, :]).then_inc(rolled, 16)
            sp.wait_ge(v_copied, NKV * 3)
            sp.dma_start(vnew_dram, v_tok[:, TT - 1, :]).then_inc(vnew_stored, 16)
            for s in stored:
                sp.wait_ge(s, 16 * G_Q)
            sp.wait_ge(vnew_stored, 16)
            sp.wait_ge(rolled, 32)

        @block.scalar
        def _(act):
            def high(g, r):
                act.wait_ge(w_in_sem[r], 16 * (g + 1))
                wait(act, product, 2 * g + r - 1)
                act.activation(w_hi[r][:], w_raw[r][:], ACT.Copy).then_inc(w_hi_done, 1)

            def first_high(g, r):
                if g > 0:
                    return high(g, r)
                if r == 0:
                    high(0, 0)
                for k in range(5 * r, 5 + 3 * r):
                    act.wait_ge(x_in[k], 16)
                    if k == 0:
                        act.wait_ge(gain_in, 16)
                    act.activation(x_hi[:, k, :], x_raw[:, k, :], ACT.Copy,
                                   scale=g_pre[:, k:k + 1]).then_inc(x_hi_done, 1)
                if r == 1:
                    high(0, 1)
                    for k in range(KT // 2, KT):
                        if k >= KT // 2 + 2:
                            act.wait_ge(added, max(2, k - KT // 2 - 1))
                        act.activation(squares[k % 2][:], x_raw[:, k, :], ACT.Square).then_inc(squared, 1)
                    norm.scalar(act)

            def copy_v(g, r):
                if r == 0:
                    return
                for j, (t0, n) in enumerate(((0, 4), (4, 4), (8, 1))):
                    act.wait_ge(v_turned, 3 * (g - G_KV) + j + 1)
                    act.activation(v_tok[:, t0:t0 + n, bass.ds((g - G_KV) * P, P)],
                                   small[:, j % 2, 0:n * P].rearrange("p (t c) -> p t c", t=n),
                                   ACT.Copy).then_inc(v_copied, 1)

            def store_kv(g, r):
                act.wait_ge(evacuated, 2 * g + r + 1)
                if r == 0:
                    act.dma_start(kT_out[g - G_KV], kT[:, g - G_KV, :]).then_inc(stored[0], 16)
                else:
                    act.dma_start(vT_out[g - G_KV], tmp[1][:]).then_inc(stored[1], 16)

            def gate(g, r):
                act.wait_ge(evacuated, 2 * g + r + 1)
                wait(act, stored[r], 16 * g)
                act.activation(squares[r][:], tmp[r][:], ACT.Sigmoid).then_inc(sigmoid, 1)

            def store_z(g, r):
                act.wait_ge(silu, 2 * g + r + 1)
                act.dma_start(z_dram[2 * g + r], squares[r][:]).then_inc(stored[r], 16)

            pipeline(act, (0, 2, 2), [(G_KV, (first_high, gate, store_z)), (G_Q, (high, copy_v, store_kv)),
                                      (G_IN, (high, None, None))], 2)

        @block.gpsimd
        def _(pool):
            for k in range(KT // 2):
                pool.wait_ge(x_in[k], 16)
                to = half if k == 0 else tmp[0]
                pool.tensor_tensor(to[:], x_raw[:, k, :], x_raw[:, k, :], ALU.mult).then_inc(half_steps, 1)
                if k >= 1:
                    pool.wait_ge(half_steps, 2 * k)
                    pool.tensor_tensor(half[:], half[:], tmp[0][:], ALU.add).then_inc(half_steps, 1)
                    pool.wait_ge(half_steps, 2 * k + 1)

            def low(g, r):
                if isinstance(g, int) and g == r == 0:
                    return
                if isinstance(g, int) and 2 * g + r == 1:
                    pool.wait_ge(w_lo_done, 1)
                pool.wait_ge(w_hi_done, 2 * g + r + 1)
                wait(pool, product, 2 * g + r - 1)
                pool.tensor_tensor(w_lo[r][:], w_raw[r][:], w_hi[r][:].bitcast(F32),
                                   ALU.subtract).then_inc(w_lo_done, 1)

            def swish(g, r):
                pool.wait_ge(sigmoid, 2 * g + r + 1)
                pool.tensor_tensor(squares[r][:], tmp[r][:], squares[r][:], ALU.mult).then_inc(silu, 1)

            pipeline(pool, (0, 2), [(G_KV, (low, swish)), (G_IN, (low, None))], 2)

        @block.tensor
        def _(pe):
            def multiply(g, r):
                pe.wait_ge(w_lo_done, 2 * g + r + 1)
                wait(pe, evacuated, 2 * g + r - 1)
                for k in range(KT):
                    if isinstance(g, int) and g == 0:
                        if r == 0:
                            pe.wait_ge(x_hi_done, k + 1)
                            pe.wait_ge(x_lo_done, k + 1)
                        elif k == 4:
                            pe.wait_ge(added, KT // 2 + 1)
                            pe.wait_ge(consts_in, 16)
                            for t in range(TT):
                                last = pe.matmul(small[:, 0, t:t + 1], total[:, t * P:(t + 1) * P], ones[:, 0:1],
                                                 start=True, stop=True)
                            last.then_inc(sums, 1)
                        elif k == KT - 1:
                            for n in range(NCH):
                                pe.wait_ge(diag_done, TT // NCH * (n + 1))
                                if n == 2:
                                    pe.wait_ge(rms_done, 1)
                                pe.matmul(small[:, n % 2, 0:RUN], ones, run(diag[:], n),
                                          start=True, stop=True).then_inc(spread, 1)
                    for n in range(NCH):
                        last = three_passes(pe, acc[r][:, n, 0:RUN], w_hi[r][:, k, :], w_lo[r][:, k, :],
                                            run(x_hi[:, k, :], n), run(x_lo[:, k, :], n),
                                            start=(k == 0), stop=(k == KT - 1))
                last.then_inc(product, 1)

            def turn_v(g, r):
                if r == 0:
                    return
                pe.wait_ge(evacuated, 2 * g + 2)
                for j, (t0, n) in enumerate(((0, 4), (4, 4), (8, 1))):
                    wait(pe, v_copied, 3 * (g - G_KV) + (0, -1, 1)[j])
                    for t in range(n):
                        last = pe.transpose(small[:, j % 2, t * P:(t + 1) * P],
                                            tmp[1][:, (t0 + t) * P:(t0 + t + 1) * P], ident)
                    last.then_inc(v_turned, 1)

            pipeline(pe, (0, 1), [(G_KV, (multiply, None)), (G_Q, (multiply, turn_v)), (G_IN, (multiply, None))], 2)

        @block.vector
        def _(dve):
            dve.wait_ge(w_hi_done, 1)
            dve.tensor_tensor(w_lo[0][:], w_raw[0][:], w_hi[0][:].bitcast(F32), ALU.subtract).then_inc(w_lo_done, 1)
            for k in range(KT):
                dve.wait_ge(x_hi_done, k + 1)
                dve.scalar_tensor_tensor(out=x_lo[:, k, :], in0=x_raw[:, k, :], scalar=g_pre[:, k:k + 1],
                                         in1=x_hi[:, k, :].bitcast(F32), op0=ALU.mult,
                                         op1=ALU.subtract).then_inc(x_lo_done, 1)
            dve.wait_ge(squared, 2)
            dve.tensor_tensor(total[:], squares[0][:], squares[1][:], ALU.add).then_inc(added, 2)
            for k in range(2, KT // 2):
                dve.wait_ge(squared, k + 1)
                dve.wait_ge(added, k)
                dve.tensor_tensor(total[:], total[:], squares[k % 2][:], ALU.add).then_inc(added, 1)
            dve.wait_ge(added, KT // 2)
            dve.wait_ge(half_steps, KT - 1)
            dve.tensor_tensor(total[:], total[:], half[:], ALU.add).then_inc(added, 1)
            dve.wait_ge(sums, 1)
            norm.vector(dve, small[:, 0, 0:TT])
            for t in range(TT):
                dve.tensor_scalar(diag[:, t * P:(t + 1) * P], ident, norm.out[:, t:t + 1], None,
                                  ALU.mult).then_inc(diag_done, 1)
            for n in range(NCH):
                dve.wait_ge(spread, n + 1)
                dve.tensor_copy(run(rms[:], n), small[:, n % 2, 0:RUN]).then_inc(rms_done, 1)
            dve.wait_ge(rms_done, NCH)

            def out_z(g, r):
                dve.wait_ge(product, 2 * g + r + 1)
                wait(dve, silu, 2 * g + r - 1)
                dve.tensor_tensor(by_runs(tmp[r][:]), acc_runs(r), by_runs(rms[:]), ALU.mult).then_inc(evacuated, 1)

            def out_kv(g, r):
                dve.wait_ge(product, 2 * g + r + 1)
                if r == 0:
                    to = kT[:, g - G_KV, :]
                else:
                    if isinstance(g, int) and g == G_KV:
                        dve.wait_ge(silu, NZ)
                    else:
                        dve.wait_ge(v_turned, 3 * (g - G_KV))
                        dve.wait_ge(stored[1], 16 * g)
                    to = tmp[1][:]
                dve.tensor_tensor(by_runs(to), acc_runs(r), by_runs(rms[:]), ALU.mult).then_inc(evacuated, 1)

            def out_q(g, r):
                dve.wait_ge(product, 2 * g + r + 1)
                dve.scalar_tensor_tensor(out=by_runs(qo[:, 2 * (g - G_Q) + r, :]), in0=acc_runs(r), scalar=SCALE,
                                         in1=by_runs(rms[:]), op0=ALU.mult, op1=ALU.mult).then_inc(evacuated, 1)

            pipeline(dve, (0,), [(G_KV, (out_z,)), (G_Q, (out_kv,)), (G_IN, (out_q,))], 2)
            dve.wait_ge(evacuated, NB_IN)


class Ahead:

    def __init__(self, nc, ctx, lam_in, sinks, tables, kb_cache, vb_cache, ka_cache, va_cache, vnew_dram):
        mk = Maker(nc, ctx, "ahead")
        self.strip = mk.sb("strip", [P, SEQ])
        self.band = mk.sb("band", [P, AG, BAND])
        self.sink = mk.sb("sink", [P, AG + 1])
        self.bias_b, self.bias_a = mk.sb("bias_b", [P, PAST + DSEQ]), mk.sb("bias_a", [P, WIN + DSEQ])
        self.pick = mk.sb("pick", [P, P])
        self.is_map = mk.sb("is_map", [P, 2])
        self.ka = [mk.sb(f"ka{p}", [P, WIN]) for p in range(2)]
        self.va = [mk.sb(f"va{p}", [P, P]) for p in range(2)]
        self.vn = [mk.sb(f"vn{p}", [DSEQ, ROWS]) for p in range(2)]
        self.kb, self.vb = [mk.sb("kb0", [P, BH, PAST])], [mk.sb("vb0", [P, PAST // P, BH * P])]
        self.neg_lam, self.load_lambda, self.lambda_vector, self.lambda_scalar = neg_lambda(mk, lam_in)
        self.strip_in, self.band_in, self.sample_in = mk.sem("strip_in"), mk.sem("band_in"), mk.sem("sample_in")
        self.kb_in = [mk.sem(f"kb_in{p}") for p in range(2)]
        self.vb_in = [mk.sem(f"vb_in{p}") for p in range(2)]
        self.tables, self.sinks = tables, sinks
        self.caches = kb_cache, ka_cache, vb_cache, va_cache, vnew_dram

    def load_tables(self, sp):
        self.load_lambda(sp)
        sp.dma_start(self.strip[:], self.tables["strip"]).then_inc(self.strip_in, 16)
        for dst, src in ((self.band, self.tables["band"]), (self.sink, self.sinks)):
            sp.dma_start(dst[:], src).then_inc(self.band_in, 16)
        for dst, name in ((self.bias_b, "sample_b"), (self.bias_a, "sample_a"), (self.pick, "pick"),
                          (self.is_map, "is_map")):
            sp.dma_start(dst[:], self.tables[name]).then_inc(self.sample_in, 16)

    def load_keys(self, sp, item, r):
        sp.dma_start(self.kb[r][:], self.caches[0][item]).then_inc(self.kb_in[r], 16)
        sp.dma_start(self.ka[r][:], self.caches[1][item]).then_inc(self.kb_in[r], 16)

    def load_values(self, sp, item, r):
        sp.dma_start(self.vb[r][:], self.caches[2][item]).then_inc(self.vb_in[r], 16)
        sp.dma_start(self.va[r][:], self.caches[3][item]).then_inc(self.vb_in[r], 16)
        sp.dma_start(self.vn[r][:], self.caches[4][bass.ds(item * DSEQ, DSEQ), :]).then_inc(self.vb_in[r], 16)


def neg_lambda(mk, lam_in):
    vec, prod = mk.sb("lam_vec", [P, 4, HD]), mk.sb("lam_prod", [P, 2, HD])
    dots, exps = mk.sb("lam_dots", [P, 2]), mk.sb("lam_exps", [P, 2])
    out = mk.sb("neg_lambda", [P, 1])
    arrived, by_dve, by_act = mk.sem("lam_in"), mk.sem("lam_dve"), mk.sem("lam_act")

    def load(sp):
        sp.dma_start(vec[:], lam_in).then_inc(arrived, 16)

    def vector(dve):
        dve.wait_ge(arrived, 16)
        dve.tensor_tensor(prod[:], vec[:, 0:4:2, :], vec[:, 1:4:2, :], ALU.mult).then_inc(by_dve, 1)
        dve.wait_ge(by_dve, 1)
        dve.reduce_sum(dots[:], prod[:], axis=AX_X).then_inc(by_dve, 1)
        dve.wait_ge(by_act, 1)
        dve.tensor_scalar(exps[:, 0:1], exps[:, 0:1], LAMBDA_INIT, None, ALU.add).then_inc(by_dve, 1)
        dve.wait_ge(by_dve, 3)
        dve.tensor_tensor(out[:], exps[:, 1:2], exps[:, 0:1], ALU.subtract).then_inc(by_dve, 1)
        dve.wait_ge(by_dve, 4)

    def scalar(act):
        act.wait_ge(by_dve, 2)
        act.activation(exps[:], dots[:], ACT.Exp).then_inc(by_act, 1)

    return out, load, vector, scalar


def diff_prompt(nc, ahead, o, qo, kT, v_tok, ident):
    with ExitStack() as ctx:
        mk = Maker(nc, ctx, "diff")
        slot = [[mk.sb(f"slot{p}{m}", [P, P]) for m in range(2)] for p in range(2)]
        prob = [mk.sb(f"prob{p}", [P, 2, SEQ]) for p in range(4)]
        turned = [mk.sb(f"turned{p}", [P, NT, P]) for p in range(2)]
        nmax = [mk.sb(f"nmax{p}", [P, 2]) for p in range(2)]
        top = [mk.sb(f"top{p}", [P, 2]) for p in range(2)]
        norm = [mk.sb(f"norm{p}", [P, 2]) for p in range(2)]
        inv = [mk.sb(f"inv{p}", [P, 2]) for p in range(4)]
        coef = mk.sb("coef", [P, 1])
        waited = mk.sb("waited", [P, 1])
        neg_lam, strip = ahead.neg_lam, ahead.strip
        score = [mk.ps(f"score{m}", [P, SEQ]) for m in range(2)]
        blocks = mk.ps("blocks", [P, 2, 512])
        mixed = [mk.ps(f"mixed{p}", [P, 512]) for p in range(2)]

        padded, q_ready, scored, biased = mk.sem("padded"), mk.sem("q_ready"), mk.sem("scored"), mk.sem("biased")
        max_ready, exp_done, inv_done = mk.sem("max_ready"), mk.sem("exp_done"), mk.sem("inv_done")
        coef_done, weighted = mk.sem("coef_done"), mk.sem("weighted")
        block_ready, block_out = mk.sem("block_ready"), mk.sem("block_out")
        av_done, o_done, stripped = mk.sem("av_done"), mk.sem("o_done"), mk.sem("stripped")

        banks_before = [sum(1 + (u >= 4) for u in range(t)) for t in range(NT + 1)]
        PER_HEAD = banks_before[NT]

        def banks(t):
            return [(b, min(4, t + 1 - 4 * b)) for b in range(1 + (t >= 4))]

        block = ctx.enter_context(nc.Block())

        @block.sync
        def _(sp):
            ahead.load_tables(sp)
            ahead.load_keys(sp, 0, 0)
            ahead.load_values(sp, 0, 0)

        @block.gpsimd
        def _(pool):
            for p in range(2):
                for m in range(2):
                    pool.memset(slot[p][m][:], 0.0).then_inc(padded, 1)
            pool.wait_ge(padded, 4)

            def place(h, t):
                wait(pool, scored, 2 * (8 * h + t) - 2)
                for m in range(2):
                    rows = slice(m * HD, (m + 1) * HD)
                    pool.tensor_copy(slot[t % 2][m][rows, :], qo[rows, BH + h, t * P:(t + 1) * P]).then_inc(q_ready, 1)

            stages(pool, BH, NT, [(0, place)])

        @block.tensor
        def _(pe):
            def scores(h, t):
                for m in range(2):
                    pe.wait_ge(q_ready, 2 * (8 * h + t) + m + 1)
                    wait(pe, biased, 2 * (8 * h + t) + m - 1)
                    for c in range(0, (t + 1) * P, 512):
                        n = min(512, (t + 1) * P - c)
                        last = pe.matmul(score[m][:, c:c + n], slot[t % 2][m][:], kT[:, h + 1, c:c + n],
                                         start=True, stop=True)
                    last.then_inc(scored, 1)

            def turn(h, t):
                pe.wait_ge(weighted, 8 * h + t + 1)
                for b, n in banks(t):
                    count = PER_HEAD * h + banks_before[t] + b
                    wait(pe, block_out, count - 1)
                    side = (banks_before[t] + b) % 2
                    for j in range(n):
                        k = 4 * b + j
                        last = pe.transpose(blocks[:, side, j * P:(j + 1) * P],
                                            prob[t % 4][:, 0, k * P:(k + 1) * P], ident)
                    last.then_inc(block_ready, 1)

            def average(h, t):
                pe.wait_ge(block_out, PER_HEAD * h + banks_before[t + 1])
                wait(pe, o_done, 8 * h + t - 1)
                for k in range(t + 1):
                    last = pe.matmul(mixed[t % 2][:, 0:P], turned[t % 2][:, k, :], v_tok[:, k, bass.ds((h + 1) * P, P)],
                                     start=(k == 0), stop=(k == t))
                last.then_inc(av_done, 1)

            stages(pe, BH, NT, [(0, scores), (2, turn), (3, average)])

        @block.vector
        def _(dve):
            ahead.lambda_vector(dve)
            dve.wait_ge(ahead.strip_in, 16)

            def negate(item, t, m):
                dve.wait_ge(biased, 2 * item + m + 1)
                dve.tensor_scalar(nmax[t % 2][:, m:m + 1], top[t % 2][:, m:m + 1], -1.0, None,
                                  ALU.mult).then_inc(max_ready, 1)

            def bias(h, t):
                item = 8 * h + t
                if t == 0 and not (isinstance(h, int) and h == 0):
                    dve.wait_ge(biased, 2 * item)
                    dve.tensor_scalar(strip[:], strip[:], 0.25, None, ALU.mult).then_inc(stripped, 1)
                    dve.wait_ge(stripped, h)
                n = (t + 1) * P
                wait(dve, block_ready, PER_HEAD * h + (banks_before[t - 3] if t >= 3 else
                                                       banks_before[t + NT - 3] - PER_HEAD))
                dve.wait_ge(scored, 2 * item + 1)
                dve.memset(waited[:], 0.0)
                for m in range(2):
                    if m:
                        dve.wait_ge(scored, 2 * item + 2)
                        negate(item, t, 0)
                    dve.tensor_tensor_reduce(prob[t % 4][:, m, 0:n], score[m][:, 0:n], strip[:, SEQ - n:SEQ],
                                             1.0, LOWEST, ALU.add, ALU.max,
                                             top[t % 2][:, m:m + 1]).then_inc(biased, 1)
                negate(item, t, 1)

            def weigh(h, t):
                item = 8 * h + t
                dve.wait_ge(exp_done, 2 * item + 2)
                dve.reciprocal(inv[t % 4][:], norm[t % 2][:]).then_inc(inv_done, 1)
                dve.wait_ge(inv_done, item + 1)
                dve.scalar_tensor_tensor(out=coef[:], in0=inv[t % 4][:, 1:2], scalar=neg_lam[:, 0:1],
                                         in1=norm[t % 2][:, 0:1], op0=ALU.mult, op1=ALU.mult).then_inc(coef_done, 1)
                dve.wait_ge(coef_done, item + 1)
                n = (t + 1) * P
                dve.scalar_tensor_tensor(out=prob[t % 4][:, 0, 0:n], in0=prob[t % 4][:, 1, 0:n],
                                         scalar=coef[:, 0:1], in1=prob[t % 4][:, 0, 0:n],
                                         op0=ALU.mult, op1=ALU.add).then_inc(weighted, 1)

            def take(h, t):
                dve.wait_ge(av_done, 8 * h + t + 1)
                dve.tensor_scalar(o[:, 8 * h + t, :], mixed[t % 2][:, 0:P], inv[t % 4][:, 0:1], None,
                                  ALU.mult).then_inc(o_done, 1)

            stages(dve, BH, NT, [(4, take), (0, bias), (1, weigh)])

        @block.scalar
        def _(act):
            ahead.lambda_scalar(act)

            def clear(h, t):
                wait(act, av_done, 8 * h + t - 1)
                for b, n in banks(t):
                    count = PER_HEAD * h + banks_before[t] + b
                    side = (banks_before[t] + b) % 2
                    act.wait_ge(block_ready, count + 1)
                    act.activation(turned[t % 2][:, 4 * b:4 * b + n, :],
                                   blocks[:, side, 0:n * P].rearrange("p (k c) -> p k c", k=n),
                                   ACT.Copy).then_inc(block_out, 1)

            def exponent(h, t):
                item = 8 * h + t
                wait(act, weighted, item - 1)
                n = (t + 1) * P
                for m in range(2):
                    act.wait_ge(max_ready, 2 * item + m + 1)
                    act.activation(prob[t % 4][:, m, 0:n], prob[t % 4][:, m, 0:n], ACT.Exp,
                                   bias=nmax[t % 2][:, m:m + 1],
                                   accum_out=norm[t % 2][:, m:m + 1]).then_inc(exp_done, 1)

            stages(act, BH, NT, [(0, exponent), (2, clear)])


def window_prompt(nc, ahead, diff_o, qo, kT, v_tok, ident, g_sub):
    NORM = NCHUNK // 4
    with ExitStack() as ctx:
        mk = Maker(nc, ctx, "win")
        bias_tab = ahead.band
        nsink = mk.sb("nsink", [P, AG])
        slot = [mk.sb(f"slot{p}", [P, AG, P]) for p in range(2)]
        prob = [mk.sb(f"prob{p}", [P, AG, 2 * P]) for p in range(2)]
        turned = [mk.sb(f"turned{p}", [P, 2, AG * P]) for p in range(2)]
        o = [mk.sb(f"o{p}", [P, AG, P]) for p in range(2)]
        top = [mk.sb(f"top{p}", [P, AG]) for p in range(2)]
        nmax = [mk.sb(f"nmax{p}", [P, AG]) for p in range(2)]
        over = [mk.sb(f"over{p}", [P, AG]) for p in range(2)]
        sink_e = [mk.sb(f"sink_e{p}", [P, AG]) for p in range(2)]
        norm = [mk.sb(f"norm{p}", [P, AG]) for p in range(2)]
        den = [mk.sb(f"den{p}", [P, AG]) for p in range(2)]
        inv = [mk.sb(f"inv{p}", [P, AG]) for p in range(2)]
        waited = mk.sb("waited", [P, 1])
        squares = mk.sb("squares", [P, 4, P])
        normed = mk.sb("normed", [P, 4, P])
        ssq = mk.sb("ssq", [P, BH * NT])
        sub = Rsqrt(mk, "sub", P, BH * NT, P, SUB_EPS)
        gain_sub = mk.sb("gain_sub", [P, 1])
        score = mk.ps("score", [P, 2, 512])
        blocks = mk.ps("blocks", [P, 2, 512])
        mixed = mk.ps("mixed", [P, 512])
        o_turn = mk.ps("o_turn", [P, 512])
        d_turn = mk.ps("d_turn", [P, 512])

        padded, nsink_done, q_ready, scored = mk.sem("padded"), mk.sem("nsink_done"), mk.sem("q_ready"), mk.sem("scored")
        biased, max_ready, over_done = mk.sem("biased"), mk.sem("max_ready"), mk.sem("over_done")
        exp_done, den_done, inv_done = mk.sem("exp_done"), mk.sem("den_done"), mk.sem("inv_done")
        block_ready, out_act, out_dve = mk.sem("block_ready"), mk.sem("out_act"), mk.sem("out_dve")
        av_done, o_done, o_turned, o_out = mk.sem("av_done"), mk.sem("o_done"), mk.sem("o_turned"), mk.sem("o_out")
        d_squared, d_summed, d_scaled = mk.sem("d_squared"), mk.sem("d_summed"), mk.sem("d_scaled")
        d_turned, d_out, gain_done = mk.sem("d_turned"), mk.sem("d_out"), mk.sem("gain_done")

        def seen(g, r):
            if isinstance(g, int) and g == 0:
                return P, CHUNK * (r + 1)
            return CHUNK * r, BAND

        block = ctx.enter_context(nc.Block())

        @block.gpsimd
        def _(pool):
            for p in range(2):
                pool.memset(slot[p][:], 0.0).then_inc(padded, 1)
                pool.memset(prob[p][:], 0.0).then_inc(padded, 1)
            pool.wait_ge(padded, 4)

            def place(g, r):
                wait(pool, scored, 2 * g + r - 1)
                for m in range(2):
                    rows, cols = slice(m * HD, (m + 1) * HD), slice(m * CHUNK, (m + 1) * CHUNK)
                    pool.tensor_copy(slot[r][rows, :, cols],
                                     qo[rows, 0:AG, bass.ds((2 * g + r) * CHUNK, CHUNK)]).then_inc(q_ready, 1)

            stages(pool, NCHUNK // 2, 2, [(0, place)])

        @block.tensor
        def _(pe):
            def scores(g, r):
                item = 2 * g + r
                _, n = seen(g, r)
                pe.wait_ge(q_ready, 2 * item + 2)
                wait(pe, biased, AG * item)
                for h in range(AG):
                    last = pe.matmul(score[:, h // 2, (h % 2) * 256:(h % 2) * 256 + n], slot[r][:, h, :],
                                     kT[:, 0, bass.ds((item + 1) * CHUNK - n, n)], start=True, stop=True)
                last.then_inc(scored, 1)

            def turn(g, r):
                item = 2 * g + r
                pe.wait_ge(exp_done, (AG + 1) * (item + 1))
                first = 1 if isinstance(g, int) and g == 0 else 0
                for b in range(first, 2):
                    wait(pe, (out_act, out_dve)[b], item)
                    for h in range(AG):
                        last = pe.transpose(blocks[:, b, h * P:(h + 1) * P],
                                            prob[r][:, h, b * P:(b + 1) * P], ident)
                last.then_inc(block_ready, 1)

            def average(g, r):
                item = 2 * g + r
                pe.wait_ge(out_act, item + 1)
                pe.wait_ge(out_dve, item + 1)
                wait(pe, o_done, item)
                first = 1 if isinstance(g, int) and g == 0 else 0
                for h in range(AG):
                    for b in range(first, 2):
                        last = pe.matmul(mixed[:, h * P:(h + 1) * P], turned[r][:, b, h * P:(h + 1) * P],
                                         v_tok[:, g - 1 + b, 0:P], start=(b == first), stop=(b == 1))
                last.then_inc(av_done, 1)

            def turn_o(g, r):
                item = 2 * g + r
                pe.wait_ge(o_done, item + 1)
                wait(pe, o_out, 2 * item)
                for h in range(AG):
                    last = pe.transpose(o_turn[:, h * P:(h + 1) * P], o[r][:, h, :], ident)
                last.then_inc(o_turned, 1)

            def turn_diff(g, r):
                j = 2 * (g - NORM) + r
                pe.wait_ge(d_scaled, j + 1)
                wait(pe, d_out, j)
                for i in range(4):
                    last = pe.transpose(d_turn[:, i * P:(i + 1) * P], normed[:, i, :], ident)
                last.then_inc(d_turned, 1)

            pipeline(pe, (0, 1, 2, 3, 1), [(NORM, (scores, turn, average, turn_o, None)),
                                           (2 * NORM, (scores, turn, average, turn_o, turn_diff))], 2)

        @block.vector
        def _(dve):
            dve.wait_ge(ahead.band_in, 32)
            dve.wait_ge(padded, 4)
            dve.tensor_scalar(nsink[:], ahead.sink[:, 0:AG], -1.0, None, ALU.mult).then_inc(nsink_done, 1)
            dve.wait_ge(nsink_done, 1)
            dve.tensor_scalar(gain_sub[:], g_sub, 1.0 - LAMBDA_INIT, None, ALU.mult).then_inc(gain_done, 1)

            def bias(g, r):
                item = 2 * g + r
                col, n = seen(g, r)
                dve.wait_ge(scored, item + 1)
                wait(dve, block_ready, item - 1)
                dve.memset(waited[:], 0.0)
                for h in range(AG):
                    dve.tensor_tensor_reduce(prob[r][:, h, col:col + n],
                                             score[:, h // 2, (h % 2) * 256:(h % 2) * 256 + n],
                                             bias_tab[:, h, BAND - n:BAND], 1.0, LOWEST, ALU.add, ALU.max,
                                             top[r][:, h:h + 1]).then_inc(biased, 1)
                dve.wait_ge(biased, AG * (item + 1))
                dve.scalar_tensor_tensor(out=nmax[r][:], in0=top[r][:], scalar=-1.0, in1=nsink[:],
                                         op0=ALU.mult, op1=ALU.min).then_inc(max_ready, 1)
                dve.wait_ge(max_ready, item + 1)
                dve.tensor_tensor(over[r][:], nmax[r][:], nsink[:], ALU.subtract).then_inc(over_done, 1)

            def total(g, r):
                item = 2 * g + r
                dve.wait_ge(exp_done, (AG + 1) * (item + 1))
                dve.tensor_tensor(den[r][:], norm[r][:], sink_e[r][:], ALU.add).then_inc(den_done, 1)
                dve.wait_ge(den_done, item + 1)
                dve.reciprocal(inv[r][:], den[r][:]).then_inc(inv_done, 1)

            def clear(g, r):
                item = 2 * g + r
                dve.wait_ge(block_ready, item + 1)
                dve.tensor_copy(turned[r][:, 1, :], blocks[:, 1, :]).then_inc(out_dve, 1)

            def take(g, r):
                item = 2 * g + r
                dve.wait_ge(av_done, item + 1)
                wait(dve, o_turned, item - 1)
                dve.tensor_tensor(o[r][:], mixed[:].rearrange("p (h c) -> p h c", h=AG),
                                  inv[r][:, :, None].to_broadcast([P, AG, P]), ALU.mult).then_inc(o_done, 1)

            def sum_diff(g, r):
                j = 2 * g + r
                dve.wait_ge(d_squared, j + 1)
                dve.reduce_sum(ssq[:, bass.ds(4 * j, 4)], squares[:], axis=AX_X).then_inc(d_summed, 1)

            def scale_diff(g, r):
                j = 2 * (g - NORM) + r
                if isinstance(g, int) and j == 0:
                    dve.wait_ge(d_summed, 2 * NORM)
                    sub.vector(dve, ssq[:])
                wait(dve, d_turned, j)
                dve.tensor_tensor(normed[:], diff_o[:, bass.ds(4 * j, 4), :],
                                  sub.out[:, bass.ds(4 * j, 4), None].to_broadcast([P, 4, P]),
                                  ALU.mult).then_inc(d_scaled, 1)

            pipeline(dve, (3, 0, 1, 1, 1, 1), [(NORM, (take, bias, total, clear, sum_diff, None)),
                                               (2 * NORM, (take, bias, total, clear, None, scale_diff))], 2)

        @block.scalar
        def _(act):
            def exponent(g, r):
                item = 2 * g + r
                col, n = seen(g, r)
                act.wait_ge(over_done, item + 1)
                for h in range(AG):
                    act.activation(prob[r][:, h, col:col + n], prob[r][:, h, col:col + n], ACT.Exp,
                                   bias=nmax[r][:, h:h + 1], accum_out=norm[r][:, h:h + 1]).then_inc(exp_done, 1)
                act.activation(sink_e[r][:], over[r][:], ACT.Exp).then_inc(exp_done, 1)

            def clear(g, r):
                item = 2 * g + r
                act.wait_ge(block_ready, item + 1)
                if isinstance(g, int) and g == 0:
                    act.nop().then_inc(out_act, 1)
                else:
                    act.activation(turned[r][:, 0, :], blocks[:, 0, :], ACT.Copy).then_inc(out_act, 1)

            def store_o(g, r):
                item = 2 * g + r
                act.wait_ge(o_turned, item + 1)
                for m in range(2):
                    rows = slice(m * HD, (m + 1) * HD)
                    act.activation(qo[rows, 0:AG, bass.ds(item * CHUNK, CHUNK)],
                                   o_turn[:].rearrange("p (h c) -> p h c", h=AG)[rows, :, m * CHUNK:(m + 1) * CHUNK],
                                   ACT.Copy).then_inc(o_out, 1)

            def square_diff(g, r):
                j = 2 * g + r
                wait(act, d_summed, j)
                act.activation(squares[:], diff_o[:, bass.ds(4 * j, 4), :], ACT.Square).then_inc(d_squared, 1)

            def store_diff(g, r):
                j = 2 * (g - NORM) + r
                if isinstance(g, int) and j == 0:
                    act.wait_ge(gain_done, 1)
                act.wait_ge(d_turned, j + 1)
                act.activation(qo[:, BH + g - NORM, 512 * r:512 * r + 512], d_turn[:], ACT.Copy,
                               scale=gain_sub[:]).then_inc(d_out, 1)

            def root_diff(g, r):
                if isinstance(g, int) and g == NORM and r == 0:
                    sub.scalar(act)

            pipeline(act, (1, 0, 3, 0, 1, 1), [
                (NORM, (clear, exponent, store_o, square_diff, None, None)),
                (2 * NORM, (clear, exponent, store_o, None, root_diff, store_diff))], 2)
            act.wait_ge(o_out, 2 * NCHUNK)
            act.wait_ge(d_out, 2 * NORM)


def sample(nc, ahead, z_dram, qo, kT, ident):
    ROW = 2 * DSEQ
    with ExitStack() as ctx:
        mk = Maker(nc, ctx, "smp")
        ahead.kb.append(mk.sb("kb1", [P, BH, PAST]))
        ahead.vb.append(mk.sb("vb1", [P, PAST // P, BH * P]))
        kb, vb, ka, va, vn = ahead.kb, ahead.vb, ahead.ka, ahead.va, ahead.vn
        nsink = mk.sb("nsink", [P, 1])
        row_coef = mk.sb("row_coef", [P, 1])
        slot_b = [mk.sb(f"slot_b{p}", [P, BH * P]) for p in range(2)]
        slot_a = [mk.sb(f"slot_a{p}", [P, P]) for p in range(2)]
        z = [mk.sb(f"z{p}", [P, SEQ]) for p in range(2)]
        prob_b, prob_a = mk.sb("prob_b", [P, PAST + DSEQ]), mk.sb("prob_a", [P, WIN + DSEQ])
        turned = mk.sb("turned", [P, 11, P])
        waited = mk.sb("waited", [P, 1])
        by_b, by_a = mk.sb("by_b", [P, P]), mk.sb("by_a", [P, P])
        o_b = mk.sb("o_b", [P, P])
        top, nmax, inv = mk.sb("top", [P, 2]), mk.sb("nmax", [P, 2]), mk.sb("inv", [P, 2])
        over, coef, den = mk.sb("over", [P, 1]), mk.sb("coef", [P, 1]), mk.sb("den", [P, 2])
        norm = mk.sb("norm", [P, 3])
        score = mk.ps("score", [P, 3, 512])
        blocks = mk.ps("blocks", [P, 3, 512])
        mixed_b = mk.ps("mixed_b", [P, 512])
        mixed_a = mk.ps("mixed_a", [P, 512])
        score_b = score[:].rearrange("p b c -> p (b c)")[:, 0:PAST + DSEQ]
        score_a = score[:, 2, P:P + WIN + DSEQ]

        z_in = [mk.sem(f"z_in{p}") for p in range(2)]
        padded, rows_done, q_ready, scored = mk.sem("padded"), mk.sem("rows_done"), mk.sem("q_ready"), mk.sem("scored")
        biased, max_ready, over_done = mk.sem("biased"), mk.sem("max_ready"), mk.sem("over_done")
        exp_done, den_done, inv_done = mk.sem("exp_done"), mk.sem("den_done"), mk.sem("inv_done")
        coef_done, turner_ready, block_ready = mk.sem("coef_done"), mk.sem("turner_ready"), mk.sem("block_ready")
        out_act, out_dve = mk.sem("out_act"), mk.sem("out_dve")
        av_done, o_done, posted = mk.sem("av_done"), mk.sem("o_done"), mk.sem("posted")
        stored_a, stored_b, gated = mk.sem("stored_a"), mk.sem("stored_b"), mk.sem("gated")

        block = ctx.enter_context(nc.Block())

        @block.sync
        def _(sp):
            def load(g, r):
                item = 2 * g + r
                if not isinstance(g, int) or item > 0:
                    wait(sp, scored, item - 1)
                    ahead.load_keys(sp, item, r)
                    wait(sp, av_done, item - 1)
                    ahead.load_values(sp, item, r)
                wait(sp, gated, item - 1)
                sp.dma_start(z[r][:], z_dram[item][:, 0:SEQ]).then_inc(z_in[r], 16)

            stages(sp, DEC // 2, 2, [(0, load)])

        @block.gpsimd
        def _(pool):
            for p in range(2):
                pool.memset(slot_b[p][:], 0.0).then_inc(padded, 1)
                pool.memset(slot_a[p][:], 0.0).then_inc(padded, 1)
            pool.wait_ge(padded, 4)

            def place(g, r):
                item = 2 * g + r
                wait(pool, scored, item - 1)
                wait(pool, gated, item - 1)
                for m in range(2):
                    rows = slice(m * HD, (m + 1) * HD)
                    to = slot_b[r][rows, :].rearrange("p (h x) -> p h x", x=P)
                    for h in range(BH):
                        pool.tensor_copy(to[:, h, h * ROW + m * DSEQ:h * ROW + (m + 1) * DSEQ],
                                         qo[rows, BH + h, bass.ds(SEQ + item * DSEQ, DSEQ)]).then_inc(q_ready, 1)
                    pool.tensor_copy(slot_a[r][rows, m * HD:(m + 1) * HD].rearrange("p (g t) -> p g t", g=AG),
                                     qo[rows, 0:AG, bass.ds(SEQ + item * DSEQ, DSEQ)]).then_inc(q_ready, 1)

            def gate(g, r):
                item = 2 * g + r
                pool.wait_ge(z_in[r], 16 * (g + 1))
                last = isinstance(g, int) and item == DEC - 1
                pool.wait_ge(q_ready, 10 * (item + 1 if last else item + 2))
                pool.tensor_tensor(qo[:, item, 0:SEQ], qo[:, item, 0:SEQ], z[r][:], ALU.mult).then_inc(gated, 1)

            stages(pool, DEC // 2, 2, [(0, place), (1, gate)])
            pool.wait_ge(gated, DEC)

        @block.tensor
        def _(pe):
            def scores(g, r):
                item = 2 * g + r
                pe.wait_ge(ahead.kb_in[r], 32 * (g + 1))
                pe.wait_ge(q_ready, 10 * (item + 1))
                wait(pe, biased, 2 * item)
                for c in range(3):
                    n = 512 if c < 2 else DSEQ
                    for h in range(BH):
                        keys = (kb[r][:, h, c * 512:(c + 1) * 512] if c < 2 else
                                kT[:, h + 1, bass.ds(SEQ + item * DSEQ, DSEQ)])
                        pe.matmul(score[:, c, 0:n], slot_b[r][:, h * P:(h + 1) * P], keys,
                                  start=(h == 0), stop=(h == BH - 1))
                pe.matmul(score_a[:, 0:WIN], slot_a[r][:], ka[r][:], start=True, stop=True)
                pe.matmul(score_a[:, WIN:WIN + DSEQ], slot_a[r][:], kT[:, 0, bass.ds(SEQ + item * DSEQ, DSEQ)],
                          start=True, stop=True).then_inc(scored, 1)

            def turn(g, r):
                item = 2 * g + r
                pe.wait_ge(turner_ready, 2 * (item + 1))
                pe.matmul(blocks[:, 2, 0:P], prob_a[:, 0:P], by_a[:], start=True, stop=True)
                pe.matmul(blocks[0:DSEQ, 2, P:2 * P], prob_b[:, PAST:PAST + DSEQ], by_b[:], start=True, stop=True)
                pe.matmul(blocks[0:DSEQ, 2, 2 * P:3 * P], prob_a[:, WIN:WIN + DSEQ], by_a[:],
                          start=True, stop=True).then_inc(block_ready, 1)
                for j in range(2):
                    for i in range(4):
                        last = pe.matmul(blocks[:, j, i * P:(i + 1) * P],
                                         prob_b[:, (4 * j + i) * P:(4 * j + i + 1) * P], by_b[:], start=True, stop=True)
                    last.then_inc(block_ready, 1)

            def post(g, r):
                item = 2 * g + r
                pe.wait_ge(o_done, BH * (item + 1))
                pe.wait_ge(stored_a, 2 * (item + 1))
                pe.transpose(mixed_a[:, P:2 * P], o_b[:], ident).then_inc(posted, 1)

            def average(g, r):
                item = 2 * g + r
                pe.wait_ge(ahead.vb_in[r], 48 * (g + 1))
                pe.wait_ge(out_act, 2 * (item + 1))
                pe.wait_ge(out_dve, 2 * (item + 1))
                wait(pe, o_done, BH * item)
                wait(pe, stored_b, item)
                for k in range(PAST // P):
                    pe.matmul(mixed_b[:], turned[:, k, :], vb[r][:, k, :], start=(k == 0), stop=False)
                pe.matmul(mixed_b[:], turned[0:DSEQ, 9, :], vn[r][:, P:ROWS], start=False, stop=True)
                pe.matmul(mixed_a[:, 0:P], va[r][:], turned[:, 8, :], start=True, stop=False)
                pe.matmul(mixed_a[:, 0:P], vn[r][:, 0:P], turned[0:DSEQ, 10, :],
                          start=False, stop=True).then_inc(av_done, 1)

            stages(pe, DEC // 2, 2, [(1, turn), (2, post), (0, scores), (1, average)])

        @block.vector
        def _(dve):
            dve.wait_ge(ahead.sample_in, 64)
            dve.tensor_scalar(nsink[:], ahead.sink[:, AG:AG + 1], -1.0, None, ALU.mult).then_inc(rows_done, 1)
            dve.scalar_tensor_tensor(out=row_coef[:], in0=ahead.is_map[:, 1:2], scalar=ahead.neg_lam[:, 0:1],
                                     in1=ahead.is_map[:, 0:1], op0=ALU.mult, op1=ALU.add).then_inc(rows_done, 1)
            dve.wait_ge(rows_done, 2)

            def bias(g, r):
                item = 2 * g + r
                dve.wait_ge(scored, item + 1)
                wait(dve, block_ready, 3 * item)
                dve.memset(waited[:], 0.0)
                dve.tensor_tensor_reduce(prob_b[:], score_b, ahead.bias_b[:], 1.0, LOWEST, ALU.add, ALU.max,
                                         top[:, 0:1]).then_inc(biased, 1)
                dve.tensor_tensor_reduce(prob_a[:], score_a, ahead.bias_a[:], 1.0, LOWEST, ALU.add, ALU.max,
                                         top[:, 1:2]).then_inc(biased, 1)
                dve.wait_ge(biased, 2 * (item + 1))
                dve.tensor_scalar(nmax[:, 0:1], top[:, 0:1], -1.0, None, ALU.mult).then_inc(max_ready, 1)
                dve.scalar_tensor_tensor(out=nmax[:, 1:2], in0=top[:, 1:2], scalar=-1.0, in1=nsink[:],
                                         op0=ALU.mult, op1=ALU.min).then_inc(max_ready, 1)
                dve.wait_ge(max_ready, 2 * (item + 1))
                dve.tensor_tensor(over[:], nmax[:, 1:2], nsink[:], ALU.subtract).then_inc(over_done, 1)

            def factors(g, r):
                item = 2 * g + r
                dve.wait_ge(exp_done, 3 * (item + 1))
                dve.tensor_copy(den[:, 0:1], norm[:, 0:1]).then_inc(den_done, 1)
                dve.tensor_tensor(den[:, 1:2], norm[:, 1:2], norm[:, 2:3], ALU.add).then_inc(den_done, 1)
                dve.wait_ge(den_done, 2 * (item + 1))
                dve.reciprocal(inv[:], den[:]).then_inc(inv_done, 1)
                dve.wait_ge(inv_done, item + 1)
                dve.tensor_scalar(by_a[:], ident, inv[:, 1:2], None, ALU.mult).then_inc(turner_ready, 1)
                dve.tensor_tensor(coef[:], inv[:, 0:1], row_coef[:], ALU.mult).then_inc(coef_done, 1)
                dve.wait_ge(coef_done, item + 1)
                dve.tensor_scalar(by_b[:], ahead.pick[:], coef[:, 0:1], None, ALU.mult).then_inc(turner_ready, 1)

            def clear(g, r):
                item = 2 * g + r
                dve.wait_ge(block_ready, 3 * item + 1)
                wait(dve, av_done, item)
                dve.tensor_copy(turned[:, 8, :], blocks[:, 2, 0:P]).then_inc(out_dve, 1)
                dve.tensor_copy(turned[0:DSEQ, 9:11, :],
                                blocks[0:DSEQ, 2, P:3 * P].rearrange("p (k c) -> p k c", k=2)).then_inc(out_dve, 1)

            def take(g, r):
                item = 2 * g + r
                dve.wait_ge(av_done, item + 1)
                wait(dve, posted, item)
                for h in range(BH):
                    rows = slice(h * ROW, (h + 1) * ROW)
                    dve.tensor_copy(o_b[rows, :], mixed_b[rows, h * P:(h + 1) * P]).then_inc(o_done, 1)

            stages(dve, DEC // 2, 2, [(1, factors), (2, take), (1, clear), (0, bias)])

        @block.scalar
        def _(act):
            def exponent(g, r):
                item = 2 * g + r
                act.wait_ge(over_done, item + 1)
                act.activation(prob_b[:], prob_b[:], ACT.Exp, bias=nmax[:, 0:1],
                               accum_out=norm[:, 0:1]).then_inc(exp_done, 1)
                act.activation(prob_a[:], prob_a[:], ACT.Exp, bias=nmax[:, 1:2],
                               accum_out=norm[:, 1:2]).then_inc(exp_done, 1)
                act.activation(norm[:, 2:3], over[:], ACT.Exp).then_inc(exp_done, 1)

            def clear(g, r):
                item = 2 * g + r
                for j in range(2):
                    act.wait_ge(block_ready, 3 * item + j + 2)
                    act.activation(turned[:, 4 * j:4 * j + 4, :], blocks[:, j, :].rearrange("p (k c) -> p k c", k=4),
                                   ACT.Copy).then_inc(out_act, 1)

            def store_a(g, r):
                item = 2 * g + r
                act.wait_ge(av_done, item + 1)
                for m in range(2):
                    rows = slice(m * HD, (m + 1) * HD)
                    act.activation(qo[rows, 0:AG, bass.ds(SEQ + item * DSEQ, DSEQ)],
                                   mixed_a[rows, m * HD:(m + 1) * HD].rearrange("p (g t) -> p g t", g=AG),
                                   ACT.Copy).then_inc(stored_a, 1)

            def store_b(g, r):
                item = 2 * g + r
                act.wait_ge(posted, item + 1)
                act.activation(qo[:, BH:8, bass.ds(SEQ + item * DSEQ, DSEQ)],
                               mixed_a[:, P:2 * P].rearrange("p (h x) -> p h x", x=ROW)[:, :, 0:DSEQ],
                               ACT.Copy).then_inc(stored_b, 1)

            stages(act, DEC // 2, 2, [(2, store_a), (1, clear), (2, store_b), (0, exponent)])
            act.wait_ge(stored_a, 2 * DEC)
            act.wait_ge(stored_b, DEC)


def merge(nc, xT, pT, w_out, w_gate, w_ple, z_dram, yT, qo, ident, ones, g_sub, g_post, g_ple):
    NB = 8
    PLE0, GATE0, END = NB, 2 * NB, 3 * NB
    with ExitStack() as ctx:
        mk = Maker(nc, ctx, "mrg")
        a_hi, a_lo = mk.sb("a_hi", [P, KT, TOK], F32R), mk.sb("a_lo", [P, KT, TOK], F32R)
        mix = mk.sb("mix", [P, KT, TOK])
        x = qo
        p_emb = mk.sb("p_emb", [P, PKT, TOK])
        w_raw = [mk.sb(f"w_raw{s}", [P, KT, P]) for s in range(2)]
        w_hi = [mk.sb(f"w_hi{s}", [P, KT, P], F32R) for s in range(2)]
        w_lo = [mk.sb(f"w_lo{s}", [P, KT, P], F32R) for s in range(2)]
        work = [mk.sb(f"work{s}", [P, TOK]) for s in range(2)]
        total = mk.sb("total", [P, TOK])
        rms = mk.sb("rms", [P, TOK])
        gain_sub = mk.sb("gain_sub", [P, 1])
        SAMPLE = DEC * DSEQ
        z = mix[:, 1, 0:8 * SAMPLE].rearrange("p (b t) -> p b t", b=8)
        sample_o = qo[:, BH:8, SEQ:TOK]
        sub_norm = Rsqrt(mk, "sub", P, BH * SAMPLE, P, SUB_EPS,
                         [mix[:, j // 2 * 2, j % 2 * 512:j % 2 * 512 + 512] for j in range(4)])
        mix_norm = Rsqrt(mk, "mix_norm", P, TT, D, EPS)
        ple_norm = Rsqrt(mk, "ple_norm", P, TT, D, EPS)
        acc = [mk.ps(f"acc{s}", [P, NCH, 512]) for s in range(2)]
        small = mk.ps("small", [P, 2, 512])

        z_in = mk.sem("z_in")
        w_in = [mk.sem(f"w_in{s}") for s in range(2)]
        x_in, p_in, y_out = mk.sem("x_in"), mk.sem("p_in"), mk.sem("y_out")
        sub_squared, sub_summed, sub_scaled = mk.sem("sub_squared"), mk.sem("sub_summed"), mk.sem("sub_scaled")
        gain_done, gated, a_hi_done, a_lo_done = mk.sem("gain_done"), mk.sem("gated"), mk.sem("a_hi_done"), mk.sem("a_lo_done")
        w_hi_done, w_lo_done = mk.sem("w_hi_done"), mk.sem("w_lo_done")
        product = mk.sem("product")
        mix_out, ple_out = mk.sem("mix_out"), mk.sem("ple_out")
        squared, added = mk.sem("squared"), mk.sem("added")
        sums, diag_done, spread, rms_done = mk.sem("sums"), mk.sem("diag"), mk.sem("spread"), mk.sem("rms_done")
        normed, h_done, h_hi_done, h_lo_done = mk.sem("normed"), mk.sem("h_done"), mk.sem("h_hi"), mk.sem("h_lo")
        sigmoid, ple_scaled, ple_gated, y_done = mk.sem("sigmoid"), mk.sem("ple_scaled"), mk.sem("ple_gated"), mk.sem("y_done")

        def split_count(j):
            return j + 1 if j < PLE0 else j - GATE0 + NB + 1

        def loads_of_slot(j):
            return j // 2 + 1 if j < PLE0 else NB // 2 + 1 + (j >= GATE0) * ((j - GATE0) // 2 + 1)

        def ple_weights(j):
            return w_raw[j // 4][:].rearrange("p (b k) c -> p b k c", k=PKT)[:, j % 4]

        block = ctx.enter_context(nc.Block())

        @block.sync
        def _(sp):
            for j in range(2):
                sp.dma_start(w_raw[j][:], w_out[j]).then_inc(w_in[j], 16)
                if j == 0:
                    sp.dma_start(z, z_dram[:, :, SEQ:TOK].rearrange("b p t -> p b t")).then_inc(z_in, 16)
            for j in range(2, 4):
                sp.wait_ge(w_lo_done, j - 1)
                sp.dma_start(w_raw[j % 2][:], w_out[j]).then_inc(w_in[j % 2], 16)
            for k in range(KT):
                sp.wait_ge(a_lo_done, k + 1)
                sp.dma_start(x[:, k, :], xT[:, k, :]).then_inc(x_in, 16)
            sp.dma_start(p_emb[:], pT).then_inc(p_in, 16)
            for j in range(4, NB):
                sp.wait_ge(w_lo_done, j - 1)
                sp.dma_start(w_raw[j % 2][:], w_out[j]).then_inc(w_in[j % 2], 16)
            for r in range(2):
                sp.wait_ge(w_lo_done, NB - 1 + r)
                sp.dma_start(w_raw[r][:].rearrange("p (b k) c -> p b (k c)", k=PKT),
                             w_ple[4 * r:4 * r + 4].rearrange("b p k c -> p b (k c)")).then_inc(w_in[r], 16)
            for r in range(2):
                sp.wait_ge(product, PLE0 + 4 * r + 4)
                sp.dma_start(w_raw[r][:], w_gate[r]).then_inc(w_in[r], 16)

            def store_y(j):
                sp.wait_ge(y_done, j + 1)
                sp.dma_start(yT[j], mix[:, j, :]).then_inc(y_out, 16)

            for j in range(2, NB):
                sp.wait_ge(w_lo_done, NB + j - 1)
                sp.dma_start(w_raw[j % 2][:], w_gate[j]).then_inc(w_in[j % 2], 16)
                if j >= 4:
                    store_y(j - 4)
            for j in range(NB - 4, NB):
                store_y(j)
            sp.wait_ge(y_out, 16 * NB)

        @block.scalar
        def _(act):
            def high(j):
                act.wait_ge(w_in[j % 2], 16 * loads_of_slot(j))
                if j >= 2:
                    act.wait_ge(product, j - 1 if j < PLE0 or j >= GATE0 + 2 else NB)
                act.activation(w_hi[j % 2][:], w_raw[j % 2][:], ACT.Copy).then_inc(w_hi_done, 1)

            def square(j, counted):
                if counted + j >= 2:
                    act.wait_ge(added, counted + max(j - 1, 2) if j >= 2 else counted)
                act.activation(work[j % 2][:], mix[:, j, :], ACT.Square).then_inc(squared, 1)

            act.activation(work[0][:, 0:BH * SAMPLE].rearrange("p (h t) -> p h t", h=BH), sample_o,
                           ACT.Square).then_inc(sub_squared, 1)
            high(0)
            for k in range(KT):
                act.wait_ge(gated, 1 if k < AG else 2)
                act.activation(a_hi[:, k, :], qo[:, k, :], ACT.Copy).then_inc(a_hi_done, 1)
                if k == 0:
                    sub_norm.scalar(act)
                    high(1)
            for j in range(2, NB):
                high(j)
                act.wait_ge(mix_out, j - 1)
                square(j - 2, 0)
            for j in range(NB - 2, NB):
                act.wait_ge(mix_out, j + 1)
                square(j, 0)
            mix_norm.scalar(act)

            for j in range(NB):
                act.wait_ge(product, PLE0 + j + 1)
                act.wait_ge(h_done, j + 1)
                act.activation(by_runs(mix[:, j, :]), acc[j % 2][:, :, 0:RUN], ACT.Copy).then_inc(ple_out, 1)
                act.activation(a_hi[:, j, :], x[:, j, :], ACT.Copy).then_inc(h_hi_done, 1)
                act.wait_ge(ple_out, j + 1)
                square(j, NB)
                if j == NB - 2:
                    high(GATE0)
            high(GATE0 + 1)
            ple_norm.scalar(act)

            for j in range(GATE0, END):
                i = j - GATE0
                act.wait_ge(product, j + 1)
                if i < 2:
                    act.wait_ge(added, 2 * NB)
                else:
                    act.wait_ge(ple_gated, i - 1)
                act.activation(by_runs(work[j % 2][:]), acc[j % 2][:, :, 0:RUN], ACT.Sigmoid).then_inc(sigmoid, 1)
                if j + 2 < END:
                    high(j + 2)

        @block.gpsimd
        def _(pool):
            def low(j):
                pool.wait_ge(w_hi_done, split_count(j))
                pool.tensor_tensor(w_lo[j % 2][:], w_raw[j % 2][:], w_hi[j % 2][:].bitcast(F32),
                                   ALU.subtract).then_inc(w_lo_done, 1)

            for j in range(NB):
                low(j)
            pool.wait_ge(x_in, 16 * KT)
            for j in range(NB):
                pool.wait_ge(normed, j + 1)
                pool.tensor_tensor(x[:, j, :], x[:, j, :], mix[:, j, :], ALU.add).then_inc(h_done, 1)
            for j in range(GATE0, END):
                low(j)

        @block.tensor
        def _(pe):
            def free_banks(j):
                if j >= GATE0 + 2:
                    pe.wait_ge(sigmoid, j - GATE0 - 1)
                elif j >= PLE0 + 2:
                    pe.wait_ge(ple_out, j - PLE0 - 1)
                elif j >= 2:
                    pe.wait_ge(mix_out, j - 1)

            def multiply(j, parts=()):
                pe.wait_ge(w_lo_done, split_count(j))
                free_banks(j)
                for k in range(KT):
                    for s in parts:
                        pe.wait_ge(s, k + 1)
                    for n in range(NCH):
                        last = three_passes(pe, acc[j % 2][:, n, 0:RUN], w_hi[j % 2][:, k, :], w_lo[j % 2][:, k, :],
                                            run(a_hi[:, k, :], n), run(a_lo[:, k, :], n),
                                            start=(k == 0), stop=(k == KT - 1))
                last.then_inc(product, 1)

            def embed(j):
                i = j - PLE0
                pe.wait_ge(w_in[i // 4], 16 * (NB // 2 + 1))
                free_banks(j)
                for k in range(PKT):
                    for n in range(NCH):
                        last = pe.matmul(acc[j % 2][:, n, 0:RUN], ple_weights(i)[:, k, :], run(p_emb[:, k, :], n),
                                         start=(k == 0), stop=(k == PKT - 1))
                last.then_inc(product, 1)

            def statistics(which):
                pe.wait_ge(added, NB * (which + 1))
                for t in range(TT):
                    last = pe.matmul(small[:, 0, t:t + 1], total[:, t * P:(t + 1) * P], ones[:, 0:1],
                                     start=True, stop=True)
                last.then_inc(sums, 1)

            def to_all(which):
                pe.wait_ge(diag_done, TT * (which + 1))
                for n in range(NCH):
                    if n == 2:
                        pe.wait_ge(rms_done, NCH * which + 1)
                    pe.matmul(small[:, n % 2, 0:RUN], ones, run(total[:], n), start=True, stop=True).then_inc(spread, 1)

            pe.wait_ge(sub_squared, 1)
            pe.matmul(small[:, 0, :], ones, work[0][:, 0:BH * SAMPLE], start=True, stop=True).then_inc(sub_summed, 1)
            for j in range(NB):
                multiply(j, (a_hi_done, a_lo_done) if j == 0 else ())
            pe.wait_ge(p_in, 16)
            embed(PLE0)
            statistics(0)
            embed(PLE0 + 1)
            to_all(0)
            for j in range(PLE0 + 2, GATE0):
                embed(j)
            multiply(GATE0, (h_hi_done, h_lo_done))
            statistics(1)
            to_all(1)
            for j in range(GATE0 + 1, END):
                multiply(j)

        @block.vector
        def _(dve):
            def low(source, done, j, count):
                dve.wait_ge(done, j + 1)
                dve.tensor_tensor(a_lo[:, j, :], source[:, j, :], a_hi[:, j, :].bitcast(F32),
                                  ALU.subtract).then_inc(count, 1)

            dve.tensor_scalar(gain_sub[:], g_sub, 1.0 - LAMBDA_INIT, None, ALU.mult).then_inc(gain_done, 1)
            dve.wait_ge(z_in, 16)
            dve.tensor_tensor(qo[:, 0:AG, SEQ:TOK], qo[:, 0:AG, SEQ:TOK], z[:, 0:AG], ALU.mult).then_inc(gated, 1)
            dve.wait_ge(sub_summed, 1)
            sub_norm.mean(dve, small[:, 0, :])
            low(qo, a_hi_done, 0, a_lo_done)
            sub_norm.invert(dve)
            dve.wait_ge(gain_done, 1)
            dve.scalar_tensor_tensor(out=sample_o, in0=sample_o, scalar=gain_sub[:, 0:1],
                                     in1=sub_norm.out.rearrange("p (h t) -> p h t", h=BH),
                                     op0=ALU.mult, op1=ALU.mult).then_inc(sub_scaled, 1)
            dve.wait_ge(sub_scaled, 1)
            dve.tensor_tensor(sample_o, sample_o, z[:, BH:8], ALU.mult).then_inc(gated, 1)
            for k in range(1, KT):
                low(qo, a_hi_done, k, a_lo_done)

            def add(j, counted):
                dve.wait_ge(squared, counted + j + 1)
                if j == 1:
                    dve.tensor_tensor(total[:], work[0][:], work[1][:], ALU.add).then_inc(added, 2)
                elif j > 1:
                    dve.wait_ge(added, counted + j)
                    dve.tensor_tensor(total[:], total[:], work[j % 2][:], ALU.add).then_inc(added, 1)

            def spread_norm(norm, which):
                dve.wait_ge(sums, which + 1)
                norm.vector(dve, small[:, 0, 0:TT])
                for t in range(TT):
                    dve.tensor_scalar(total[:, t * P:(t + 1) * P], ident, norm.out[:, t:t + 1], None,
                                      ALU.mult).then_inc(diag_done, 1)
                for n in range(NCH):
                    dve.wait_ge(spread, NCH * which + n + 1)
                    dve.tensor_copy(run(rms[:], n), small[:, n % 2, 0:RUN]).then_inc(rms_done, 1)
                dve.wait_ge(rms_done, NCH * (which + 1))

            for j in range(NB):
                dve.wait_ge(product, j + 1)
                dve.tensor_copy(by_runs(mix[:, j, :]), acc[j % 2][:, :, 0:RUN]).then_inc(mix_out, 1)
                if j >= 1:
                    add(j - 1, 0)
            add(NB - 1, 0)
            spread_norm(mix_norm, 0)
            for j in range(NB):
                dve.scalar_tensor_tensor(out=mix[:, j, :], in0=mix[:, j, :], scalar=g_post[:, j:j + 1],
                                         in1=rms[:], op0=ALU.mult, op1=ALU.mult).then_inc(normed, 1)
                if j >= 1:
                    low(x, h_hi_done, j - 1, h_lo_done)
                    add(j - 1, NB)
            low(x, h_hi_done, NB - 1, h_lo_done)
            add(NB - 1, NB)
            spread_norm(ple_norm, 1)

            for j in range(NB):
                dve.scalar_tensor_tensor(out=mix[:, j, :], in0=mix[:, j, :], scalar=g_ple[:, j:j + 1],
                                         in1=rms[:], op0=ALU.mult, op1=ALU.mult).then_inc(ple_scaled, 1)
                dve.wait_ge(ple_scaled, j + 1)
                dve.wait_ge(sigmoid, j + 1)
                dve.tensor_tensor(mix[:, j, :], mix[:, j, :], work[j % 2][:], ALU.mult).then_inc(ple_gated, 1)
                dve.wait_ge(ple_gated, j + 1)
                dve.tensor_tensor(mix[:, j, :], mix[:, j, :], x[:, j, :], ALU.add).then_inc(y_done, 1)



def _slopes(n):
    return 2.0 ** (-8.0 * np.arange(1, n + 1) / n)


def _tables():
    row = np.arange(P)
    eye = np.eye(P)
    dist = np.abs(row[:, None] + SEQ - P - np.arange(SEQ)[None, :])
    strip = -_slopes(BH)[0] * dist
    strip[:CHUNK, SEQ - CHUNK:] = MASKED * 64
    rel = np.abs((row % CHUNK)[:, None] + WIN - np.arange(BAND)[None, :])
    slope_a = _slopes(2 * AG).reshape(2, AG)
    band = np.stack([-slope_a[row // CHUNK, g][:, None] * rel for g in range(AG)], 1)
    query = row % DSEQ
    sample_b = -_slopes(BH)[row // (2 * DSEQ)][:, None] * np.abs(query[:, None] + PAST - np.arange(PAST + DSEQ)[None, :])
    sample_a = -slope_a.reshape(-1)[row // DSEQ][:, None] * np.abs(query[:, None] + WIN - np.arange(WIN + DSEQ)[None, :])
    pick = (row[None, :] == (row // (2 * DSEQ) * 2 * DSEQ + query)[:, None])
    second = (row // DSEQ) % 2
    made = dict(consts=np.concatenate([eye, np.ones((P, P))], 1), strip=strip, band=band,
                sample_b=sample_b, sample_a=sample_a, pick=pick, is_map=np.stack([1 - second, second], 1))
    return {k: np.ascontiguousarray(v, dtype=np.float32) for k, v in made.items()}


def _blocks(w, columns):
    picked = w[:, columns]
    k = w.shape[0] // P
    return picked.reshape(k, P, -1, P).transpose(2, 1, 0, 3)


def _feature_major(a):
    return a.reshape(TOK, -1, P).transpose(2, 1, 0)


def kernel(**inputs):
    import concourse.bacc as _bacc
    from concourse.bass_utils import run_bass_kernel_spmd as _run

    f = {k: np.asarray(v) for k, v in inputs.items()}
    window = np.concatenate([np.concatenate([m * 4 * HD + g * HD + np.arange(HD) for m in range(2)])
                             for g in range(AG)])
    a_q, a_k, a_v, a_z, b_q, b_k, b_v, b_z = np.cumsum([0, 512, 128, 128, 512, 512, 512, 512])
    ks = [a_k + np.arange(P)] + [b_k + h * P + np.arange(P) for h in range(BH)]
    vs = [a_v + np.arange(P)] + [b_v + h * P + np.arange(P) for h in range(BH)]
    order = np.concatenate([a_z + window, b_z + np.arange(512)] + [c for kv in zip(ks, vs) for c in kv]
                           + [a_q + window, b_q + np.arange(512)])
    x_all = np.concatenate([f["x_prompt"].reshape(SEQ, D), f["x_sample"].reshape(-1, D)])
    p_all = np.concatenate([f["p_prompt"].reshape(SEQ, PLE), f["p_sample"].reshape(-1, PLE)])
    gains = np.concatenate([f[k][0].reshape(KT, P).T for k in ("pre_norm_g", "post_norm_g", "ple_norm_g")]
                           + [f["b_subln_g"][0][:, None]], 1)
    sink = f["a_sinks"][0]
    sinks = np.concatenate([np.repeat(sink.reshape(2, AG), CHUNK, 0), np.repeat(sink, DSEQ)[:, None]], 1)
    lam = np.stack([f["b_lambda_" + k][0] for k in ("q1", "k1", "q2", "k2")])
    arrays = dict(
        xT=_feature_major(x_all), pT=_feature_major(p_all),
        w_in=_blocks(f["w_in"][0], order),
        w_out=_blocks(f["w_out"][0][np.concatenate([window, 512 + np.arange(512)])], np.arange(D)),
        w_gate=_blocks(f["w_gate"][0], np.arange(D)), w_ple=_blocks(f["w_ple"][0], np.arange(D)),
        gains=gains, lam_in=np.broadcast_to(lam, (P, 4, HD)), sinks=sinks,
        kb_cache=f["cache_b_k"][0].transpose(0, 3, 2, 1),
        vb_cache=f["cache_b_v"][0].reshape(DEC, PAST // P, P, BH * P).transpose(0, 2, 1, 3),
        ka_cache=f["cache_a_k"][0].reshape(DEC, WIN, P).transpose(0, 2, 1),
        va_cache=f["cache_a_v"][0].reshape(DEC, WIN, P),
    )
    arrays = {k: np.ascontiguousarray(v) for k, v in arrays.items()}
    tables = _tables()
    nc = _bacc.Bacc("TRN2", target_bir_lowering=False, num_devices=1)

    def dram(name, shape, kind):
        return nc.dram_tensor(name, list(shape), F32, kind=kind).ap()

    args = {k: dram(k, v.shape, "ExternalInput") for k, v in arrays.items()}
    table_args = {k: dram("table_" + k, v.shape, "ExternalInput") for k, v in tables.items()}
    outs = {"yT": (KT, P, TOK), "kT_out": (5, P, TOK), "vT_out": (5, P, TOK),
            "rolled_k": (DEC, P, WIN - DSEQ), "rolled_v": (DEC, WIN - DSEQ, P)}
    args.update({k: dram(k, s, "ExternalOutput") for k, s in outs.items()})
    encoder_step(nc, tables=table_args, **args)
    arrays.update({"table_" + k: v for k, v in tables.items()})
    r = _run(nc, [arrays], core_ids=[0]).results[0]

    y = r["yT"].reshape(D, TOK).T
    k_all, v_all = (r[n].reshape(ROWS, TOK).T for n in ("kT_out", "vT_out"))
    new_a, new_b = [], []
    for a in (k_all, v_all):
        new_a.append((a[SEQ - WIN:SEQ, 0:P].reshape(1, 1, WIN, 2, HD), a[SEQ:, 0:P].reshape(1, DEC, DSEQ, 2, HD)))
        new_b.append((a[:SEQ, P:].reshape(1, 1, SEQ, BH, P), a[SEQ:, P:].reshape(1, DEC, DSEQ, BH, P)))
    kept = (r["rolled_k"].transpose(0, 2, 1), r["rolled_v"])
    rolled = [np.concatenate([kept[i].reshape(1, DEC, WIN - DSEQ, 2, HD), new_a[i][1]], 2) for i in range(2)]
    return tuple(np.ascontiguousarray(a) for a in (
        y[:SEQ].reshape(1, SEQ, D), y[SEQ:].reshape(DEC, DSEQ, D),
        new_a[0][0], new_a[1][0], new_b[0][0], new_b[1][0], rolled[0], rolled[1], new_b[0][1], new_b[1][1]))
```

```python
from contextlib import ExitStack

import numpy as np
import concourse.bass as bass
from concourse import mybir

F32 = mybir.dt.float32
F32R = mybir.dt.float32r
ALU = mybir.AluOpType
ACT = mybir.ActivationFunctionType
AX_X = mybir.AxisListType.X

P = 128
D = 1024
KT = D // P
SEQ = 1024
NT = SEQ // P
DEC = 8
DSEQ = 16
TOK = SEQ + DEC * DSEQ
TT = TOK // P
NCH = 3
RUN = TOK // NCH
PAST = 1024
CHUNK = 64
NCHUNK = SEQ // CHUNK
BAND = 3 * CHUNK
WIN = 2 * CHUNK
HD = 64
AG = 4
BH = 4
PLE = 256
PKT = PLE // P
ROWS = 5 * P
LAMBDA_INIT = 0.2
EPS = 1e-6
SUB_EPS = 1e-5
MASKED = -1e30
HIGHEST = 3e38
SCALE = HD ** -0.5

NZ = 8
NKV = 5
NQ = 8
NB_IN = NZ + 2 * NKV + NQ
G_KV = NZ // 2
G_Q = G_KV + NKV
G_IN = NB_IN // 2


def wait(eng, sem, value):
    if not isinstance(value, int) or value > 0:
        eng.wait_ge(sem, value)


def pipeline(eng, lags, pieces, period):
    most, end = max(lags), pieces[-1][0]

    def tick(group, newest, piece=None):
        for i, lag in enumerate(lags):
            at = newest - lag
            g = group + at // period
            if isinstance(g, int):
                steps = next((s for last, s in pieces if g < last), None) if g >= 0 else None
            else:
                steps = piece
            if steps and steps[i]:
                steps[i](g, at % period)

    first = 0
    for last, steps in pieces:
        start = min(first - (-(most + 2) // period), last)
        if last - start == 1:
            start = last
        for g in range(first, start):
            for r in range(period):
                tick(g, r)
        if start < last:
            with eng.Fori(start, last) as g:
                for r in range(period):
                    tick(g, r, steps)
        first = last
    for extra in range(most):
        tick(end, extra)


def stages(eng, last, period, steps):
    pipeline(eng, [lag for lag, _ in steps], [(last, [step for _, step in steps])], period)


def encoder_step(nc, xT, pT, w_in, w_out, w_gate, w_ple, gains, lam_in, sinks, tables,
                 kb_cache, vb_cache, ka_cache, va_cache, yT, kT_out, vT_out, rolled_k, rolled_v):
    z_dram = nc.dram_tensor("z_scratch", [NZ, P, TOK], F32, kind="Internal").ap()
    vnew_dram = nc.dram_tensor("v_new_scratch", [DEC * DSEQ, ROWS], F32, kind="Internal").ap()

    with ExitStack() as whole:
        qo = whole.enter_context(nc.sbuf_tensor("qo", [P, 8, TOK], F32))
        consts = whole.enter_context(nc.sbuf_tensor("consts", [P, 2 * P], F32))
        ident = consts[:, 0:P]
        ones = consts[:, P:2 * P]
        gain = whole.enter_context(nc.sbuf_tensor("gain", [P, gains.shape[1]], F32))
        g_pre, g_post, g_ple, g_sub = gain[:, 0:8], gain[:, 8:16], gain[:, 16:24], gain[:, 24:25]
        w_slot = [whole.enter_context(nc.sbuf_tensor(name, [P, KT, P], dtype))
                  for name, dtype in (("w_raw", F32), ("w_hi", F32R), ("w_lo", F32R))]
        with ExitStack() as attention:
            kT = attention.enter_context(nc.sbuf_tensor("kT", [P, 5, TOK], F32))
            v_tok = attention.enter_context(nc.sbuf_tensor("v_tok", [P, TT, ROWS], F32))
            diff_q = DiffQ(nc, attention, qo, lam_in, tables)
            project(nc, xT, w_in, gains, tables, z_dram, vnew_dram, kT_out, vT_out,
                    ka_cache, va_cache, rolled_k, rolled_v, qo, kT, v_tok, consts, gain, w_slot, diff_q)
            ahead = Ahead(nc, attention, kT, v_tok, diff_q.neg_lam, sinks, tables, kb_cache, vb_cache, ka_cache, va_cache, vnew_dram)
            window_q, sample_q = WindowQ(nc, attention, qo), SampleQ(nc, attention, qo)
            with ExitStack() as prompt:
                diff_o = prompt.enter_context(nc.sbuf_tensor("diff_o", [P, BH * NT, P], F32))
                diff_prompt(nc, ahead, diff_q, window_q, diff_o, qo, kT, v_tok, ident)
                window_prompt(nc, ahead, window_q, sample_q, diff_o, qo, kT, v_tok, ident, g_sub)
            sample(nc, ahead, sample_q, w_out, w_slot, z_dram, qo, kT, ident)
        merge(nc, w_slot, xT, pT, w_out, w_gate, w_ple, z_dram, yT, qo, ident, ones, g_sub, g_post, g_ple)


class Maker:

    def __init__(self, nc, ctx, phase):
        self.nc, self.ctx, self.phase = nc, ctx, phase

    def sb(self, name, shape, dtype=F32):
        return self.ctx.enter_context(self.nc.sbuf_tensor(f"{self.phase}_{name}", shape, dtype))

    def ps(self, name, shape):
        return self.ctx.enter_context(self.nc.psum_tensor(f"{self.phase}_{name}", shape, F32))

    def sem(self, name):
        return self.ctx.enter_context(self.nc.semaphore(f"{self.phase}_{name}"))


class Rsqrt:

    STEPS = 5

    def __init__(self, mk, name, rows, cols, width, eps, places=None):
        if places is None:
            places = [mk.sb(f"{name}_{what}", [rows, cols])[:] for what in ("mean", "root", "guess", "rstd")]
        self.v, self.s, self.y, self.out = places
        self.by_dve = mk.sem(name + "_dve")
        self.by_act = mk.sem(name + "_act")
        self.width, self.eps = width, eps

    def mean(self, dve, total):
        dve.tensor_scalar(self.v, total, 1.0 / self.width, self.eps, ALU.mult, ALU.add).then_inc(self.by_dve, 1)

    def scalar(self, act, before=0):
        act.wait_ge(self.by_dve, self.STEPS * before + 1)
        act.activation(self.s, self.v, ACT.Sqrt).then_inc(self.by_act, 1)

    def invert(self, dve, before=0):
        done = self.STEPS * before
        dve.wait_ge(self.by_act, before + 1)
        dve.reciprocal(self.y, self.s).then_inc(self.by_dve, 1)
        dve.wait_ge(self.by_dve, done + 2)
        dve.scalar_tensor_tensor(out=self.s, in0=self.y, scalar=-0.5, in1=self.y,
                                 op0=ALU.mult, op1=ALU.mult).then_inc(self.by_dve, 1)
        dve.wait_ge(self.by_dve, done + 3)
        dve.tensor_tensor(self.v, self.s, self.v, ALU.mult).then_inc(self.by_dve, 1)
        dve.wait_ge(self.by_dve, done + 4)
        dve.scalar_tensor_tensor(out=self.out, in0=self.v, scalar=1.5, in1=self.y,
                                 op0=ALU.add, op1=ALU.mult).then_inc(self.by_dve, 1)
        dve.wait_ge(self.by_dve, done + 5)

    def vector(self, dve, total, before=0):
        self.mean(dve, total)
        self.invert(dve, before)


def three_passes(pe, out, w_hi, w_lo, x_hi, x_lo, start, stop):
    pe.matmul(out, w_hi, x_hi, start=start, stop=False)
    pe.matmul(out, w_hi, x_lo, start=False, stop=False)
    return pe.matmul(out, w_lo, x_hi, start=False, stop=stop)


def weight_slots(mk, w_slot):
    own = [mk.sb(name, [P, KT, P], dtype) for name, dtype in (("w_raw1", F32), ("w_hi1", F32R), ("w_lo1", F32R))]
    return tuple([lasting, new] for lasting, new in zip(w_slot, own))


def run(x, n):
    return x[:, n * RUN:(n + 1) * RUN]


def by_runs(x):
    return x.rearrange("p (n c) -> p n c", n=NCH)


def project(nc, xT, w_in, gains, tables, z_dram, vnew_dram, kT_out, vT_out,
            ka_cache, va_cache, rolled_k, rolled_v, qo, kT, v_tok, consts, gain, w_slot, diff_q):
    ident, ones, g_pre = consts[:, 0:P], consts[:, P:2 * P], gain[:, 0:8]
    with ExitStack() as ctx:
        mk = Maker(nc, ctx, "in")
        x_hi, x_lo = mk.sb("x_hi", [P, KT, TOK], F32R), mk.sb("x_lo", [P, KT, TOK], F32R)
        w_raw, w_hi, w_lo = weight_slots(mk, w_slot)
        squares = [mk.sb(f"squares{s}", [P, TOK]) for s in range(2)]
        rms = mk.sb("rms", [P, TOK])
        tmp = [mk.sb(f"tmp{s}", [P, TOK]) for s in range(2)]
        total = tmp[1]
        half = rms
        diag = total
        norm = Rsqrt(mk, "norm", P, TT, D, EPS, [tmp[0][:, i * TT:(i + 1) * TT] for i in range(4)])
        x_raw = qo
        acc = [mk.ps(f"acc{s}", [P, NCH, 512]) for s in range(2)]
        small = mk.ps("small", [P, 2, 512])

        consts_in, gain_in = mk.sem("consts_in"), mk.sem("gain_in")
        x_in = [mk.sem(f"x_in{k}") for k in range(KT)]
        w_in_sem = [mk.sem(f"w_in{s}") for s in range(2)]
        stored = [mk.sem(f"stored{s}") for s in range(2)]
        vnew_stored, rolled = mk.sem("vnew_stored"), mk.sem("rolled")
        x_hi_done, x_lo_done = mk.sem("x_hi_done"), mk.sem("x_lo_done")
        squared, added, half_steps = mk.sem("squared"), mk.sem("added"), mk.sem("half_steps")
        w_hi_done, w_lo_done = mk.sem("w_hi_done"), mk.sem("w_lo_done")
        product = mk.sem("product")
        evacuated = mk.sem("evacuated")
        sums, diag_done, spread, rms_done = mk.sem("sums"), mk.sem("diag"), mk.sem("spread"), mk.sem("rms_done")
        v_turned, v_copied = mk.sem("v_turned"), mk.sem("v_copied")
        sigmoid, silu = mk.sem("sigmoid"), mk.sem("silu")

        def acc_runs(r):
            return acc[r][:, :, 0:RUN]

        block = ctx.enter_context(nc.Block())

        @block.sync
        def _(sp):
            def load(g, r):
                wait(sp, w_lo_done, 2 * g + r - 1)
                sp.dma_start(w_raw[r][:], w_in[2 * g + r]).then_inc(w_in_sem[r], 16)
                if isinstance(g, int) and g == 0:
                    if r == 0:
                        sp.dma_start(gain[:], gains).then_inc(gain_in, 16)
                    for k in range(5 * r, 5 + 3 * r):
                        sp.dma_start(x_raw[:, k, :], xT[:, k, :]).then_inc(x_in[k], 16)
                    if r == 0:
                        sp.dma_start(consts[:], tables["consts"]).then_inc(consts_in, 16)

                    if r == 1:
                        diff_q.load(sp)

            stages(sp, G_IN, 2, [(0, load)])
            sp.dma_start(rolled_k, ka_cache[:, :, DSEQ:WIN]).then_inc(rolled, 16)
            sp.dma_start(rolled_v, va_cache[:, DSEQ:WIN, :]).then_inc(rolled, 16)
            sp.wait_ge(v_copied, NKV * 3)
            sp.dma_start(vnew_dram, v_tok[:, TT - 1, :]).then_inc(vnew_stored, 16)
            for s in stored:
                sp.wait_ge(s, 16 * G_Q)
            sp.wait_ge(vnew_stored, 16)
            sp.wait_ge(rolled, 32)

        @block.scalar
        def _(act):
            def high(g, r):
                act.wait_ge(w_in_sem[r], 16 * (g + 1))
                wait(act, product, 2 * g + r - 1)
                act.activation(w_hi[r][:], w_raw[r][:], ACT.Copy).then_inc(w_hi_done, 1)

            def first_high(g, r):
                if g > 0:
                    return high(g, r)
                if r == 0:
                    high(0, 0)
                for k in range(5 * r, 5 + 3 * r):
                    if k == 6:
                        high(0, 1)
                    act.wait_ge(x_in[k], 16)
                    if k == 0:
                        act.wait_ge(gain_in, 16)
                    act.activation(x_hi[:, k, :], x_raw[:, k, :], ACT.Copy,
                                   scale=g_pre[:, k:k + 1]).then_inc(x_hi_done, 1)
                if r == 1:
                    for k in range(KT // 2, KT):
                        if k >= KT // 2 + 2:
                            act.wait_ge(added, max(2, k - KT // 2 - 1))
                        act.activation(squares[k % 2][:], x_raw[:, k, :], ACT.Square).then_inc(squared, 1)
                    norm.scalar(act)

            def copy_v(g, r):
                if r == 0:
                    return
                for j, (t0, n) in enumerate(((0, 4), (4, 4), (8, 1))):
                    act.wait_ge(v_turned, 3 * (g - G_KV) + j + 1)
                    act.activation(v_tok[:, t0:t0 + n, bass.ds((g - G_KV) * P, P)],
                                   small[:, j % 2, 0:n * P].rearrange("p (t c) -> p t c", t=n),
                                   ACT.Copy).then_inc(v_copied, 1)

            def store_kv(g, r):
                act.wait_ge(evacuated, 2 * g + r + 1)
                if r == 0:
                    act.dma_start(kT_out[g - G_KV], kT[:, g - G_KV, :]).then_inc(stored[0], 16)
                else:
                    act.dma_start(vT_out[g - G_KV], tmp[1][:]).then_inc(stored[1], 16)

            def gate(g, r):
                act.wait_ge(evacuated, 2 * g + r + 1)
                wait(act, stored[r], 16 * g)
                act.activation(squares[r][:], tmp[r][:], ACT.Sigmoid).then_inc(sigmoid, 1)

            def store_z(g, r):
                act.wait_ge(silu, 2 * g + r + 1)
                act.dma_start(z_dram[2 * g + r], squares[r][:]).then_inc(stored[r], 16)

            def lambda_step(g, r):
                if isinstance(g, int) and 2 * g + r == NZ - 1:
                    diff_q.lambda_scalar(act)

            pipeline(act, (0, 2, 2, 2), [(G_KV, (first_high, gate, store_z, lambda_step)),
                                         (G_Q, (high, copy_v, store_kv, None)), (G_IN, (high, None, None, None))], 2)

        @block.gpsimd
        def _(pool):
            for k in range(KT // 2):
                pool.wait_ge(x_in[k], 16)
                to = half if k == 0 else tmp[0]
                pool.tensor_tensor(to[:], x_raw[:, k, :], x_raw[:, k, :], ALU.mult).then_inc(half_steps, 1)
                if k >= 1:
                    pool.wait_ge(half_steps, 2 * k)
                    pool.tensor_tensor(half[:], half[:], tmp[0][:], ALU.add).then_inc(half_steps, 1)
                    pool.wait_ge(half_steps, 2 * k + 1)

            def low(g, r):
                if isinstance(g, int) and g == 0:
                    return
                if isinstance(g, int) and 2 * g + r == 2:
                    pool.wait_ge(w_lo_done, 2)
                pool.wait_ge(w_hi_done, 2 * g + r + 1)
                wait(pool, product, 2 * g + r - 1)
                pool.tensor_tensor(w_lo[r][:], w_raw[r][:], w_hi[r][:].bitcast(F32),
                                   ALU.subtract).then_inc(w_lo_done, 1)

            def swish(g, r):
                pool.wait_ge(sigmoid, 2 * g + r + 1)
                pool.tensor_tensor(squares[r][:], tmp[r][:], squares[r][:], ALU.mult).then_inc(silu, 1)

            pipeline(pool, (0, 2), [(G_KV, (low, swish)), (G_IN, (low, None))], 2)
            pool.wait_ge(w_lo_done, NB_IN)
            diff_q.zero(pool)
            pool.wait_ge(diff_q.zeroed, 4)
            pool.wait_ge(evacuated, 2 * G_Q + NQ // 2 + 1)
            for t in range(2):
                diff_q.place(pool, 0, t)

        @block.tensor
        def _(pe):
            def multiply(g, r):
                pe.wait_ge(w_lo_done, 2 * g + r + 1)
                wait(pe, evacuated, 2 * g + r - 1)
                for k in range(KT):
                    if isinstance(g, int) and g == 0:
                        if r == 0:
                            pe.wait_ge(x_hi_done, k + 1)
                            pe.wait_ge(x_lo_done, k + 1)
                        elif k == 4:
                            pe.wait_ge(added, KT // 2 + 1)
                            pe.wait_ge(consts_in, 16)
                            for t in range(TT):
                                last = pe.matmul(small[:, 0, t:t + 1], total[:, t * P:(t + 1) * P], ones[:, 0:1],
                                                 start=True, stop=True)
                            last.then_inc(sums, 1)
                        elif k == KT - 1:
                            for n in range(NCH):
                                pe.wait_ge(diag_done, TT // NCH * (n + 1))
                                if n == 2:
                                    pe.wait_ge(rms_done, 1)
                                pe.matmul(small[:, n % 2, 0:RUN], ones, run(diag[:], n),
                                          start=True, stop=True).then_inc(spread, 1)
                    for n in range(NCH):
                        last = three_passes(pe, acc[r][:, n, 0:RUN], w_hi[r][:, k, :], w_lo[r][:, k, :],
                                            run(x_hi[:, k, :], n), run(x_lo[:, k, :], n),
                                            start=(k == 0), stop=(k == KT - 1))
                last.then_inc(product, 1)

            def turn_v(g, r):
                if r == 0:
                    return
                pe.wait_ge(evacuated, 2 * g + 2)
                for j, (t0, n) in enumerate(((0, 4), (4, 4), (8, 1))):
                    wait(pe, v_copied, 3 * (g - G_KV) + (0, -1, 1)[j])
                    for t in range(n):
                        last = pe.transpose(small[:, j % 2, t * P:(t + 1) * P],
                                            tmp[1][:, (t0 + t) * P:(t0 + t + 1) * P], ident)
                    last.then_inc(v_turned, 1)

            pipeline(pe, (0, 1), [(G_KV, (multiply, None)), (G_Q, (multiply, turn_v)), (G_IN, (multiply, None))], 2)

        @block.vector
        def _(dve):
            def low(r):
                dve.wait_ge(w_hi_done, r + 1)
                dve.tensor_tensor(w_lo[r][:], w_raw[r][:], w_hi[r][:].bitcast(F32), ALU.subtract).then_inc(w_lo_done, 1)

            low(0)
            for k in range(KT):
                dve.wait_ge(x_hi_done, k + 1)
                dve.scalar_tensor_tensor(out=x_lo[:, k, :], in0=x_raw[:, k, :], scalar=g_pre[:, k:k + 1],
                                         in1=x_hi[:, k, :].bitcast(F32), op0=ALU.mult,
                                         op1=ALU.subtract).then_inc(x_lo_done, 1)
            low(1)
            dve.wait_ge(squared, 2)
            dve.tensor_tensor(total[:], squares[0][:], squares[1][:], ALU.add).then_inc(added, 2)
            for k in range(2, KT // 2):
                dve.wait_ge(squared, k + 1)
                dve.wait_ge(added, k)
                dve.tensor_tensor(total[:], total[:], squares[k % 2][:], ALU.add).then_inc(added, 1)
            dve.wait_ge(added, KT // 2)
            dve.wait_ge(half_steps, KT - 1)
            dve.tensor_tensor(total[:], total[:], half[:], ALU.add).then_inc(added, 1)
            dve.wait_ge(sums, 1)
            norm.vector(dve, small[:, 0, 0:TT])
            for t in range(TT):
                dve.tensor_scalar(diag[:, t * P:(t + 1) * P], ident, norm.out[:, t:t + 1], None,
                                  ALU.mult).then_inc(diag_done, 1)
            for n in range(NCH):
                dve.wait_ge(spread, n + 1)
                dve.tensor_copy(run(rms[:], n), small[:, n % 2, 0:RUN]).then_inc(rms_done, 1)
            dve.wait_ge(rms_done, NCH)

            def out_z(g, r):
                dve.wait_ge(product, 2 * g + r + 1)
                wait(dve, silu, 2 * g + r - 1)
                dve.tensor_tensor(by_runs(tmp[r][:]), acc_runs(r), by_runs(rms[:]), ALU.mult).then_inc(evacuated, 1)

            def out_kv(g, r):
                if isinstance(g, int) and g == G_KV and r == 1:
                    diff_q.lambda_vector(dve)
                dve.wait_ge(product, 2 * g + r + 1)
                if r == 0:
                    to = kT[:, g - G_KV, :]
                else:
                    if isinstance(g, int) and g == G_KV:
                        dve.wait_ge(silu, NZ)
                    else:
                        dve.wait_ge(v_turned, 3 * (g - G_KV))
                        dve.wait_ge(stored[1], 16 * g)
                    to = tmp[1][:]
                dve.tensor_tensor(by_runs(to), acc_runs(r), by_runs(rms[:]), ALU.mult).then_inc(evacuated, 1)

            def out_q(g, r):
                dve.wait_ge(product, 2 * g + r + 1)
                dve.scalar_tensor_tensor(out=by_runs(qo[:, 2 * (g - G_Q) + r, :]), in0=acc_runs(r), scalar=-SCALE,
                                         in1=by_runs(rms[:]), op0=ALU.mult, op1=ALU.mult).then_inc(evacuated, 1)

            pipeline(dve, (0,), [(G_KV, (out_z,)), (G_Q, (out_kv,)), (G_IN, (out_q,))], 2)
            dve.wait_ge(evacuated, NB_IN)


class Ahead:

    def __init__(self, nc, ctx, kT, v_tok, neg_lam, sinks, tables, kb_cache, vb_cache, ka_cache, va_cache, vnew_dram):
        mk = Maker(nc, ctx, "ahead")
        self.band = mk.sb("band", [P, AG, BAND])
        self.sink = mk.sb("sink", [P, AG + 1])
        self.bias_b, self.bias_a = mk.sb("bias_b", [P, PAST + DSEQ]), mk.sb("bias_a", [P, WIN + DSEQ])
        self.pick = mk.sb("pick", [P, P])
        self.is_map = mk.sb("is_map", [P, 2])
        self.ka = [mk.sb(f"ka{p}", [P, WIN]) for p in range(2)]
        self.va = [mk.sb(f"va{p}", [P, P]) for p in range(2)]
        self.vn = [mk.sb(f"vn{p}", [DSEQ, ROWS]) for p in range(2)]
        self.kb, self.vb = [kT[:, 1:1 + BH, 0:PAST]], [v_tok[:, 0:PAST // P, P:ROWS]]
        self.band_in, self.sample_in = mk.sem("band_in"), mk.sem("sample_in")
        self.kb_in = [mk.sem(f"kb_in{p}") for p in range(2)]
        self.vb_in = [mk.sem(f"vb_in{p}") for p in range(2)]
        self.neg_lam, self.tables, self.sinks = neg_lam, tables, sinks
        self.caches = kb_cache, ka_cache, vb_cache, va_cache, vnew_dram

    def load_tables(self, sp):
        for dst, src in ((self.band, self.tables["band"]), (self.sink, self.sinks)):
            sp.dma_start(dst[:], src).then_inc(self.band_in, 16)
        for dst, name in ((self.bias_b, "sample_b"), (self.bias_a, "sample_a"), (self.pick, "pick"),
                          (self.is_map, "is_map")):
            sp.dma_start(dst[:], self.tables[name]).then_inc(self.sample_in, 16)

    def load_keys(self, sp, item, r):
        sp.dma_start(self.kb[r][:], self.caches[0][item]).then_inc(self.kb_in[r], 16)
        sp.dma_start(self.ka[r][:], self.caches[1][item]).then_inc(self.kb_in[r], 16)

    def load_values(self, sp, item, r):
        sp.dma_start(self.vb[r][:], self.caches[2][item]).then_inc(self.vb_in[r], 16)
        sp.dma_start(self.va[r][:], self.caches[3][item]).then_inc(self.vb_in[r], 16)
        sp.dma_start(self.vn[r][:], self.caches[4][bass.ds(item * DSEQ, DSEQ), :]).then_inc(self.vb_in[r], 16)


def neg_lambda(mk, lam_in):
    vec = mk.sb("lam_vec", [P, 4, HD])
    dots, exps = mk.sb("lam_dots", [P, 2]), mk.sb("lam_exps", [P, 2])
    out = mk.sb("neg_lambda", [P, 1])
    arrived, by_dve, by_act = mk.sem("lam_in"), mk.sem("lam_dve"), mk.sem("lam_act")

    def load(sp):
        sp.dma_start(vec[:], lam_in).then_inc(arrived, 16)

    def vector(dve):
        dve.wait_ge(arrived, 16)
        dve.tensor_tensor(vec[:, 0:4:2, :], vec[:, 0:4:2, :], vec[:, 1:4:2, :], ALU.mult).then_inc(by_dve, 1)
        dve.wait_ge(by_dve, 1)
        dve.reduce_sum(dots[:], vec[:, 0:4:2, :], axis=AX_X).then_inc(by_dve, 1)
        dve.wait_ge(by_act, 1)
        dve.tensor_scalar(exps[:, 0:1], exps[:, 0:1], LAMBDA_INIT, None, ALU.add).then_inc(by_dve, 1)
        dve.wait_ge(by_dve, 3)
        dve.tensor_tensor(out[:], exps[:, 1:2], exps[:, 0:1], ALU.subtract).then_inc(by_dve, 1)
        dve.wait_ge(by_dve, 4)

    def scalar(act):
        act.wait_ge(by_dve, 2)
        act.activation(exps[:], dots[:], ACT.Exp).then_inc(by_act, 1)

    return out, load, vector, scalar


class DiffQ:

    def __init__(self, nc, ctx, qo, lam_in, tables):
        mk = Maker(nc, ctx, "diff_q")
        self.strip, self.strip_in = mk.sb("strip", [P, SEQ]), mk.sem("strip_in")
        self.tables = tables
        self.neg_lam, self.load_lambda, self.lambda_vector, self.lambda_scalar = neg_lambda(mk, lam_in)
        self.slot = [[mk.sb(f"slot{p}{m}", [P, P]) for m in range(2)] for p in range(2)]
        self.zeroed, self.ready, self.qo = mk.sem("zeroed"), mk.sem("ready"), qo

    def load(self, sp):
        self.load_lambda(sp)
        sp.dma_start(self.strip[:], self.tables["strip"]).then_inc(self.strip_in, 16)

    def zero(self, pool):
        for p in range(2):
            for m in range(2):
                pool.memset(self.slot[p][m][:], 0.0).then_inc(self.zeroed, 1)

    def place(self, pool, h, t):
        for m in range(2):
            rows = slice(m * HD, (m + 1) * HD)
            pool.tensor_copy(self.slot[t % 2][m][rows, :],
                             self.qo[rows, BH + h, t * P:(t + 1) * P]).then_inc(self.ready, 1)


class WindowQ:

    def __init__(self, nc, ctx, qo):
        mk = Maker(nc, ctx, "window_q")
        self.slot = [mk.sb(f"slot{p}", [P, AG, P]) for p in range(2)]
        self.zeroed, self.ready, self.qo = mk.sem("zeroed"), mk.sem("ready"), qo

    def zero(self, pool):
        for p in range(2):
            pool.memset(self.slot[p][:], 0.0).then_inc(self.zeroed, 1)

    def place(self, pool, item, r):
        for m in range(2):
            rows, cols = slice(m * HD, (m + 1) * HD), slice(m * CHUNK, (m + 1) * CHUNK)
            pool.tensor_copy(self.slot[r][rows, :, cols],
                             self.qo[rows, 0:AG, bass.ds(item * CHUNK, CHUNK)]).then_inc(self.ready, 1)


class SampleQ:

    def __init__(self, nc, ctx, qo):
        mk = Maker(nc, ctx, "sample_q")
        self.slot_b = [mk.sb(f"slot_b{p}", [P, BH * P]) for p in range(2)]
        self.slot_a = [mk.sb(f"slot_a{p}", [P, P]) for p in range(2)]
        self.zeroed, self.ready, self.qo = mk.sem("zeroed"), mk.sem("ready"), qo

    def zero(self, pool):
        for p in range(2):
            pool.memset(self.slot_b[p][:], 0.0).then_inc(self.zeroed, 1)
            pool.memset(self.slot_a[p][:], 0.0).then_inc(self.zeroed, 1)

    def place(self, pool, item, r):
        tokens = bass.ds(SEQ + item * DSEQ, DSEQ)
        for m in range(2):
            rows = slice(m * HD, (m + 1) * HD)
            to = self.slot_b[r][rows, :].rearrange("p (h x) -> p h x", x=P)
            for h in range(BH):
                first = (2 * h + m) * DSEQ
                pool.tensor_copy(to[:, h, first:first + DSEQ], self.qo[rows, BH + h, tokens]).then_inc(self.ready, 1)
            pool.tensor_copy(self.slot_a[r][rows, m * HD:(m + 1) * HD].rearrange("p (g t) -> p g t", g=AG),
                             self.qo[rows, 0:AG, tokens]).then_inc(self.ready, 1)


def diff_prompt(nc, ahead, diff_q, window_q, o, qo, kT, v_tok, ident):
    with ExitStack() as ctx:
        mk = Maker(nc, ctx, "diff")
        slot, q_ready = diff_q.slot, diff_q.ready
        prob = [mk.sb(f"prob{p}", [P, 2, SEQ]) for p in range(4)]
        turned = [mk.sb(f"turned{p}", [P, NT, P]) for p in range(2)]
        nmax = [mk.sb(f"nmax{p}", [P, 2]) for p in range(2)]
        norm = [mk.sb(f"norm{p}", [P, 2]) for p in range(2)]
        inv = [mk.sb(f"inv{p}", [P, 2]) for p in range(4)]
        coef = mk.sb("coef", [P, 1])
        waited = mk.sb("waited", [P, 4])
        neg_lam, strip = ahead.neg_lam, diff_q.strip
        score = [mk.ps(f"score{m}", [P, SEQ]) for m in range(2)]
        blocks = mk.ps("blocks", [P, 2, 512])
        mixed = [mk.ps(f"mixed{p}", [P, 512]) for p in range(2)]

        scored, biased = mk.sem("scored"), mk.sem("biased")
        exp_done, inv_done = mk.sem("exp_done"), mk.sem("inv_done")
        coef_done, weighted = mk.sem("coef_done"), mk.sem("weighted")
        block_ready, block_out = mk.sem("block_ready"), mk.sem("block_out")
        av_done, o_done, stripped = mk.sem("av_done"), mk.sem("o_done"), mk.sem("stripped")

        banks_before = [sum(1 + (u >= 4) for u in range(t)) for t in range(NT + 1)]
        PER_HEAD = banks_before[NT]

        def banks(t):
            return [(b, min(4, t + 1 - 4 * b)) for b in range(1 + (t >= 4))]

        block = ctx.enter_context(nc.Block())

        @block.sync
        def _(sp):
            ahead.load_tables(sp)

        @block.gpsimd
        def _(pool):
            def place(h, t):
                if isinstance(h, int) and h == 0 and t < 2:
                    return
                pool.wait_ge(scored, 2 * (8 * h + t) - 2)
                diff_q.place(pool, h, t)

            stages(pool, BH, NT, [(0, place)])
            pool.wait_ge(q_ready, 2 * BH * NT)
            window_q.zero(pool)
            pool.wait_ge(window_q.zeroed, 2)
            for item in range(2):
                window_q.place(pool, item, item)

        @block.tensor
        def _(pe):
            def scores(h, t):
                for m in range(2):
                    pe.wait_ge(q_ready, 2 * (8 * h + t) + m + 1)
                    wait(pe, biased, 2 * (8 * h + t) + m - 1)
                    for c in range(0, (t + 1) * P, 512):
                        n = min(512, (t + 1) * P - c)
                        last = pe.matmul(score[m][:, c:c + n], slot[t % 2][m][:], kT[:, h + 1, c:c + n],
                                         start=True, stop=True)
                    last.then_inc(scored, 1)

            def turn(h, t):
                pe.wait_ge(weighted, 8 * h + t + 1)
                for b, n in banks(t):
                    count = PER_HEAD * h + banks_before[t] + b
                    wait(pe, block_out, count - 1)
                    side = (banks_before[t] + b) % 2
                    for j in range(n):
                        k = 4 * b + j
                        last = pe.transpose(blocks[:, side, j * P:(j + 1) * P],
                                            prob[t % 4][:, 0, k * P:(k + 1) * P], ident)
                    last.then_inc(block_ready, 1)

            def average(h, t):
                pe.wait_ge(block_out, PER_HEAD * h + banks_before[t + 1])
                wait(pe, o_done, 8 * h + t - 1)
                for k in range(t + 1):
                    last = pe.matmul(mixed[t % 2][:, 0:P], turned[t % 2][:, k, :], v_tok[:, k, bass.ds((h + 1) * P, P)],
                                     start=(k == 0), stop=(k == t))
                last.then_inc(av_done, 1)

            stages(pe, BH, NT, [(0, scores), (2, turn), (3, average)])

        @block.vector
        def _(dve):
            dve.wait_ge(diff_q.strip_in, 16)

            def bias(h, t):
                item = 8 * h + t
                if t == 0 and not (isinstance(h, int) and h == 0):
                    dve.wait_ge(biased, 2 * item)
                    dve.tensor_scalar(strip[:], strip[:], 0.25, None, ALU.mult).then_inc(stripped, 1)
                    dve.wait_ge(stripped, h)
                n = (t + 1) * P
                wait(dve, block_ready, PER_HEAD * h + (banks_before[t - 3] if t >= 3 else
                                                       banks_before[t + NT - 3] - PER_HEAD))
                dve.wait_ge(scored, 2 * item + 1)
                dve.memset(waited[:, 2 * (t % 2):2 * (t % 2) + 1], 0.0)
                for m in range(2):
                    if m:
                        dve.wait_ge(scored, 2 * item + 2)
                        dve.memset(waited[:, 2 * (t % 2) + 1:2 * (t % 2) + 2], 0.0)
                    dve.tensor_tensor_reduce(prob[t % 4][:, m, 0:n], score[m][:, 0:n], strip[:, SEQ - n:SEQ],
                                             1.0, HIGHEST, ALU.add, ALU.min,
                                             nmax[t % 2][:, m:m + 1]).then_inc(biased, 1)

            def weigh(h, t):
                item = 8 * h + t
                dve.wait_ge(exp_done, 2 * item + 2)
                dve.reciprocal(inv[t % 4][:], norm[t % 2][:]).then_inc(inv_done, 1)
                dve.wait_ge(inv_done, item + 1)
                dve.scalar_tensor_tensor(out=coef[:], in0=inv[t % 4][:, 1:2], scalar=neg_lam[:, 0:1],
                                         in1=norm[t % 2][:, 0:1], op0=ALU.mult, op1=ALU.mult).then_inc(coef_done, 1)
                dve.wait_ge(coef_done, item + 1)
                n = (t + 1) * P
                dve.scalar_tensor_tensor(out=prob[t % 4][:, 0, 0:n], in0=prob[t % 4][:, 1, 0:n],
                                         scalar=coef[:, 0:1], in1=prob[t % 4][:, 0, 0:n],
                                         op0=ALU.mult, op1=ALU.add).then_inc(weighted, 1)

            def take(h, t):
                dve.wait_ge(av_done, 8 * h + t + 1)
                dve.tensor_scalar(o[:, 8 * h + t, :], mixed[t % 2][:, 0:P], inv[t % 4][:, 0:1], None,
                                  ALU.mult).then_inc(o_done, 1)

            stages(dve, BH, NT, [(4, take), (0, bias), (1, weigh)])

        @block.scalar
        def _(act):
            def clear(h, t):
                wait(act, av_done, 8 * h + t - 1)
                for b, n in banks(t):
                    count = PER_HEAD * h + banks_before[t] + b
                    side = (banks_before[t] + b) % 2
                    act.wait_ge(block_ready, count + 1)
                    act.activation(turned[t % 2][:, 4 * b:4 * b + n, :],
                                   blocks[:, side, 0:n * P].rearrange("p (k c) -> p k c", k=n),
                                   ACT.Copy).then_inc(block_out, 1)

            def exponent(h, t):
                item = 8 * h + t
                wait(act, weighted, item - 1)
                n = (t + 1) * P
                for m in range(2):
                    act.wait_ge(biased, 2 * item + m + 1)
                    act.activation(prob[t % 4][:, m, 0:n], prob[t % 4][:, m, 0:n], ACT.Exp,
                                   scale=-1.0, bias=nmax[t % 2][:, m:m + 1],
                                   accum_out=norm[t % 2][:, m:m + 1]).then_inc(exp_done, 1)

            stages(act, BH, NT, [(0, exponent), (2, clear)])


def window_prompt(nc, ahead, window_q, sample_q, diff_o, qo, kT, v_tok, ident, g_sub):
    NORM = NCHUNK // 4
    with ExitStack() as ctx:
        mk = Maker(nc, ctx, "win")
        bias_tab = ahead.band
        nsink = mk.sb("nsink", [P, AG])
        slot = window_q.slot
        prob = [mk.sb(f"prob{p}", [P, AG, 2 * P]) for p in range(2)]
        turned = [mk.sb(f"turned{p}", [P, 2, AG * P]) for p in range(2)]
        o = [mk.sb(f"o{p}", [P, AG, P]) for p in range(2)]
        top = [mk.sb(f"top{p}", [P, AG]) for p in range(2)]
        nmax = [mk.sb(f"nmax{p}", [P, AG]) for p in range(2)]
        over = [mk.sb(f"over{p}", [P, AG]) for p in range(2)]
        sink_e = [mk.sb(f"sink_e{p}", [P, AG]) for p in range(2)]
        norm = [mk.sb(f"norm{p}", [P, AG]) for p in range(2)]
        den = [mk.sb(f"den{p}", [P, AG]) for p in range(2)]
        inv = [mk.sb(f"inv{p}", [P, AG]) for p in range(2)]
        waited = mk.sb("waited", [P, 1])
        squares = mk.sb("squares", [P, 4, P])
        normed = mk.sb("normed", [P, 4, P])
        ssq = mk.sb("ssq", [P, BH * NT])
        sub = Rsqrt(mk, "sub", P, BH * NT, P, SUB_EPS)
        gain_sub = mk.sb("gain_sub", [P, 1])
        score = mk.ps("score", [P, 2, 512])
        blocks = mk.ps("blocks", [P, 2, 512])
        mixed = mk.ps("mixed", [P, 512])
        o_turn = mk.ps("o_turn", [P, 512])
        d_turn = mk.ps("d_turn", [P, 512])

        padded, nsink_done, scored = mk.sem("padded"), mk.sem("nsink_done"), mk.sem("scored")
        biased, max_ready, over_done = mk.sem("biased"), mk.sem("max_ready"), mk.sem("over_done")
        exp_done, den_done, inv_done = mk.sem("exp_done"), mk.sem("den_done"), mk.sem("inv_done")
        block_ready, out_act, out_dve = mk.sem("block_ready"), mk.sem("out_act"), mk.sem("out_dve")
        av_done, o_done, o_turned, o_out = mk.sem("av_done"), mk.sem("o_done"), mk.sem("o_turned"), mk.sem("o_out")
        d_squared, d_summed, d_scaled = mk.sem("d_squared"), mk.sem("d_summed"), mk.sem("d_scaled")
        d_turned, d_out, gain_done = mk.sem("d_turned"), mk.sem("d_out"), mk.sem("gain_done")

        def seen(g, r):
            if isinstance(g, int) and g == 0:
                return P, CHUNK * (r + 1)
            return CHUNK * r, BAND

        block = ctx.enter_context(nc.Block())

        @block.sync
        def _(sp):
            ahead.load_keys(sp, 0, 0)
            ahead.load_values(sp, 0, 0)

        @block.gpsimd
        def _(pool):
            for p in range(2):
                pool.memset(prob[p][:, :, (1 - p) * BAND:(1 - p) * BAND + CHUNK], 0.0).then_inc(padded, 1)
            pool.wait_ge(padded, 2)

            def place(g, r):
                if isinstance(g, int) and g == 0:
                    return
                pool.wait_ge(scored, 2 * g + r - 1)
                window_q.place(pool, 2 * g + r, r)

            stages(pool, NCHUNK // 2, 2, [(0, place)])
            pool.wait_ge(window_q.ready, 2 * NCHUNK)
            sample_q.zero(pool)
            pool.wait_ge(sample_q.zeroed, 4)
            for item in range(2):
                sample_q.place(pool, item, item)

        @block.tensor
        def _(pe):
            def scores(g, r):
                item = 2 * g + r
                _, n = seen(g, r)
                pe.wait_ge(window_q.ready, 2 * item + 2)
                wait(pe, biased, AG * item)
                for h in range(AG):
                    last = pe.matmul(score[:, h // 2, (h % 2) * 256:(h % 2) * 256 + n], slot[r][:, h, :],
                                     kT[:, 0, bass.ds((item + 1) * CHUNK - n, n)], start=True, stop=True)
                last.then_inc(scored, 1)

            def turn(g, r):
                item = 2 * g + r
                pe.wait_ge(exp_done, (AG + 1) * (item + 1))
                first = 1 if isinstance(g, int) and g == 0 else 0
                for b in range(first, 2):
                    wait(pe, (out_act, out_dve)[b], item)
                    for h in range(AG):
                        last = pe.transpose(blocks[:, b, h * P:(h + 1) * P],
                                            prob[r][:, h, b * P:(b + 1) * P], ident)
                last.then_inc(block_ready, 1)

            def average(g, r):
                item = 2 * g + r
                pe.wait_ge(out_act, item + 1)
                pe.wait_ge(out_dve, item + 1)
                wait(pe, o_done, item)
                first = 1 if isinstance(g, int) and g == 0 else 0
                for h in range(AG):
                    for b in range(first, 2):
                        last = pe.matmul(mixed[:, h * P:(h + 1) * P], turned[r][:, b, h * P:(h + 1) * P],
                                         v_tok[:, g - 1 + b, 0:P], start=(b == first), stop=(b == 1))
                last.then_inc(av_done, 1)

            def turn_o(g, r):
                item = 2 * g + r
                pe.wait_ge(o_done, item + 1)
                wait(pe, o_out, 2 * item)
                for h in range(AG):
                    last = pe.transpose(o_turn[:, h * P:(h + 1) * P], o[r][:, h, :], ident)
                last.then_inc(o_turned, 1)

            def turn_diff(g, r):
                j = 2 * (g - NORM) + r
                pe.wait_ge(d_scaled, j + 1)
                wait(pe, d_out, j)
                for i in range(4):
                    last = pe.transpose(d_turn[:, i * P:(i + 1) * P], normed[:, i, :], ident)
                last.then_inc(d_turned, 1)

            pipeline(pe, (0, 1, 2, 3, 2), [(NORM, (scores, turn, average, turn_o, None)),
                                           (2 * NORM, (scores, turn, average, turn_o, turn_diff))], 2)

        @block.vector
        def _(dve):
            dve.wait_ge(ahead.band_in, 32)
            dve.wait_ge(padded, 2)
            dve.tensor_scalar(nsink[:], ahead.sink[:, 0:AG], -1.0, None, ALU.mult).then_inc(nsink_done, 1)
            dve.wait_ge(nsink_done, 1)
            dve.tensor_scalar(gain_sub[:], g_sub, 1.0 - LAMBDA_INIT, None, ALU.mult).then_inc(gain_done, 1)

            def bias(g, r):
                item = 2 * g + r
                col, n = seen(g, r)
                dve.wait_ge(scored, item + 1)
                wait(dve, block_ready, item - 1)
                dve.memset(waited[:], 0.0)
                for h in range(AG):
                    dve.tensor_tensor_reduce(prob[r][:, h, col:col + n],
                                             score[:, h // 2, (h % 2) * 256:(h % 2) * 256 + n],
                                             bias_tab[:, h, BAND - n:BAND], 1.0, HIGHEST, ALU.add, ALU.min,
                                             top[r][:, h:h + 1]).then_inc(biased, 1)
                dve.wait_ge(biased, AG * (item + 1))
                dve.tensor_tensor(nmax[r][:], top[r][:], nsink[:], ALU.min).then_inc(max_ready, 1)
                dve.wait_ge(max_ready, item + 1)
                dve.tensor_tensor(over[r][:], nmax[r][:], nsink[:], ALU.subtract).then_inc(over_done, 1)

            def total(g, r):
                item = 2 * g + r
                dve.wait_ge(exp_done, (AG + 1) * (item + 1))
                dve.tensor_tensor(den[r][:], norm[r][:], sink_e[r][:], ALU.add).then_inc(den_done, 1)
                dve.wait_ge(den_done, item + 1)
                dve.reciprocal(inv[r][:], den[r][:]).then_inc(inv_done, 1)

            def clear(g, r):
                item = 2 * g + r
                dve.wait_ge(block_ready, item + 1)
                dve.tensor_copy(turned[r][:, 1, :], blocks[:, 1, :]).then_inc(out_dve, 1)

            def take(g, r):
                item = 2 * g + r
                dve.wait_ge(av_done, item + 1)
                wait(dve, o_turned, item - 1)
                dve.tensor_tensor(o[r][:], mixed[:].rearrange("p (h c) -> p h c", h=AG),
                                  inv[r][:, :, None].to_broadcast([P, AG, P]), ALU.mult).then_inc(o_done, 1)

            def sum_diff(g, r):
                j = 2 * g + r
                dve.wait_ge(d_squared, j + 1)
                dve.reduce_sum(ssq[:, bass.ds(4 * j, 4)], squares[:], axis=AX_X).then_inc(d_summed, 1)

            def scale_diff(g, r):
                j = 2 * (g - NORM) + r
                if isinstance(g, int) and j == 0:
                    sub.invert(dve)
                wait(dve, d_turned, j)
                dve.tensor_tensor(normed[:], diff_o[:, bass.ds(4 * j, 4), :],
                                  sub.out[:, bass.ds(4 * j, 4), None].to_broadcast([P, 4, P]),
                                  ALU.mult).then_inc(d_scaled, 1)

            def mean_diff(g, r):
                if isinstance(g, int) and g == NORM and r == 0:
                    dve.wait_ge(d_summed, 2 * NORM)
                    sub.mean(dve, ssq[:])

            pipeline(dve, (3, 0, 1, 1, 1, 2), [(NORM, (take, bias, total, clear, sum_diff, None)),
                                               (2 * NORM, (take, bias, total, clear, mean_diff, scale_diff))], 2)

        @block.scalar
        def _(act):
            def exponent(g, r):
                item = 2 * g + r
                col, n = seen(g, r)
                act.wait_ge(over_done, item + 1)
                for h in range(AG):
                    act.activation(prob[r][:, h, col:col + n], prob[r][:, h, col:col + n], ACT.Exp, scale=-1.0,
                                   bias=nmax[r][:, h:h + 1], accum_out=norm[r][:, h:h + 1]).then_inc(exp_done, 1)
                act.activation(sink_e[r][:], over[r][:], ACT.Exp).then_inc(exp_done, 1)

            def clear(g, r):
                item = 2 * g + r
                act.wait_ge(block_ready, item + 1)
                if isinstance(g, int) and g == 0:
                    act.nop().then_inc(out_act, 1)
                else:
                    act.activation(turned[r][:, 0, :], blocks[:, 0, :], ACT.Copy).then_inc(out_act, 1)

            def store_o(g, r):
                item = 2 * g + r
                act.wait_ge(o_turned, item + 1)
                for m in range(2):
                    rows = slice(m * HD, (m + 1) * HD)
                    act.activation(qo[rows, 0:AG, bass.ds(item * CHUNK, CHUNK)],
                                   o_turn[:].rearrange("p (h c) -> p h c", h=AG)[rows, :, m * CHUNK:(m + 1) * CHUNK],
                                   ACT.Copy).then_inc(o_out, 1)

            def square_diff(g, r):
                j = 2 * g + r
                wait(act, d_summed, j)
                act.activation(squares[:], diff_o[:, bass.ds(4 * j, 4), :], ACT.Square).then_inc(d_squared, 1)

            def store_diff(g, r):
                j = 2 * (g - NORM) + r
                if isinstance(g, int) and j == 0:
                    act.wait_ge(gain_done, 1)
                act.wait_ge(d_turned, j + 1)
                act.activation(qo[:, BH + g - NORM, 512 * r:512 * r + 512], d_turn[:], ACT.Copy,
                               scale=gain_sub[:]).then_inc(d_out, 1)

            def root_diff(g, r):
                if isinstance(g, int) and g == NORM and r == 0:
                    sub.scalar(act)

            pipeline(act, (1, 0, 3, 0, 1, 2), [
                (NORM, (clear, exponent, store_o, square_diff, None, None)),
                (2 * NORM, (clear, exponent, store_o, None, root_diff, store_diff))], 2)
            act.wait_ge(o_out, 2 * NCHUNK)
            act.wait_ge(d_out, 2 * NORM)


def sample(nc, ahead, sample_q, w_out, w_slot, z_dram, qo, kT, ident):
    ROW = 2 * DSEQ
    with ExitStack() as ctx:
        mk = Maker(nc, ctx, "smp")
        ahead.kb.append(mk.sb("kb1", [P, BH, PAST]))
        ahead.vb.append(mk.sb("vb1", [P, PAST // P, BH * P]))
        kb, vb, ka, va, vn = ahead.kb, ahead.vb, ahead.ka, ahead.va, ahead.vn
        nsink = mk.sb("nsink", [P, 1])
        row_coef = mk.sb("row_coef", [P, 1])
        slot_b, slot_a, q_ready = sample_q.slot_b, sample_q.slot_a, sample_q.ready
        z = mk.sb("z", [P, SEQ])
        prob_b, prob_a = mk.sb("prob_b", [P, PAST + DSEQ]), mk.sb("prob_a", [P, WIN + DSEQ])
        turned = mk.sb("turned", [P, 11, P])
        waited = mk.sb("waited", [P, 1])
        by_b, by_a = mk.sb("by_b", [P, P]), mk.sb("by_a", [P, P])
        o_b = mk.sb("o_b", [P, P])
        top, nmax, inv = mk.sb("top", [P, 1]), mk.sb("nmax", [P, 2]), mk.sb("inv", [P, 2])
        over, coef, den = mk.sb("over", [P, 1]), mk.sb("coef", [P, 1]), mk.sb("den", [P, 2])
        norm = mk.sb("norm", [P, 3])
        score = mk.ps("score", [P, 3, 512])
        blocks = mk.ps("blocks", [P, 3, 512])
        mixed_b = mk.ps("mixed_b", [P, 512])
        mixed_a = mk.ps("mixed_a", [P, 512])
        score_b = score[:].rearrange("p b c -> p (b c)")[:, 0:PAST + DSEQ]
        score_a = score[:, 2, P:P + WIN + DSEQ]

        z_in, w_in, w_hi_done, w_lo_done = mk.sem("z_in"), mk.sem("w_in"), mk.sem("w_hi_done"), mk.sem("w_lo_done")
        rows_done, scored, z_sample_in = mk.sem("rows_done"), mk.sem("scored"), mk.sem("z_sample_in")
        biased, max_ready, over_done = mk.sem("biased"), mk.sem("max_ready"), mk.sem("over_done")
        exp_done, den_done, inv_done = mk.sem("exp_done"), mk.sem("den_done"), mk.sem("inv_done")
        coef_done, turner_ready, block_ready = mk.sem("coef_done"), mk.sem("turner_ready"), mk.sem("block_ready")
        out_act, out_dve = mk.sem("out_act"), mk.sem("out_dve")
        av_done, o_done, posted = mk.sem("av_done"), mk.sem("o_done"), mk.sem("posted")
        stored_a, stored_b, gated = mk.sem("stored_a"), mk.sem("stored_b"), mk.sem("gated")

        block = ctx.enter_context(nc.Block())

        @block.sync
        def _(sp):
            sp.dma_start(w_slot[0][:], w_out[0]).then_inc(w_in, 16)

            def load(g, r):
                item = 2 * g + r
                if not isinstance(g, int) or item > 0:
                    wait(sp, scored, item - 1)
                    ahead.load_keys(sp, item, r)
                    wait(sp, av_done, item - 1)
                    ahead.load_values(sp, item, r)
                wait(sp, gated, item)
                sp.dma_start(z[:], z_dram[item][:, 0:SEQ]).then_inc(z_in, 16)

            stages(sp, DEC // 2, 2, [(0, load)])
            sp.wait_ge(w_lo_done, 1)
            sp.dma_start(w_slot[0][:],
                         z_dram[:, :, SEQ:TOK].rearrange("b p t -> p b t")).then_inc(z_sample_in, 16)
            sp.wait_ge(z_sample_in, 16)

        @block.gpsimd
        def _(pool):
            def place(g, r):
                item = 2 * g + r
                if isinstance(g, int) and g == 0:
                    return
                pool.wait_ge(scored, item - 1)
                pool.wait_ge(gated, item - 1)
                sample_q.place(pool, item, r)

            def gate(g, r):
                item = 2 * g + r
                pool.wait_ge(z_in, 16 * (item + 1))
                last = isinstance(g, int) and item == DEC - 1
                pool.wait_ge(q_ready, 10 * (item + 1 if last else item + 2))
                pool.tensor_tensor(qo[:, item, 0:SEQ], qo[:, item, 0:SEQ], z[:], ALU.mult).then_inc(gated, 1)

            stages(pool, DEC // 2, 2, [(0, place), (1, gate)])
            pool.wait_ge(gated, DEC)
            pool.wait_ge(w_hi_done, 1)
            pool.tensor_tensor(w_slot[2][:], w_slot[0][:], w_slot[1][:].bitcast(F32),
                               ALU.subtract).then_inc(w_lo_done, 1)
            pool.wait_ge(w_lo_done, 1)

        @block.tensor
        def _(pe):
            def scores(g, r):
                item = 2 * g + r
                pe.wait_ge(ahead.kb_in[r], 32 * (g + 1))
                pe.wait_ge(q_ready, 10 * (item + 1))
                wait(pe, biased, 2 * item)
                for c in range(3):
                    n = 512 if c < 2 else DSEQ
                    for h in range(BH):
                        keys = (kb[r][:, h, c * 512:(c + 1) * 512] if c < 2 else
                                kT[:, h + 1, bass.ds(SEQ + item * DSEQ, DSEQ)])
                        pe.matmul(score[:, c, 0:n], slot_b[r][:, h * P:(h + 1) * P], keys,
                                  start=(h == 0), stop=(h == BH - 1))
                pe.matmul(score_a[:, 0:WIN], slot_a[r][:], ka[r][:], start=True, stop=True)
                pe.matmul(score_a[:, WIN:WIN + DSEQ], slot_a[r][:], kT[:, 0, bass.ds(SEQ + item * DSEQ, DSEQ)],
                          start=True, stop=True).then_inc(scored, 1)

            def turn(g, r):
                item = 2 * g + r
                pe.wait_ge(turner_ready, 2 * (item + 1))
                pe.matmul(blocks[:, 2, 0:P], prob_a[:, 0:P], by_a[:], start=True, stop=True)
                pe.matmul(blocks[0:DSEQ, 2, P:2 * P], prob_b[:, PAST:PAST + DSEQ], by_b[:], start=True, stop=True)
                pe.matmul(blocks[0:DSEQ, 2, 2 * P:3 * P], prob_a[:, WIN:WIN + DSEQ], by_a[:],
                          start=True, stop=True).then_inc(block_ready, 1)
                for j in range(2):
                    for i in range(4):
                        last = pe.matmul(blocks[:, j, i * P:(i + 1) * P],
                                         prob_b[:, (4 * j + i) * P:(4 * j + i + 1) * P], by_b[:], start=True, stop=True)
                    last.then_inc(block_ready, 1)

            def post(g, r):
                item = 2 * g + r
                pe.wait_ge(o_done, BH * (item + 1))
                pe.wait_ge(stored_a, 2 * (item + 1))
                pe.transpose(mixed_a[:, P:2 * P], o_b[:], ident).then_inc(posted, 1)

            def average(g, r):
                item = 2 * g + r
                pe.wait_ge(ahead.vb_in[r], 48 * (g + 1))
                pe.wait_ge(out_act, 2 * (item + 1))
                pe.wait_ge(out_dve, 2 * (item + 1))
                wait(pe, o_done, BH * item)
                wait(pe, stored_b, item)
                for k in range(PAST // P):
                    pe.matmul(mixed_b[:], turned[:, k, :], vb[r][:, k, :], start=(k == 0), stop=False)
                pe.matmul(mixed_b[:], turned[0:DSEQ, 9, :], vn[r][:, P:ROWS], start=False, stop=True)
                pe.matmul(mixed_a[:, 0:P], va[r][:], turned[:, 8, :], start=True, stop=False)
                pe.matmul(mixed_a[:, 0:P], vn[r][:, 0:P], turned[0:DSEQ, 10, :],
                          start=False, stop=True).then_inc(av_done, 1)

            stages(pe, DEC // 2, 2, [(1, turn), (2, post), (0, scores), (1, average)])

        @block.vector
        def _(dve):
            dve.wait_ge(ahead.sample_in, 64)
            dve.tensor_scalar(nsink[:], ahead.sink[:, AG:AG + 1], -1.0, None, ALU.mult).then_inc(rows_done, 1)
            dve.scalar_tensor_tensor(out=row_coef[:], in0=ahead.is_map[:, 1:2], scalar=ahead.neg_lam[:, 0:1],
                                     in1=ahead.is_map[:, 0:1], op0=ALU.mult, op1=ALU.add).then_inc(rows_done, 1)
            dve.wait_ge(rows_done, 2)

            def bias(g, r):
                item = 2 * g + r
                dve.wait_ge(scored, item + 1)
                wait(dve, block_ready, 3 * item)
                dve.memset(waited[:], 0.0)
                dve.tensor_tensor_reduce(prob_b[:], score_b, ahead.bias_b[:], 1.0, HIGHEST, ALU.add, ALU.min,
                                         nmax[:, 0:1]).then_inc(biased, 1)
                dve.tensor_tensor_reduce(prob_a[:], score_a, ahead.bias_a[:], 1.0, HIGHEST, ALU.add, ALU.min,
                                         top[:]).then_inc(biased, 1)
                dve.wait_ge(biased, 2 * (item + 1))
                dve.tensor_tensor(nmax[:, 1:2], top[:], nsink[:], ALU.min).then_inc(max_ready, 1)
                dve.wait_ge(max_ready, item + 1)
                dve.tensor_tensor(over[:], nmax[:, 1:2], nsink[:], ALU.subtract).then_inc(over_done, 1)

            def factors(g, r):
                item = 2 * g + r
                dve.wait_ge(exp_done, 3 * (item + 1))
                dve.tensor_copy(den[:, 0:1], norm[:, 0:1]).then_inc(den_done, 1)
                dve.tensor_tensor(den[:, 1:2], norm[:, 1:2], norm[:, 2:3], ALU.add).then_inc(den_done, 1)
                dve.wait_ge(den_done, 2 * (item + 1))
                dve.reciprocal(inv[:], den[:]).then_inc(inv_done, 1)
                dve.wait_ge(inv_done, item + 1)
                dve.tensor_scalar(by_a[:], ident, inv[:, 1:2], None, ALU.mult).then_inc(turner_ready, 1)
                dve.tensor_tensor(coef[:], inv[:, 0:1], row_coef[:], ALU.mult).then_inc(coef_done, 1)
                dve.wait_ge(coef_done, item + 1)
                dve.tensor_scalar(by_b[:], ahead.pick[:], coef[:, 0:1], None, ALU.mult).then_inc(turner_ready, 1)

            def clear(g, r):
                item = 2 * g + r
                dve.wait_ge(block_ready, 3 * item + 1)
                wait(dve, av_done, item)
                dve.tensor_copy(turned[:, 8, :], blocks[:, 2, 0:P]).then_inc(out_dve, 1)
                dve.tensor_copy(turned[0:DSEQ, 9:11, :],
                                blocks[0:DSEQ, 2, P:3 * P].rearrange("p (k c) -> p k c", k=2)).then_inc(out_dve, 1)

            def take(g, r):
                item = 2 * g + r
                dve.wait_ge(av_done, item + 1)
                wait(dve, posted, item)
                for h in range(BH):
                    rows = slice(h * ROW, (h + 1) * ROW)
                    dve.tensor_copy(o_b[rows, :], mixed_b[rows, h * P:(h + 1) * P]).then_inc(o_done, 1)

            stages(dve, DEC // 2, 2, [(1, factors), (2, take), (1, clear), (0, bias)])

        @block.scalar
        def _(act):
            act.wait_ge(w_in, 16)
            act.activation(w_slot[1][:], w_slot[0][:], ACT.Copy).then_inc(w_hi_done, 1)

            def exponent(g, r):
                item = 2 * g + r
                act.wait_ge(over_done, item + 1)
                act.activation(prob_b[:], prob_b[:], ACT.Exp, scale=-1.0, bias=nmax[:, 0:1],
                               accum_out=norm[:, 0:1]).then_inc(exp_done, 1)
                act.activation(prob_a[:], prob_a[:], ACT.Exp, scale=-1.0, bias=nmax[:, 1:2],
                               accum_out=norm[:, 1:2]).then_inc(exp_done, 1)
                act.activation(norm[:, 2:3], over[:], ACT.Exp).then_inc(exp_done, 1)

            def clear(g, r):
                item = 2 * g + r
                for j in range(2):
                    act.wait_ge(block_ready, 3 * item + j + 2)
                    act.activation(turned[:, 4 * j:4 * j + 4, :], blocks[:, j, :].rearrange("p (k c) -> p k c", k=4),
                                   ACT.Copy).then_inc(out_act, 1)

            def store_a(g, r):
                item = 2 * g + r
                act.wait_ge(av_done, item + 1)
                for m in range(2):
                    rows = slice(m * HD, (m + 1) * HD)
                    act.activation(qo[rows, 0:AG, bass.ds(SEQ + item * DSEQ, DSEQ)],
                                   mixed_a[rows, m * HD:(m + 1) * HD].rearrange("p (g t) -> p g t", g=AG),
                                   ACT.Copy).then_inc(stored_a, 1)

            def store_b(g, r):
                item = 2 * g + r
                act.wait_ge(posted, item + 1)
                act.activation(qo[:, BH:8, bass.ds(SEQ + item * DSEQ, DSEQ)],
                               mixed_a[:, P:2 * P].rearrange("p (h x) -> p h x", x=ROW)[:, :, 0:DSEQ],
                               ACT.Copy).then_inc(stored_b, 1)

            stages(act, DEC // 2, 2, [(2, store_a), (1, clear), (2, store_b), (0, exponent)])
            act.wait_ge(stored_a, 2 * DEC)
            act.wait_ge(stored_b, DEC)


def merge(nc, w_slot, xT, pT, w_out, w_gate, w_ple, z_dram, yT, qo, ident, ones, g_sub, g_post, g_ple):
    NB = 8
    PLE0, GATE0, END = NB, 2 * NB, 3 * NB
    with ExitStack() as ctx:
        mk = Maker(nc, ctx, "mrg")
        a_hi, a_lo = mk.sb("a_hi", [P, KT, TOK], F32R), mk.sb("a_lo", [P, KT, TOK], F32R)
        mix = mk.sb("mix", [P, KT, TOK])
        x = qo
        p_emb = mk.sb("p_emb", [P, PKT, TOK])
        w_raw, w_hi, w_lo = weight_slots(mk, w_slot)
        work = [mk.sb(f"work{s}", [P, TOK]) for s in range(2)]
        total = mk.sb("total", [P, TOK])
        rms = mk.sb("rms", [P, TOK])
        gain_sub = mk.sb("gain_sub", [P, 1])
        z = w_raw[0]
        sample_o = qo[:, BH:8, SEQ:TOK]
        sub_norm = Rsqrt(mk, "sub", P, BH, P, SUB_EPS)
        mix_norm = Rsqrt(mk, "mix_norm", P, TT, D, EPS)
        ple_norm = Rsqrt(mk, "ple_norm", P, TT, D, EPS)
        acc = [mk.ps(f"acc{s}", [P, NCH, 512]) for s in range(2)]
        small = mk.ps("small", [P, 2, 512])

        w_in = [mk.sem(f"w_in{s}") for s in range(2)]
        x_in, p_in, y_out = mk.sem("x_in"), mk.sem("p_in"), mk.sem("y_out")
        sub_squared, sub_summed, sub_diag = mk.sem("sub_squared"), mk.sem("sub_summed"), mk.sem("sub_diag")
        sub_spread, sub_scaled = mk.sem("sub_spread"), mk.sem("sub_scaled")
        gain_done, gated, a_hi_done, a_lo_done = mk.sem("gain_done"), mk.sem("gated"), mk.sem("a_hi_done"), mk.sem("a_lo_done")
        w_hi_done, w_lo_done = mk.sem("w_hi_done"), mk.sem("w_lo_done")
        product = mk.sem("product")
        mix_out, ple_out = mk.sem("mix_out"), mk.sem("ple_out")
        ple_moved = mk.sem("ple_moved")
        squared, added = mk.sem("squared"), mk.sem("added")
        sums, diag_done, spread, rms_done = mk.sem("sums"), mk.sem("diag"), mk.sem("spread"), mk.sem("rms_done")
        normed, h_by_dve, h_by_pool = mk.sem("normed"), mk.sem("h_by_dve"), mk.sem("h_by_pool")
        h_hi_done, h_lo_done = mk.sem("h_hi"), mk.sem("h_lo")
        sigmoid, ple_scaled, ple_gated, y_done = mk.sem("sigmoid"), mk.sem("ple_scaled"), mk.sem("ple_gated"), mk.sem("y_done")

        def split_count(j):
            return j if j < PLE0 else j - GATE0 + NB

        def loads_of_slot(j):
            here = j // 2 + 1 if j < PLE0 else NB // 2 + 1 + (j >= GATE0) * ((j - GATE0) // 2 + 1)
            return here - (j % 2 == 0 if j < PLE0 or j >= GATE0 else j < PLE0 + NB // 2)

        BY_DVE = (0, 2)

        def wait_h(eng, j):
            if j in BY_DVE:
                eng.wait_ge(h_by_dve, 1 + BY_DVE.index(j))
            else:
                eng.wait_ge(h_by_pool, sum(i not in BY_DVE for i in range(j + 1)))

        def ple_weights(j):
            return w_raw[j // 4][:].rearrange("p (b k) c -> p b k c", k=PKT)[:, j % 4]

        block = ctx.enter_context(nc.Block())

        @block.sync
        def _(sp):
            sp.dma_start(w_raw[1][:], w_out[1]).then_inc(w_in[1], 16)
            for j in range(2, 4):
                if j == 2:
                    sp.wait_ge(gated, 2)
                else:
                    sp.wait_ge(w_lo_done, split_count(j - 2))
                sp.dma_start(w_raw[j % 2][:], w_out[j]).then_inc(w_in[j % 2], 16)
            for k in range(KT):
                sp.wait_ge(a_lo_done, k + 1)
                sp.dma_start(x[:, k, :], xT[:, k, :]).then_inc(x_in, 16)
            sp.dma_start(p_emb[:], pT).then_inc(p_in, 16)
            for j in range(4, NB):
                sp.wait_ge(w_lo_done, split_count(j - 2))
                sp.dma_start(w_raw[j % 2][:], w_out[j]).then_inc(w_in[j % 2], 16)
            for r in range(2):
                sp.wait_ge(w_lo_done, split_count(NB - 2 + r))
                sp.dma_start(w_raw[r][:].rearrange("p (b k) c -> p b (k c)", k=PKT),
                             w_ple[4 * r:4 * r + 4].rearrange("b p k c -> p b (k c)")).then_inc(w_in[r], 16)
            for r in range(2):
                sp.wait_ge(product, PLE0 + 4 * r + 4)
                sp.dma_start(w_raw[r][:], w_gate[r]).then_inc(w_in[r], 16)

            def store_y(j):
                sp.wait_ge(y_done, j + 1)
                sp.dma_start(yT[j], mix[:, j, :]).then_inc(y_out, 16)

            for j in range(2, NB):
                sp.wait_ge(w_lo_done, split_count(GATE0 + j - 2))
                sp.dma_start(w_raw[j % 2][:], w_gate[j]).then_inc(w_in[j % 2], 16)
                if j >= 4:
                    store_y(j - 4)
            for j in range(NB - 4, NB - 1):
                store_y(j)
            for n in range(NCH):
                sp.wait_ge(y_done, NB + n)
                sp.dma_start(run(yT[NB - 1], n), run(mix[:, NB - 1, :], n)).then_inc(y_out, 16)
            sp.wait_ge(y_out, 16 * (NB - 1 + NCH))

        @block.scalar
        def _(act):
            def high(j):
                act.wait_ge(w_in[j % 2], 16 * loads_of_slot(j))
                if j >= 2:
                    act.wait_ge(product, j - 1 if j < PLE0 or j >= GATE0 + 2 else NB)
                act.activation(w_hi[j % 2][:], w_raw[j % 2][:], ACT.Copy).then_inc(w_hi_done, 1)

            def square(j, counted):
                if counted + j >= 2:
                    act.wait_ge(added, counted + max(j - 1, 2) if j >= 2 else counted)
                act.activation(work[j % 2][:], mix[:, j, :], ACT.Square).then_inc(squared, 1)

            act.activation(work[0][:, 0:BH * P].rearrange("p (h t) -> p h t", h=BH), sample_o,
                           ACT.Square).then_inc(sub_squared, 1)
            for k in range(KT):
                act.wait_ge(gated, 1 if k < AG else 2)
                act.activation(a_hi[:, k, :], qo[:, k, :], ACT.Copy).then_inc(a_hi_done, 1)
                if k == 0:
                    sub_norm.scalar(act)
                if k == AG - 1:
                    high(1)
            for j in range(2, NB):
                high(j)
                act.wait_ge(mix_out, j - 1)
                square(j - 2, 0)
            for j in range(NB - 2, NB):
                act.wait_ge(mix_out, j + 1)
                square(j, 0)
            for j in range(2):
                act.wait_ge(product, PLE0 + j + 1)
                act.wait_ge(added, NB - 1 + j)
                act.activation(by_runs(work[j][:]), acc[j][:, :, 0:RUN], ACT.Copy).then_inc(ple_out, 1)
                if j == 0:
                    mix_norm.scalar(act)

            def take_ple(j):
                wait_h(act, j)
                if j < 2:
                    act.wait_ge(ple_out, 2)
                    act.activation(mix[:, j, :], work[j][:], ACT.Copy).then_inc(ple_moved, 1)
                else:
                    act.wait_ge(product, PLE0 + j + 1)
                    act.activation(by_runs(mix[:, j, :]), acc[j % 2][:, :, 0:RUN], ACT.Copy).then_inc(ple_out, 1)

            for j in range(NB):
                if j == 1:
                    take_ple(2)
                if j != 2:
                    take_ple(j)
                act.activation(a_hi[:, j, :], x[:, j, :], ACT.Copy).then_inc(h_hi_done, 1)
                if j == NB // 2:
                    high(GATE0)
            high(GATE0 + 1)
            act.wait_ge(ple_out, NB)
            act.wait_ge(ple_moved, 2)
            for j in range(NB):
                square(j, NB)
            ple_norm.scalar(act)

            for j in range(GATE0, END):
                i = j - GATE0
                act.wait_ge(product, j + 1)
                if i < 2:
                    act.wait_ge(added, 2 * NB)
                else:
                    act.wait_ge(ple_gated, i - 1)
                if j < END - 1:
                    act.activation(by_runs(work[j % 2][:]), acc[j % 2][:, :, 0:RUN], ACT.Sigmoid).then_inc(sigmoid, 1)
                else:
                    for n in range(NCH):
                        act.wait_ge(product, j + 1 + n)
                        act.activation(run(work[j % 2][:], n), acc[j % 2][:, n, 0:RUN], ACT.Sigmoid).then_inc(sigmoid, 1)
                if j + 2 < END:
                    high(j + 2)

        @block.gpsimd
        def _(pool):
            def low(j):
                pool.wait_ge(w_hi_done, split_count(j))
                pool.tensor_tensor(w_lo[j % 2][:], w_raw[j % 2][:], w_hi[j % 2][:].bitcast(F32),
                                   ALU.subtract).then_inc(w_lo_done, 1)

            for j in range(1, NB):
                low(j)
            pool.wait_ge(x_in, 16 * KT)
            for j in range(1, NB):
                if j not in BY_DVE:
                    pool.wait_ge(normed, j + 1)
                    pool.tensor_tensor(x[:, j, :], x[:, j, :], mix[:, j, :], ALU.add).then_inc(h_by_pool, 1)
                if j == NB // 2 + 1:
                    low(GATE0)
            for j in range(GATE0 + 1, END):
                low(j)

        @block.tensor
        def _(pe):
            def free_banks(j):
                if j >= GATE0 + 2:
                    pe.wait_ge(sigmoid, j - GATE0 - 1)
                elif j >= PLE0 + 2:
                    pe.wait_ge(ple_out, j - PLE0 - 1)
                elif j >= 2:
                    pe.wait_ge(mix_out, j - 1)

            def multiply(j, parts=(), between={}):
                if j > 0:
                    pe.wait_ge(w_lo_done, split_count(j))
                free_banks(j)
                for k in range(KT):
                    if k in between:
                        between[k]()
                    for s in parts:
                        pe.wait_ge(s, k + 1)
                    for n in range(NCH):
                        last = three_passes(pe, acc[j % 2][:, n, 0:RUN], w_hi[j % 2][:, k, :], w_lo[j % 2][:, k, :],
                                            run(a_hi[:, k, :], n), run(a_lo[:, k, :], n),
                                            start=(k == 0), stop=(k == KT - 1))
                last.then_inc(product, 1)

            def embed(j):
                i = j - PLE0
                pe.wait_ge(w_in[i // 4], 16 * loads_of_slot(j))
                free_banks(j)
                for k in range(PKT):
                    for n in range(NCH):
                        last = pe.matmul(acc[j % 2][:, n, 0:RUN], ple_weights(i)[:, k, :], run(p_emb[:, k, :], n),
                                         start=(k == 0), stop=(k == PKT - 1))
                last.then_inc(product, 1)

            def statistics(which):
                pe.wait_ge(added, NB * (which + 1))
                for t in range(TT):
                    last = pe.matmul(small[:, 0, t:t + 1], total[:, t * P:(t + 1) * P], ones[:, 0:1],
                                     start=True, stop=True)
                last.then_inc(sums, 1)

            def to_all(which):
                for n in range(NCH):
                    pe.wait_ge(diag_done, TT * which + TT // NCH * (n + 1))
                    if n == 2:
                        pe.wait_ge(rms_done, NCH * which + 1)
                    pe.matmul(small[:, n % 2, 0:RUN], ones, run(total[:], n), start=True, stop=True).then_inc(spread, 1)

            def spread_sub():
                pe.wait_ge(sub_diag, BH)
                pe.matmul(small[:, 1, :], ones, total[:, 0:BH * P], start=True, stop=True).then_inc(sub_spread, 1)

            pe.wait_ge(sub_squared, 1)
            for h in range(BH):
                last = pe.matmul(small[:, 0, h:h + 1], work[0][:, h * P:(h + 1) * P], ones[:, 0:1],
                                 start=True, stop=True)
            last.then_inc(sub_summed, 1)
            multiply(0, (a_hi_done, a_lo_done), {1: spread_sub})
            for j in range(1, NB):
                multiply(j)
            pe.wait_ge(p_in, 16)
            embed(PLE0)
            statistics(0)
            embed(PLE0 + 1)
            to_all(0)
            for j in range(PLE0 + 2, GATE0):
                embed(j)
            multiply(GATE0, (h_hi_done, h_lo_done))
            multiply(GATE0 + 1, between={5: lambda: statistics(1)})
            multiply(GATE0 + 2, between={2: lambda: to_all(1)})
            for j in range(GATE0 + 3, END - 1):
                multiply(j)
            pe.wait_ge(w_lo_done, split_count(END - 1))
            free_banks(END - 1)
            for n in range(NCH):
                for k in range(KT):
                    last = three_passes(pe, acc[1][:, n, 0:RUN], w_hi[1][:, k, :], w_lo[1][:, k, :],
                                        run(a_hi[:, k, :], n), run(a_lo[:, k, :], n),
                                        start=(k == 0), stop=(k == KT - 1))
                last.then_inc(product, 1)

        @block.vector
        def _(dve):
            def low(source, done, j, count):
                dve.wait_ge(done, j + 1)
                dve.tensor_tensor(a_lo[:, j, :], source[:, j, :], a_hi[:, j, :].bitcast(F32),
                                  ALU.subtract).then_inc(count, 1)

            dve.tensor_scalar(gain_sub[:], g_sub, 1.0 - LAMBDA_INIT, None, ALU.mult).then_inc(gain_done, 1)
            dve.tensor_tensor(qo[:, 0:AG, SEQ:TOK], qo[:, 0:AG, SEQ:TOK], z[:, 0:AG], ALU.mult).then_inc(gated, 1)
            dve.wait_ge(sub_summed, 1)
            sub_norm.mean(dve, small[:, 0, 0:BH])
            low(qo, a_hi_done, 0, a_lo_done)
            sub_norm.invert(dve)
            for h in range(BH):
                dve.tensor_scalar(total[:, h * P:(h + 1) * P], ident, sub_norm.out[:, h:h + 1], None,
                                  ALU.mult).then_inc(sub_diag, 1)
            low(qo, a_hi_done, 1, a_lo_done)
            low(qo, a_hi_done, 2, a_lo_done)
            dve.wait_ge(gain_done, 1)
            dve.wait_ge(sub_spread, 1)
            dve.scalar_tensor_tensor(out=sample_o, in0=sample_o, scalar=gain_sub[:, 0:1],
                                     in1=small[:, 1, :].rearrange("p (h t) -> p h t", h=BH),
                                     op0=ALU.mult, op1=ALU.mult).then_inc(sub_scaled, 1)
            dve.wait_ge(sub_scaled, 1)
            dve.tensor_tensor(sample_o, sample_o, z[:, BH:8], ALU.mult).then_inc(gated, 1)
            for k in range(3, KT):
                low(qo, a_hi_done, k, a_lo_done)

            def add(j, counted):
                dve.wait_ge(squared, counted + j + 1)
                if j == 1:
                    dve.tensor_tensor(total[:], work[0][:], work[1][:], ALU.add).then_inc(added, 2)
                elif j > 1:
                    dve.wait_ge(added, counted + j)
                    dve.tensor_tensor(total[:], total[:], work[j % 2][:], ALU.add).then_inc(added, 1)

            def spread_norm(norm, which):
                dve.wait_ge(sums, which + 1)
                norm.vector(dve, small[:, 0, 0:TT])
                for t in range(TT):
                    dve.tensor_scalar(total[:, t * P:(t + 1) * P], ident, norm.out[:, t:t + 1], None,
                                      ALU.mult).then_inc(diag_done, 1)
                for n in range(NCH):
                    dve.wait_ge(spread, NCH * which + n + 1)
                    dve.tensor_copy(run(rms[:], n), small[:, n % 2, 0:RUN]).then_inc(rms_done, 1)
                dve.wait_ge(rms_done, NCH * (which + 1))

            for j in range(NB):
                dve.wait_ge(product, j + 1)
                dve.tensor_copy(by_runs(mix[:, j, :]), acc[j % 2][:, :, 0:RUN]).then_inc(mix_out, 1)
                if j >= 1:
                    add(j - 1, 0)
            add(NB - 1, 0)
            spread_norm(mix_norm, 0)
            for j in range(NB):
                dve.scalar_tensor_tensor(out=mix[:, j, :], in0=mix[:, j, :], scalar=g_post[:, j:j + 1],
                                         in1=rms[:], op0=ALU.mult, op1=ALU.mult).then_inc(normed, 1)
                if j in BY_DVE:
                    dve.wait_ge(x_in, 16 * KT)
                    dve.wait_ge(normed, j + 1)
                    dve.tensor_tensor(x[:, j, :], x[:, j, :], mix[:, j, :], ALU.add).then_inc(h_by_dve, 1)
                if j >= 3:
                    low(x, h_hi_done, j - 3, h_lo_done)
            for j in range(NB - 3, NB):
                low(x, h_hi_done, j, h_lo_done)
            for j in range(NB):
                add(j, NB)
            spread_norm(ple_norm, 1)

            for j in range(NB):
                dve.scalar_tensor_tensor(out=mix[:, j, :], in0=mix[:, j, :], scalar=g_ple[:, j:j + 1],
                                         in1=rms[:], op0=ALU.mult, op1=ALU.mult).then_inc(ple_scaled, 1)
                dve.wait_ge(ple_scaled, j + 1)
                for n in range(1 if j < NB - 1 else NCH):
                    part = (lambda a: a) if j < NB - 1 else (lambda a: run(a, n))
                    y, gate = part(mix[:, j, :]), part(work[j % 2][:])
                    dve.wait_ge(sigmoid, j + 1 + n)
                    dve.tensor_tensor(y, y, gate, ALU.mult).then_inc(ple_gated, 1)
                    dve.wait_ge(ple_gated, j + 1 + n)
                    dve.tensor_tensor(y, y, part(x[:, j, :]), ALU.add).then_inc(y_done, 1)



def _slopes(n):
    return 2.0 ** (-8.0 * np.arange(1, n + 1) / n)


def _tables():
    row = np.arange(P)
    eye = np.eye(P)
    dist = np.abs(row[:, None] + SEQ - P - np.arange(SEQ)[None, :])
    strip = _slopes(BH)[0] * dist
    strip[:CHUNK, SEQ - CHUNK:] = -MASKED * 64
    rel = np.abs((row % CHUNK)[:, None] + WIN - np.arange(BAND)[None, :])
    slope_a = _slopes(2 * AG).reshape(2, AG)
    band = np.stack([slope_a[row // CHUNK, g][:, None] * rel for g in range(AG)], 1)
    query = row % DSEQ
    sample_b = _slopes(BH)[row // (2 * DSEQ)][:, None] * np.abs(query[:, None] + PAST - np.arange(PAST + DSEQ)[None, :])
    sample_a = slope_a.reshape(-1)[row // DSEQ][:, None] * np.abs(query[:, None] + WIN - np.arange(WIN + DSEQ)[None, :])
    pick = (row[None, :] == (row // (2 * DSEQ) * 2 * DSEQ + query)[:, None])
    second = (row // DSEQ) % 2
    made = dict(consts=np.concatenate([eye, np.ones((P, P))], 1), strip=strip, band=band,
                sample_b=sample_b, sample_a=sample_a, pick=pick, is_map=np.stack([1 - second, second], 1))
    return {k: np.ascontiguousarray(v, dtype=np.float32) for k, v in made.items()}


def _blocks(w, columns):
    picked = w[:, columns]
    k = w.shape[0] // P
    return picked.reshape(k, P, -1, P).transpose(2, 1, 0, 3)


def _feature_major(a):
    return a.reshape(TOK, -1, P).transpose(2, 1, 0)


def kernel(**inputs):
    import concourse.bacc as _bacc
    from concourse.bass_utils import run_bass_kernel_spmd as _run

    f = {k: np.asarray(v) for k, v in inputs.items()}
    window = np.concatenate([np.concatenate([m * 4 * HD + g * HD + np.arange(HD) for m in range(2)])
                             for g in range(AG)])
    a_q, a_k, a_v, a_z, b_q, b_k, b_v, b_z = np.cumsum([0, 512, 128, 128, 512, 512, 512, 512])
    ks = [a_k + np.arange(P)] + [b_k + h * P + np.arange(P) for h in range(BH)]
    vs = [a_v + np.arange(P)] + [b_v + h * P + np.arange(P) for h in range(BH)]
    order = np.concatenate([a_z + window, b_z + np.arange(512)] + [c for kv in zip(ks, vs) for c in kv]
                           + [a_q + window, b_q + np.arange(512)])
    x_all = np.concatenate([f["x_prompt"].reshape(SEQ, D), f["x_sample"].reshape(-1, D)])
    p_all = np.concatenate([f["p_prompt"].reshape(SEQ, PLE), f["p_sample"].reshape(-1, PLE)])
    gains = np.concatenate([f[k][0].reshape(KT, P).T for k in ("pre_norm_g", "post_norm_g", "ple_norm_g")]
                           + [f["b_subln_g"][0][:, None]], 1)
    sink = f["a_sinks"][0]
    sinks = np.concatenate([np.repeat(sink.reshape(2, AG), CHUNK, 0), np.repeat(sink, DSEQ)[:, None]], 1)
    lam = np.stack([f["b_lambda_" + k][0] for k in ("q1", "k1", "q2", "k2")])
    arrays = dict(
        xT=_feature_major(x_all), pT=_feature_major(p_all),
        w_in=_blocks(f["w_in"][0], order),
        w_out=_blocks(f["w_out"][0][np.concatenate([window, 512 + np.arange(512)])], np.arange(D)),
        w_gate=_blocks(f["w_gate"][0], np.arange(D)), w_ple=_blocks(f["w_ple"][0], np.arange(D)),
        gains=gains, lam_in=np.broadcast_to(lam, (P, 4, HD)), sinks=sinks,
        kb_cache=f["cache_b_k"][0].transpose(0, 3, 2, 1),
        vb_cache=f["cache_b_v"][0].reshape(DEC, PAST // P, P, BH * P).transpose(0, 2, 1, 3),
        ka_cache=f["cache_a_k"][0].reshape(DEC, WIN, P).transpose(0, 2, 1),
        va_cache=f["cache_a_v"][0].reshape(DEC, WIN, P),
    )
    arrays = {k: np.ascontiguousarray(v) for k, v in arrays.items()}
    tables = _tables()
    nc = _bacc.Bacc("TRN2", target_bir_lowering=False, num_devices=1)

    def dram(name, shape, kind):
        return nc.dram_tensor(name, list(shape), F32, kind=kind).ap()

    args = {k: dram(k, v.shape, "ExternalInput") for k, v in arrays.items()}
    table_args = {k: dram("table_" + k, v.shape, "ExternalInput") for k, v in tables.items()}
    outs = {"yT": (KT, P, TOK), "kT_out": (5, P, TOK), "vT_out": (5, P, TOK),
            "rolled_k": (DEC, P, WIN - DSEQ), "rolled_v": (DEC, WIN - DSEQ, P)}
    args.update({k: dram(k, s, "ExternalOutput") for k, s in outs.items()})
    encoder_step(nc, tables=table_args, **args)
    arrays.update({"table_" + k: v for k, v in tables.items()})
    r = _run(nc, [arrays], core_ids=[0]).results[0]

    y = r["yT"].reshape(D, TOK).T
    k_all, v_all = (r[n].reshape(ROWS, TOK).T for n in ("kT_out", "vT_out"))
    new_a, new_b = [], []
    for a in (k_all, v_all):
        new_a.append((a[SEQ - WIN:SEQ, 0:P].reshape(1, 1, WIN, 2, HD), a[SEQ:, 0:P].reshape(1, DEC, DSEQ, 2, HD)))
        new_b.append((a[:SEQ, P:].reshape(1, 1, SEQ, BH, P), a[SEQ:, P:].reshape(1, DEC, DSEQ, BH, P)))
    kept = (r["rolled_k"].transpose(0, 2, 1), r["rolled_v"])
    rolled = [np.concatenate([kept[i].reshape(1, DEC, WIN - DSEQ, 2, HD), new_a[i][1]], 2) for i in range(2)]
    return tuple(np.ascontiguousarray(a) for a in (
        y[:SEQ].reshape(1, SEQ, D), y[SEQ:].reshape(DEC, DSEQ, D),
        new_a[0][0], new_a[1][0], new_b[0][0], new_b[1][0], rolled[0], rolled[1], new_b[0][1], new_b[1][1]))
```
